# Optimizing a Trainium2 kernel written in Bass

```python
import jax, jax.numpy as jnp
from jax import lax
import numpy as np

D_MODEL = 1024
BATCH = 1
SEQ = 1024
DEPTH = 1
DEC_BATCH = 8
DEC_SEQ = 1
PAST_LEN = 4096
PAGE_SIZE = 128

RET_HEADS = 4
RET_DK = 128
RET_DV = 256
FOX_HEADS = 8
FOX_HD = 64
RET_QK_W = RET_HEADS * RET_DK
RET_V_W = RET_HEADS * RET_DV
FOX_W = FOX_HEADS * FOX_HD
D_FF = 2816
CONV_W = 3
CHUNK = 128
Q_BLOCK = 128
ROPE_BASE = 10000.0
LN_EPS = 1e-5
GN_EPS = 1e-5
ALPHA = (2 * DEPTH) ** 0.25
BETA = (8 * DEPTH) ** -0.25
IN_SPLITS = (RET_QK_W, RET_QK_W, RET_V_W, RET_V_W, FOX_W, FOX_W, FOX_W, FOX_HEADS, D_MODEL, D_MODEL)
IN_COLS = sum(IN_SPLITS)

kernel_name = 'hybrid_retention_fox_convffn_step'

def layer_norm(x, w, b):
    x32 = x.astype(jnp.float32)
    mu = jnp.mean(x32, -1, keepdims=True)
    var = jnp.mean(jnp.square(x32 - mu), -1, keepdims=True)
    return ((x32 - mu) * lax.rsqrt(var + LN_EPS) * w + b).astype(x.dtype)

def rotary(x, pos):
    half = x.shape[-1] // 2
    freq = ROPE_BASE ** (-jnp.arange(half, dtype=jnp.float32) / half)
    ang = pos[:, None] * freq[None, :]
    cos = jnp.cos(ang)[None, :, None, :]
    sin = jnp.sin(ang)[None, :, None, :]
    x32 = x.astype(jnp.float32)
    x1, x2 = x32[..., :half], x32[..., half:]
    return jnp.concatenate([x1 * cos - x2 * sin, x1 * sin + x2 * cos], -1).astype(x.dtype)

def in_projection(x, w_in, b_f, pos):
    b, t, _ = x.shape
    offsets = np.cumsum(IN_SPLITS)[:-1].tolist()
    rq, rk, rv, rg, fq, fk, fv, ff, ga, gb = jnp.split(x @ w_in, offsets, axis=-1)
    rq = rotary(rq.reshape(b, t, RET_HEADS, RET_DK), pos)
    rk = rotary(rk.reshape(b, t, RET_HEADS, RET_DK), pos) * (RET_DK ** -0.5)
    rv = rv.reshape(b, t, RET_HEADS, RET_DV)
    fq = fq.reshape(b, t, FOX_HEADS, FOX_HD)
    fk = fk.reshape(b, t, FOX_HEADS, FOX_HD)
    fv = fv.reshape(b, t, FOX_HEADS, FOX_HD)
    logf = jax.nn.log_sigmoid(ff.astype(jnp.float32) + b_f.astype(jnp.float32))
    return rq, rk, rv, rg, fq, fk, fv, logf, ga, gb

def retention_chunkwise(q, k, v, s0):
    q = q.astype(jnp.float32)
    k = k.astype(jnp.float32)
    v = v.astype(jnp.float32)
    b, t, h, _ = q.shape
    dv = v.shape[-1]
    c = CHUNK if t % CHUNK == 0 else t
    n = t // c
    log_g = jnp.log(1.0 - 2.0 ** (-5.0 - jnp.arange(h, dtype=jnp.float32)))
    i = jnp.arange(c, dtype=jnp.float32)
    rel = i[:, None] - i[None, :]
    intra = jnp.where(rel >= 0, jnp.exp(log_g[:, None, None] * jnp.maximum(rel, 0.0)), 0.0)
    q_decay = jnp.exp(log_g[None, :] * (i[:, None] + 1.0))
    k_decay = jnp.exp(log_g[None, :] * (c - 1.0 - i[:, None]))
    chunk_decay = jnp.exp(log_g * c)

    def to_chunks(a):
        return a.reshape(b, n, c, *a.shape[2:]).swapaxes(0, 1)

    def step(s, qkv):
        qc, kc, vc = qkv
        inner = jnp.einsum('bihd,bjhd->bhij', qc, kc) * intra
        o = jnp.einsum('bhij,bjhe->bihe', inner, vc) + jnp.einsum('bihd,bhde->bihe', qc * q_decay[None, :, :, None], s)
        s = s * chunk_decay[None, :, None, None] + jnp.einsum('bjhd,bjhe->bhde', kc * k_decay[None, :, :, None], vc)
        return s, o

    s, o = lax.scan(step, s0.astype(jnp.float32), (to_chunks(q), to_chunks(k), to_chunks(v)))
    return o.swapaxes(0, 1).reshape(b, t, h, dv), s

def fox_prompt(q, k, v, logf):
    b, t, h, d = q.shape
    scale = d ** -0.5
    c = jnp.cumsum(logf, axis=1)
    nb = t // Q_BLOCK
    qb = q.reshape(b, nb, Q_BLOCK, h, d).swapaxes(0, 1)
    cb = c.reshape(b, nb, Q_BLOCK, h).swapaxes(0, 1)
    starts = jnp.arange(nb, dtype=jnp.int32) * Q_BLOCK
    kpos = jnp.arange(t, dtype=jnp.int32)
    c_k = c.transpose(0, 2, 1)[:, :, None, :]

    def block(args):
        qi, ci, start = args
        s = jnp.einsum('bqhd,bkhd->bhqk', qi, k).astype(jnp.float32) * scale
        bias = ci.transpose(0, 2, 1)[..., None] - c_k
        qpos = start + jnp.arange(Q_BLOCK, dtype=jnp.int32)
        logits = jnp.where(kpos[None, :] <= qpos[:, None], s + bias, -jnp.inf)
        p = jax.nn.softmax(logits, axis=-1)
        return jnp.einsum('bhqk,bkhd->bqhd', p.astype(v.dtype), v)

    o = lax.map(block, (qb, cb, starts))
    return o.swapaxes(0, 1).reshape(b, t, h, d)

def fox_sample(q, k, v, logf, k_past, v_past, logf_past):
    p_len = k_past.shape[1]
    t = q.shape[1]
    scale = q.shape[-1] ** -0.5
    c = jnp.cumsum(jnp.concatenate([logf_past.astype(jnp.float32), logf], axis=1), axis=1)
    s = jnp.concatenate([jnp.einsum('bqhd,bkhd->bhqk', q, k_past.astype(q.dtype)),
                         jnp.einsum('bqhd,bkhd->bhqk', q, k)], axis=-1).astype(jnp.float32) * scale
    bias = c[:, p_len:].transpose(0, 2, 1)[..., None] - c.transpose(0, 2, 1)[:, :, None, :]
    kpos = jnp.arange(p_len + t, dtype=jnp.int32)
    qpos = p_len + jnp.arange(t, dtype=jnp.int32)
    logits = jnp.where(kpos[None, :] <= qpos[:, None], s + bias, -jnp.inf)
    p = jax.nn.softmax(logits, axis=-1).astype(v.dtype)
    return (jnp.einsum('bhqk,bkhd->bqhd', p[..., :p_len], v_past.astype(v.dtype))
            + jnp.einsum('bhqk,bkhd->bqhd', p[..., p_len:], v))

def merge_branches(ret_o, rg, fox_o, ga, gb, gn_w, gn_b, w_pa, w_pb, w_o):
    b, t = rg.shape[:2]
    mu = jnp.mean(ret_o, -1, keepdims=True)
    var = jnp.mean(jnp.square(ret_o - mu), -1, keepdims=True)
    rn = ((ret_o - mu) * lax.rsqrt(var + GN_EPS)).reshape(b, t, RET_V_W)
    rn = (rn * gn_w + gn_b).astype(rg.dtype)
    u_a = (jax.nn.silu(rg) * rn) @ w_pa
    u_b = fox_o.reshape(b, t, FOX_W) @ w_pb
    merged = jax.nn.sigmoid(ga) * u_a + jax.nn.sigmoid(gb) * u_b
    return merged @ w_o

def conv_ffn(h, conv_prev, w_up, w_gate, conv_w, conv_b, w_down):
    u = h @ w_up
    g = h @ w_gate
    t = u.shape[1]
    up = jnp.concatenate([conv_prev.astype(u.dtype), u], axis=1)
    acc = conv_b
    for i in range(CONV_W):
        acc = acc + up[:, i:i + t] * conv_w[i]
    a = jax.nn.gelu(acc) * g
    return a @ w_down, up[:, up.shape[1] - (CONV_W - 1):]

def post_norm_ffn(x, mix, conv_prev, ln1_w, ln1_b, w_up, w_gate, conv_w, conv_b, w_down, ln2_w, ln2_b):
    h = layer_norm(ALPHA * x + mix, ln1_w, ln1_b)
    f, conv_new = conv_ffn(h, conv_prev, w_up, w_gate, conv_w, conv_b, w_down)
    return layer_norm(ALPHA * h + f, ln2_w, ln2_b), conv_new

def setup_inputs(seed: int = 0) -> dict:
    key = jax.random.key(seed)
    ks = jax.random.split(key, 32)
    f32 = jnp.float32
    n_pages = PAST_LEN // PAGE_SIZE
    n_pool = (DEC_BATCH * n_pages * 5) // 4
    nrm = lambda k, shape: jax.random.normal(k, shape, f32)
    page_table = jax.random.permutation(ks[0], n_pool)[:DEC_BATCH * n_pages].reshape(DEC_BATCH, n_pages).astype(jnp.int32)
    scales = (1.0, 1.0, BETA, 1.0, 1.0, 1.0, BETA, 1.0, 1.0, 1.0)
    col_scale = jnp.concatenate([jnp.full((n,), s, f32) for n, s in zip(IN_SPLITS, scales)])
    return {
        'x_prompt': nrm(ks[1], (BATCH, SEQ, D_MODEL)),
        'x_sample': nrm(ks[2], (DEC_BATCH, DEC_SEQ, D_MODEL)),
        'cache_k': nrm(ks[3], (DEPTH, n_pool, PAGE_SIZE, FOX_HEADS, FOX_HD)),
        'cache_v': nrm(ks[4], (DEPTH, n_pool, PAGE_SIZE, FOX_HEADS, FOX_HD)),
        'cache_logf': jax.nn.log_sigmoid(2.0 + nrm(ks[5], (DEPTH, n_pool, PAGE_SIZE, FOX_HEADS))),
        'state_ret': 0.5 * nrm(ks[6], (DEPTH, DEC_BATCH, RET_HEADS, RET_DK, RET_DV)),
        'state_conv': nrm(ks[7], (DEPTH, DEC_BATCH, CONV_W - 1, D_FF)),
        'page_table': page_table,
        'w_in': nrm(ks[8], (DEPTH, D_MODEL, IN_COLS)) * (D_MODEL ** -0.5) * col_scale,
        'b_f': 2.0 + 0.5 * nrm(ks[9], (DEPTH, FOX_HEADS)),
        'ret_gn_w': 1.0 + 0.02 * nrm(ks[10], (DEPTH, RET_V_W)),
        'ret_gn_b': 0.02 * nrm(ks[11], (DEPTH, RET_V_W)),
        'w_pa': nrm(ks[12], (DEPTH, RET_V_W, D_MODEL)) * (RET_V_W ** -0.5) * BETA,
        'w_pb': nrm(ks[13], (DEPTH, FOX_W, D_MODEL)) * (FOX_W ** -0.5) * BETA,
        'w_o': nrm(ks[14], (DEPTH, D_MODEL, D_MODEL)) * (D_MODEL ** -0.5) * BETA,
        'ln1_w': 1.0 + 0.02 * nrm(ks[15], (DEPTH, D_MODEL)),
        'ln1_b': 0.02 * nrm(ks[16], (DEPTH, D_MODEL)),
        'w_up': nrm(ks[17], (DEPTH, D_MODEL, D_FF)) * (D_MODEL ** -0.5) * BETA,
        'w_gate': nrm(ks[18], (DEPTH, D_MODEL, D_FF)) * (D_MODEL ** -0.5) * BETA,
        'conv_w': nrm(ks[19], (DEPTH, CONV_W, D_FF)) * (CONV_W ** -0.5),
        'conv_b': 0.02 * nrm(ks[20], (DEPTH, D_FF)),
        'w_down': nrm(ks[21], (DEPTH, D_FF, D_MODEL)) * (D_FF ** -0.5) * BETA,
        'ln2_w': 1.0 + 0.02 * nrm(ks[22], (DEPTH, D_MODEL)),
        'ln2_b': 0.02 * nrm(ks[23], (DEPTH, D_MODEL)),
    }

def reference(x_prompt, x_sample, cache_k, cache_v, cache_logf, state_ret, state_conv, page_table,
              w_in, b_f, ret_gn_w, ret_gn_b, w_pa, w_pb, w_o, ln1_w, ln1_b,
              w_up, w_gate, conv_w, conv_b, w_down, ln2_w, ln2_b):
    xp, xs = x_prompt, x_sample
    bp, tp = xp.shape[0], xp.shape[1]
    bs, ts = xs.shape[0], xs.shape[1]
    n_pages = page_table.shape[1]
    past = n_pages * PAGE_SIZE
    pos_p = jnp.arange(tp, dtype=jnp.float32)
    pos_s = past + jnp.arange(ts, dtype=jnp.float32)
    kp_l, vp_l, lfp_l, rp_l, cp_l = [], [], [], [], []
    ks_l, vs_l, lfs_l, rs_l, cs_l = [], [], [], [], []
    for l in range(DEPTH):
        mix_w = (ret_gn_w[l], ret_gn_b[l], w_pa[l], w_pb[l], w_o[l])
        ffn_w = (ln1_w[l], ln1_b[l], w_up[l], w_gate[l], conv_w[l], conv_b[l], w_down[l], ln2_w[l], ln2_b[l])
        rq, rk, rv, rg, fq, fk, fv, lf, ga, gb = in_projection(xp, w_in[l], b_f[l], pos_p)
        ret_o, s_p = retention_chunkwise(rq, rk, rv, jnp.zeros((bp, RET_HEADS, RET_DK, RET_DV), jnp.float32))
        fox_o = fox_prompt(fq, fk, fv, lf)
        mix = merge_branches(ret_o, rg, fox_o, ga, gb, *mix_w)
        xp, c_p = post_norm_ffn(xp, mix, jnp.zeros((bp, CONV_W - 1, D_FF), xp.dtype), *ffn_w)
        kp_l.append(fk); vp_l.append(fv); lfp_l.append(lf); rp_l.append(s_p); cp_l.append(c_p)
        rq, rk, rv, rg, fq, fk, fv, lf, ga, gb = in_projection(xs, w_in[l], b_f[l], pos_s)
        ret_o, s_s = retention_chunkwise(rq, rk, rv, state_ret[l])
        k_past = cache_k[l][page_table].reshape(bs, past, FOX_HEADS, FOX_HD)
        v_past = cache_v[l][page_table].reshape(bs, past, FOX_HEADS, FOX_HD)
        lf_past = cache_logf[l][page_table].reshape(bs, past, FOX_HEADS)
        fox_o = fox_sample(fq, fk, fv, lf, k_past, v_past, lf_past)
        mix = merge_branches(ret_o, rg, fox_o, ga, gb, *mix_w)
        xs, c_s = post_norm_ffn(xs, mix, state_conv[l], *ffn_w)
        ks_l.append(fk); vs_l.append(fv); lfs_l.append(lf); rs_l.append(s_s); cs_l.append(c_s)
    k_prompt = jnp.stack(kp_l)
    v_prompt = jnp.stack(vp_l)
    logf_prompt = jnp.stack(lfp_l)
    k_sample = jnp.stack(ks_l)
    v_sample = jnp.stack(vs_l)
    logf_sample = jnp.stack(lfs_l)
    ret_prompt = jnp.stack(rp_l)
    ret_sample = jnp.stack(rs_l)
    conv_prompt = jnp.stack(cp_l)
    conv_sample = jnp.stack(cs_l)
    return (xp, xs, k_prompt, v_prompt, logf_prompt, k_sample, v_sample, logf_sample,
            ret_prompt, ret_sample, conv_prompt, conv_sample)


_drawn_inputs = setup_inputs


def setup_inputs(seed=0):
    import zlib

    import numpy as np

    out = dict(_drawn_inputs(seed))
    spreads = {}
    factors = {'cache_logf': 36.125,
     'ret_gn_w': 35.673,
     'ret_gn_b': 35.355,
     'ln1_w': 7.721,
     'ln1_b': 7.734,
     'conv_b': 8.0,
     'ln2_w': 22.296,
     'ln2_b': 23.118,
     'cache_k': 4.448}
    for name, (base, spread) in spreads.items():
        noise = np.random.default_rng([zlib.crc32(name.encode()), seed]).standard_normal(out[name].shape)
        drawn = base * np.exp(spread * noise) if base else spread * noise
        out[name] = __import__('jax').numpy.asarray(drawn.astype(out[name].dtype))
    for name, factor in factors.items():
        out[name] = (out[name] * factor).astype(out[name].dtype)
    return out
```

```python
from contextlib import ExitStack

import numpy as np

import concourse.bass as bass
from concourse import mybir

F32 = mybir.dt.float32
F32R = mybir.dt.float32r
BF16 = mybir.dt.bfloat16
I32 = mybir.dt.int32
ACT = mybir.ActivationFunctionType
ALU = mybir.AluOpType
AX = mybir.AxisListType

P = 128
D = 1024
SEQ = 1024
NS = 8
T = SEQ + NS
KD = D // P
NCH = 3
TC = T // NCH
RH, DK, DV = 4, 128, 256
FH, HD = 8, 64
NPG, PG = 32, 128
POOL = 320
DFF = 2816
FT = DFF // P
ALPHA = 2.0 ** 0.25
EPS = 1e-5
BIG = -1.0e30
QB = SEQ // P
C_RQ, C_RK, C_RV, C_RG = 0, 512, 1024, 2048
C_FQ, C_FK, C_FV, C_FF, C_GA, C_GB = 3072, 3584, 4096, 4608, 4616, 5640
RING = 2

ds = bass.ds


def chunk(n):
    return slice(n * TC, (n + 1) * TC)


class Shared:
    pass


class Chain:

    def __init__(self, eng, sem, base=0):
        self.eng, self.sem, self.base, self.n = eng, sem, base, 0

    def link(self, ins):
        self.n += 1
        ins.then_inc(self.sem, 1)
        self.eng.wait_ge(self.sem, self.base + self.n)


def wait_apart(eng, sem, value, held):
    value = value if isinstance(value, int) else eng.to_reg(value)
    eng.wait_ge(held, 1)
    eng.wait_ge(sem, value)



def job(base, parity, local):
    return base + local, (parity + local) % RING


def load_weight(g, eng, jb, src, kt=KD, m=P):
    j, slot = jb
    wait_apart(eng, g.w_split, j + 1, g.mm_chunk)
    eng.dma_start(g.w_raw[slot][:, 0:kt, 0:m], src).then_inc(g.w_land[slot], 16)


def split_hi(g, act, jb, kt=KD, m=P):
    j, slot = jb
    act.wait_ge(g.w_land[slot], (j - slot) * (16 // RING) + 16)
    act.wait_ge(g.mm_chunk, NCH * (j + 1))
    act.activation(g.w_hi[slot][:, 0:kt, 0:m], g.w_raw[slot][:, 0:kt, 0:m], ACT.Copy).then_inc(g.w_rounded, 1)


def split_lo(g, dve, jb, kt=KD, m=P):
    j, slot = jb
    dve.wait_ge(g.w_rounded, j + 1)
    dve.tensor_tensor(g.w_lo[slot][:, 0:kt, 0:m], g.w_raw[slot][:, 0:kt, 0:m],
                      g.w_hi[slot][:, 0:kt, 0:m].bitcast(F32), ALU.subtract).then_inc(g.w_split, 1)


def product(g, pe, jb, xh, xl, kt=KD, m=P, before=None, after=None):
    j, slot = jb
    pe.wait_ge(g.w_split, RING + j + 1)
    for n in range(NCH):
        pe.wait_ge(g.bank_free[n], j + 1)
        if before:
            before(n)
        for k in range(kt):
            for i, (w, x) in enumerate(((g.w_hi, xh), (g.w_hi, xl), (g.w_lo, xh))):
                mm = pe.matmul(g.bank[n][0:m, 0:TC], w[slot][:, k, 0:m], x[:, k, chunk(n)],
                               start=(k == 0 and i == 0), stop=(k == kt - 1 and i == 2))
        mm.then_inc(g.mm_chunk, 1)
        if after:
            after(n)


def chunk_ready(g, eng, j, n):
    eng.wait_ge(g.mm_chunk, NCH * (RING + j) + n + 1)



def constants(bf16=None):
    bf16 = bf16 or mybir.dt.np(BF16)
    f = np.float32
    c = {}
    i = np.arange(P)
    c["ident"] = np.eye(P, dtype=f)
    c["later_row"] = (i[:, None] > i[None, :]).astype(f)
    b, pg = i // NPG, i % NPG
    c["later_page"] = ((b[:, None] == b[None, :]) & (pg[:, None] > pg[None, :])).astype(f)
    pos = np.concatenate([np.arange(SEQ), np.full(NS, NPG * PG)]).astype(f)
    half = DK // 2
    freq = np.power(f(10000.0), -(np.arange(half, dtype=f) / f(half))).astype(f)
    ang = (freq[:, None] * pos[None, :]).astype(f)
    c["cos"] = np.concatenate([np.cos(ang)] * 2).astype(f)
    c["sin"] = np.concatenate([np.sin(ang), -np.sin(ang)]).astype(f)
    lg = np.log(1.0 - 2.0 ** (-5.0 - np.arange(RH, dtype=np.float64)))
    rel = i[None, :] - i[:, None]
    intra = np.where(rel[:, None, :] >= 0, np.exp(lg[None, :, None] * np.maximum(rel, 0)[:, None, :]), 0.0)
    hc = np.zeros((RH, P, 2 * P + 4))
    hc[:, :, 0:P] = intra.transpose(1, 0, 2)
    hc[:, :, P:2 * P] = np.exp(lg[:, None] * (i + 1.0)[None, :])[:, None, :]
    hc[:, :, 2 * P] = np.exp(lg[:, None] * (P - 1.0 - i)[None, :])
    hc[:, :, 2 * P + 1] = np.exp(lg * P)[:, None]
    hc[:, :, 2 * P + 2] = np.exp(lg)[:, None]
    c["head_const"] = hc.astype(f)
    sel = np.zeros((P, FH, P), f)
    for h in range(FH):
        for part in range(3):
            sel[32 * part + h, h, :] = 1.0
    c["sel_head"] = sel.astype(bf16)
    c["causal"] = np.where(i[None, :] <= i[:, None], 0.0, BIG).astype(bf16)
    c["ident_b"] = np.eye(P, dtype=f).astype(bf16)
    own = (i[:, None] == np.arange(NS)[None, :]).astype(f)
    c["own8"] = np.repeat(own[:, :, None], FH, 2).astype(f)
    c["other8"] = np.repeat(((1 - own) * BIG)[:, :, None], FH, 2).astype(f)
    c["own_col"] = np.ascontiguousarray(np.broadcast_to(np.eye(NS)[None], (P, NS, NS))).astype(f)
    return c



def prepare(nc, g, a, c):
    with ExitStack() as ctx:
        sb = lambda n, s, d=F32: ctx.enter_context(nc.sbuf_tensor(n, s, d))
        sem = lambda n: ctx.enter_context(nc.semaphore(n))
        stage = [sb(f"x_stage{i}", [P, D]) for i in range(2)]
        ids = sb("page_ids", [P, 2], I32)
        rows = [sb(f"logf_rows{i}", [P, PG * FH]) for i in range(2)]
        row_t = sb("logf_rows_t", [P, FH, P])
        total = sb("page_total", [P, FH])
        total_b = sb("page_total_wide", [P, FH, P])
        later_row = sb("later_row", [P, P])
        later_page = sb("later_page", [P, P])
        x_land = [sem(f"x_land{i}") for i in range(2)]
        xs_land, const_land, ids_land = sem("xs_land"), sem("const_land"), sem("ids_land")
        rows_land = [sem(f"rows_land{i}") for i in range(2)]
        x_turned, x_rounded, x_split = sem("x_turned"), sem("x_rounded"), sem("x_split")
        total_done, wide_done, lf_turned, lf_copied, bias_mm, bias_out = (
            sem(n) for n in ("total_done", "wide_done", "lf_turned", "lf_copied", "bias_mm", "bias_out"))
        bias_land = sem("bias_land")
        conv_rows = sb("conv_rows", [20, DFF])
        conv_land, conv_turned, conv_out = sem("conv_land"), sem("conv_turned"), sem("conv_out")
        bank = g.bank

        x_in = a["x_prompt"].rearrange("a (t p) d -> (a t) p d", p=P)
        with nc.Block() as block:
            @block.sync
            def _(sp):
                sp.dma_start(g.ident[:], c["ident"]).then_inc(const_land, 16)
                sp.dma_start(later_row[:], c["later_row"]).then_inc(const_land, 16)
                sp.dma_start(later_page[:], c["later_page"]).then_inc(const_land, 16)
                sp.dma_start(g.dec_bias[:, :, NPG, :], c["other8"]).then_inc(bias_land, 16)
                sp.dma_start(conv_rows[0:16, :], a["state_conv"].rearrange("a b w f -> (a b w) f")).then_inc(conv_land, 16)
                sp.dma_start(conv_rows[16:19, :], a["conv_w"].rearrange("a w f -> (a w) f")).then_inc(conv_land, 16)
                sp.dma_start(conv_rows[19:20, :], a["conv_b"]).then_inc(conv_land, 16)
                with sp.Fori(0, QB // 2) as it:
                    for u in range(2):
                        sp.wait_ge(x_turned, it * 4 + 2 * u + 2)
                        sp.dma_start(stage[u][:], x_in[ds(it * 2 + u, 1)].rearrange("a p d -> (a p) d")).then_inc(x_land[u], 16)
                sp.wait_ge(x_turned, 2 * QB + 2)
                sp.dma_start(stage[0][0:NS, :], a["x_sample"].rearrange("b t d -> (b t) d")).then_inc(xs_land, 16)
                sp.wait_ge(bias_land, 16)

            @block.tensor
            def _(pe):
                pe.nop().then_inc(x_turned, 4)
                pe.nop().then_inc(g.mm_chunk, NCH * RING)
                pe.wait_ge(const_land, 48)

                def turn(q, u, rows_n):
                    for half in range(2):
                        pe.wait_ge(x_split, q * 2 + half + 1)
                        for k in range(4):
                            mm = pe.transpose(bank[half][:, k * P:k * P + rows_n],
                                              stage[u][0:rows_n, (4 * half + k) * P:(4 * half + k + 1) * P],
                                              g.ident[0:rows_n, 0:rows_n])
                        mm.then_inc(x_turned, 1)
                with pe.Fori(0, QB // 2) as it:
                    for u in range(2):
                        pe.wait_ge(x_land[u], it * 16 + 16)
                        turn(it * 2 + u, u, P)
                pe.wait_ge(xs_land, 16)
                turn(QB, 0, NS)
                pe.wait_ge(conv_land, 48)
                for f in range(FT):
                    mm = pe.transpose(bank[7][:, f * 20:(f + 1) * 20], conv_rows[:, f * P:(f + 1) * P], g.ident[0:20, 0:20])
                mm.then_inc(conv_turned, 1)
                for s in range(2):
                    pe.wait_ge(rows_land[s], 16)
                    view = rows[s][:].rearrange("p (r h) -> p h r", h=FH)
                    for hg in range(2):
                        n = 2 * s + hg
                        if n:
                            pe.wait_ge(lf_copied, n)
                        for h in range(4):
                            mm = pe.transpose(bank[2][:, h * P:(h + 1) * P], view[:, 4 * hg + h, :], g.ident[:])
                        mm.then_inc(lf_turned, 1)
                        pe.wait_ge(wide_done, s + 1)
                        pe.wait_ge(lf_copied, n + 1)
                        if n:
                            pe.wait_ge(bias_out, n)
                        for h in range(4):
                            pe.matmul(bank[3][:, h * P:(h + 1) * P], later_row[:], row_t[:, 4 * hg + h, :], start=True, stop=False)
                            mm = pe.matmul(bank[3][:, h * P:(h + 1) * P], total_b[:, 4 * hg + h, :], later_page[:], start=False, stop=True)
                        mm.then_inc(bias_mm, 1)

            @block.scalar
            def _(act):
                def round_half(q, rows_n, dst):
                    for half in range(2):
                        act.wait_ge(x_turned, q * 2 + half + 5)
                        act.activation(dst[:, 4 * half:4 * half + 4, :],
                                       bank[half][:, :].rearrange("p (k t) -> p k t", k=4)[:, :, 0:rows_n],
                                       ACT.Copy).then_inc(x_rounded, 1)
                with act.Fori(0, QB) as q:
                    round_half(q, P, g.xh[:, :, ds(q * P, P)])
                round_half(QB, NS, g.xh[:, :, SEQ:T])
                for n in range(4):
                    act.wait_ge(lf_turned, n + 1)
                    act.activation(row_t[:, 4 * (n % 2):4 * (n % 2) + 4, :],
                                   bank[2][:, :].rearrange("p (h r) -> p h r", h=4), ACT.Copy).then_inc(lf_copied, 1)
                act.wait_ge(conv_turned, 1)
                act.activation(g.conv_cols[:], bank[7][:, 0:FT * 20].rearrange("p (f c) -> p f c", c=20), ACT.Copy).then_inc(conv_out, 1)
                split_hi(g, act, job(0, 0, 0), KD, FH)

            @block.vector
            def _(dve):
                dve.memset(g.eps[:], EPS).then_inc(conv_out, 1)
                dve.nop().then_inc(x_split, 2)
                dve.nop().then_inc(g.w_split, RING)
                for n in range(NCH):
                    dve.nop().then_inc(g.bank_free[n], 1)

                def split_half(q, rows_n, cols):
                    for half in range(2):
                        dve.wait_ge(x_rounded, q * 2 + half + 1)
                        dve.tensor_tensor(g.xl[:, 4 * half:4 * half + 4, cols],
                                          bank[half][:, :].rearrange("p (k t) -> p k t", k=4)[:, :, 0:rows_n],
                                          g.xh[:, 4 * half:4 * half + 4, cols].bitcast(F32),
                                          ALU.subtract).then_inc(x_split, 1)
                with dve.Fori(0, QB) as q:
                    split_half(q, P, ds(q * P, P))
                split_half(QB, NS, slice(SEQ, T))
                for s in range(2):
                    dve.wait_ge(rows_land[s], 16)
                    if s:
                        dve.wait_ge(bias_mm, 2)
                    dve.tensor_reduce(total[:], rows[s][:].rearrange("p (r h) -> p h r", h=FH), AX.X, ALU.add).then_inc(total_done, 1)
                    dve.wait_ge(total_done, s + 1)
                    dve.tensor_copy(total_b[:], total[:].unsqueeze(2).to_broadcast([P, FH, P])).then_inc(wide_done, 1)
                    for hg in range(2):
                        dve.wait_ge(bias_mm, 2 * s + hg + 1)
                        for b in range(4):
                            last = dve.tensor_copy(
                                g.dec_bias[:, 4 * s + b, 0:NPG, 4 * hg:4 * hg + 4].rearrange("p s h -> p h s"),
                                bank[3][:, :].rearrange("p (h b s) -> p b h s", h=4, b=4)[:, b])
                            if b == 3:
                                last.then_inc(bias_out, 1)
                split_lo(g, dve, job(0, 0, 0), KD, FH)

            @block.gpsimd
            def _(pool):
                pool.dma_start(ids[:], a["page_table"].rearrange("(s b) p -> (b p) s", s=2), allow_slow_non_contiguous=True).then_inc(ids_land, 16)
                load_weight(g, pool, job(0, 0, 0), w_in_tile(a, C_FF, FH), KD, FH)
                load_weight(g, pool, job(0, 0, 1), w_in_tile(a, C_FQ))
                pool.wait_ge(ids_land, 16)
                for s in range(2):
                    pool.indirect_dma_start(rows[s][:], None, a["cache_logf"].rearrange("a n r h -> (a n) (r h)"),
                                            bass.IndirectOffsetOnAxis(ap=ids[:, s:s + 1], axis=0)).then_inc(rows_land[s], 16)



def fox(nc, g, a, c, o):
    with ExitStack() as ctx:
        sb = lambda n, s, d=F32: ctx.enter_context(nc.sbuf_tensor(n, s, d))
        sem = lambda n: ctx.enter_context(nc.semaphore(n))
        qT, kT, vT = sb("fq_t", [P, T]), sb("fk_t", [P, T]), sb("fv_t", [P, T])
        kv = [sb(f"kv_rows{u}", [P, QB + 1, 2, P]) for u in range(2)]
        prob = [sb(f"prob{i}", [P, SEQ]) for i in range(2)]
        prob_t = [sb(f"prob_t{i}", [P, QB, P]) for i in range(2)]
        o_rows = sb("fox_rows", [P, QB, P])
        foT = sb("fox_t", [P, SEQ])
        nmax = [sb(f"neg_max{i}", [P, 1]) for i in range(2)]
        psum_row = [sb(f"prob_sum{i}", [P, 1]) for i in range(2)]
        inv = [sb(f"prob_inv{i}", [P, 1]) for i in range(2)]
        causal, ident_b = sb("causal", [P, P], BF16), sb("ident_b", [P, P], BF16)
        sel_all, sel = sb("sel_all", [P, FH, P], BF16), sb("sel_pair", [P, 2, P], BF16)
        nb = sb("neg_cum_parts", [P, SEQ], BF16)
        z, ez, lf = sb("ff_z", [FH, T]), sb("ff_e", [FH, T]), sb("logf", [FH, T])
        zn = sb("ff_neg", [FH, T])
        cum, rest, ones = sb("cum", [FH, SEQ]), sb("cum_rest", [FH, SEQ]), sb("ones8", [FH, SEQ])
        lf_rows = sb("logf_rows_out", [P, QB + 1, FH])
        bf_col = sb("b_f_col", [FH, 1])
        bank = g.bank
        const_land, kv_stored, fo_stored, lf_stored = sem("fox_const"), [sem("kv_stored0"), sem("kv_stored1")], sem("fo_stored"), sem("lf_stored")
        ff_ready, lf_turned, lf_out, parts_ready = (sem(n) for n in ("ff_ready", "lf_turned", "lf_out", "parts_ready"))
        turned, turned_out = sem("kv_turned"), sem("kv_turned_out")
        logits, row_max, expd = sem("logits"), sem("row_max"), sem("expd")
        pt = [sem("prob_turned0"), sem("prob_turned1")]
        pt_out = [sem("prob_t_out0"), sem("prob_t_out1")]
        pv, pv_out, inv_done, sel_ready = sem("pv"), sem("pv_out"), sem("inv_done"), sem("sel_ready")
        fo_turned, fo_out = sem("fo_turned"), sem("fo_out")
        ff_chain, ff_act = sem("ff_chain"), sem("ff_act")
        STEPS = 2 * QB
        LONG = [s for s in range(STEPS) if s // 2 >= 4]

        k_out = o[2].rearrange("d b (t p) h e -> (d b) p t (h e)", p=P)
        v_out = o[3].rearrange("d b (t p) h e -> (d b) p t (h e)", p=P)
        NIT = FH // 4

        with nc.Block() as block:
            @block.gpsimd
            def _(pool):
                with pool.Fori(0, NIT) as it:
                    for u in range(2):
                        for w, col in enumerate((C_FQ, C_FK, C_FV)):
                            j = 3 * u + w
                            if j == 0:
                                continue
                            load_weight(g, pool, job(it * 6 + 1, 1, j), w_in_tile(a, it * (2 * P) + (col + u * P)))
                    load_weight(g, pool, job(it * 6 + 1, 1, 6), w_in_tile(a, (1 - it) * (C_FQ + 2 * P)))

            @block.sync
            def _(sp):
                for dst, src in ((causal, "causal"), (ident_b, "ident_b"), (sel_all, "sel_head")):
                    sp.dma_start(dst[:], c[src]).then_inc(const_land, 16)
                sp.dma_start(bf_col[:], a["b_f"].rearrange("d h -> h d"), allow_slow_non_contiguous=True).then_inc(const_land, 16)
                sp.wait_ge(lf_out, 1)
                sp.dma_start(o[4].rearrange("d b (t p) h -> p (d b t) h", p=P), lf_rows[:, 0:QB, :]).then_inc(lf_stored, 16)
                sp.dma_start(o[7].rearrange("d b t h -> (d b t) h"), lf_rows[0:NS, QB, :]).then_inc(lf_stored, 16)
                with sp.Fori(0, NIT) as it:
                    for u in range(2):
                        pair = it * 2 + u
                        sp.wait_ge(turned_out, (pair + 1) * (QB + 1))
                        sp.dma_start(k_out[0][:, :, ds(pair * P, P)], kv[u][:, 0:QB, 0, :]).then_inc(kv_stored[u], 16)
                        sp.dma_start(v_out[0][:, :, ds(pair * P, P)], kv[u][:, 0:QB, 1, :]).then_inc(kv_stored[u], 16)
                        sp.wait_ge(fo_out, (pair + 1) * QB + 1)
                        sp.dma_start(g.fo_dram[ds(pair, 1), :, 0:SEQ].rearrange("a p t -> (a p) t"), foT[:]).then_inc(fo_stored, 16)
                sp.wait_ge(turned_out, 2 * NIT * (QB + 1))
                sp.dma_start(o[5].rearrange("d b t h e -> (d b t) (h e)"), g.knew[:]).then_inc(lf_stored, 16)
                sp.dma_start(o[6].rearrange("d b t h e -> (d b t) (h e)"), g.vnew[:]).then_inc(lf_stored, 16)
                sp.wait_ge(lf_stored, 64)
                sp.wait_ge(fo_stored, 2 * NIT * 16)
                for u in range(2):
                    sp.wait_ge(kv_stored[u], NIT * 32)

            @block.tensor
            def _(pe):
                product(g, pe, job(0, 0, 0), g.xh, g.xl, m=FH)
                pe.wait_ge(ff_ready, 1)
                for t in range(QB + 1):
                    n = P if t < QB else NS
                    mm = pe.transpose(bank[3][0:n, t * FH:(t + 1) * FH], lf[:, t * P:t * P + n], g.ident[0:FH, 0:FH])
                mm.then_inc(lf_turned, 1)
                pe.wait_ge(const_land, 64)
                pe.wait_ge(parts_ready, 1)
                with pe.Fori(0, NIT) as it:
                    for u in range(2):
                        pair = it * 2 + u
                        for w in range(3):
                            j = 3 * u + w
                            product(g, pe, job(it * 6 + 1, 1, j), g.xh, g.xl)
                        for n in range(NCH):
                            pe.wait_ge(g.bank_free[n], it * 6 + 3 * u + 5)
                        for t in range(QB + 1):
                            n = P if t < QB else NS
                            b = bank[7] if t % 2 == 0 else bank[3]
                            if t >= 2:
                                pe.wait_ge(turned_out, pair * (QB + 1) + t - 1)
                            pe.transpose(b[0:n, 0:P], kT[:, t * P:t * P + n], g.ident[:])
                            mm = pe.transpose(b[0:n, P:2 * P], vT[:, t * P:t * P + n], g.ident[:])
                            if t == QB:
                                mm = pe.transpose(b[0:n, 2 * P:3 * P], qT[:, SEQ:T], g.ident[:])
                            mm.then_inc(turned, 1)
                        pe.wait_ge(turned_out, (pair + 1) * (QB + 1))
                        pe.wait_ge(sel_ready, pair + 1)

                        def qk(s):
                            i, r = s // 2, s % 2
                            rows = slice(r * HD, (r + 1) * HD)
                            pe.wait_ge(expd, pair * STEPS + s + 1)
                            for piece in range(0, i + 1, 4):
                                n = min(4, i + 1 - piece)
                                out = bank[3 + 2 * (s % 2) + piece // 4]
                                last = piece + n == i + 1
                                pe.matmul(out[:, 0:n * P], qT[rows, i * P:(i + 1) * P], kT[rows, piece * P:(piece + n) * P],
                                          start=True, stop=False, skip_group_check=True)
                                mm = pe.matmul(out[:, 0:n * P], sel[:, r, :], nb[:, piece * P:(piece + n) * P],
                                               start=False, stop=not last, skip_group_check=True)
                                if last:
                                    mm = pe.matmul(out[:, (n - 1) * P:n * P], ident_b[:], causal[:],
                                                   start=False, stop=True, skip_group_check=True)
                            mm.then_inc(logits, 1)

                        def turn_prob(s):
                            i = s // 2
                            pe.wait_ge(expd, pair * STEPS + s + 3)
                            for part in range(1 if i < 4 else 2):
                                done = pair * STEPS + s if part == 0 else pair * len(LONG) + LONG.index(s)
                                pe.wait_ge(pt_out[part], done + 1)
                                for n, blk in enumerate(range(4 * part, min(i + 1, 4 * part + 4))):
                                    mm = pe.transpose(bank[part][:, n * P:(n + 1) * P], prob[s % 2][:, blk * P:(blk + 1) * P], g.ident[:])
                                mm.then_inc(pt[part], 1)

                        def values(s):
                            i, r = s // 2, s % 2
                            pe.wait_ge(pt_out[0], pair * STEPS + s + 2)
                            if i >= 4:
                                pe.wait_ge(pt_out[1], pair * len(LONG) + LONG.index(s) + 2)
                            pe.wait_ge(pv_out, pair * STEPS + s + 1)
                            for blk in range(i + 1):
                                mm = pe.matmul(bank[2][:, 0:HD], prob_t[s % 2][:, blk, :], kv[u][:, blk, 1, r * HD:(r + 1) * HD],
                                               start=(blk == 0), stop=(blk == i))
                            mm.then_inc(pv, 1)

                        def turn_out(i):
                            pe.wait_ge(pv_out, pair * STEPS + 2 * i + 3)
                            pe.wait_ge(fo_out, pair * QB + i + 1)
                            pe.transpose(bank[7][:, 0:P], o_rows[:, i, :], g.ident[:]).then_inc(fo_turned, 1)

                        pe.wait_ge(fo_out, pair * QB + 1)
                        qk(0)
                        for s in range(STEPS):
                            if s + 1 < STEPS:
                                qk(s + 1)
                            turn_prob(s)
                            if s >= 1:
                                values(s - 1)
                            if s >= 3 and s % 2 == 1:
                                turn_out((s - 3) // 2)
                        values(STEPS - 1)
                        turn_out(QB - 1)
                        pe.wait_ge(fo_out, (pair + 1) * QB + 1)

            @block.scalar
            def _(act):
                act.nop().then_inc(expd, 2)
                act.nop().then_inc(pt_out[1], 1)
                act.nop().then_inc(fo_out, 1)
                split_hi(g, act, job(0, 0, 1))
                act.wait_ge(const_land, 64)
                for n in range(NCH):
                    chunk_ready(g, act, 0, n)
                    act.activation(z[:, chunk(n)], bank[n][0:FH, 0:TC], ACT.Identity, bias=bf_col[:]).then_inc(g.bank_free[n], 1)
                act.wait_ge(ff_chain, 2)
                act.activation(ez[:], zn[:], ACT.Exp).then_inc(ff_act, 1)
                act.wait_ge(ff_act, 1)
                act.activation(ez[:], ez[:], ACT.Ln, bias=1.0).then_inc(ff_act, 1)
                act.wait_ge(lf_turned, 1)
                act.activation(lf_rows[:, 0:QB, :], bank[3][:, 0:QB * FH].rearrange("p (t h) -> p t h", h=FH), ACT.Copy)
                act.activation(g.lfnew[:], bank[3][0:NS, QB * FH:(QB + 1) * FH], ACT.Copy)
                act.activation(lf_rows[0:NS, QB, :], bank[3][0:NS, QB * FH:(QB + 1) * FH], ACT.Copy).then_inc(lf_out, 1)

                with act.Fori(0, NIT) as it:
                    for u in range(2):
                        pair = it * 2 + u
                        j0 = it * 6 + 1 + 3 * u
                        for w, dst in ((0, qT), (1, kT)):
                            split_hi(g, act, job(it * 6 + 1, 1, 3 * u + w + 1))
                            for n in range(NCH):
                                chunk_ready(g, act, j0 + w, n)
                                act.activation(dst[:, chunk(n)], bank[n][:, 0:TC], ACT.Copy,
                                               scale=HD ** -0.5 if w == 0 else 1.0).then_inc(g.bank_free[n], 1)
                        split_hi(g, act, job(it * 6 + 1, 1, 3 * u + 3))
                        act.wait_ge(kv_stored[u], it * 32)
                        for t in range(QB + 1):
                            n = P if t < QB else NS
                            b = bank[7] if t % 2 == 0 else bank[3]
                            act.wait_ge(turned, pair * (QB + 1) + t + 1)
                            if t == QB:
                                act.activation(g.knew[:, ds(pair * P, P)], b[0:NS, 0:P], ACT.Copy)
                                act.activation(g.vnew[:, ds(pair * P, P)], b[0:NS, P:2 * P], ACT.Copy)
                                act.activation(g.qnew[:, ds(pair * P, P)], b[0:NS, 2 * P:3 * P], ACT.Copy).then_inc(turned_out, 1)
                            else:
                                act.activation(kv[u][:, t, :, :], b[:, 0:2 * P].rearrange("p (w e) -> p w e", w=2), ACT.Copy).then_inc(turned_out, 1)

                        def softmax(s):
                            i = s // 2
                            act.wait_ge(row_max, pair * STEPS + s + 1)
                            act.wait_ge(pt_out[0], pair * STEPS + s)
                            act.wait_ge(pt_out[1], pair * len(LONG) + max(0, s - 2 - LONG[0] + 1) + 1)
                            act.wait_ge(inv_done, pair * STEPS + s + 1)
                            span = (i + 1) * P
                            act.activation(prob[s % 2][:, 0:span], g.pair[s % 2][:, 0:span], ACT.Exp,
                                           bias=nmax[s % 2][:], accum_out=psum_row[s % 2][:]).then_inc(expd, 1)

                        softmax(0)
                        for s in range(STEPS):
                            if s + 1 < STEPS:
                                softmax(s + 1)
                            if s in LONG:
                                n = s // 2 + 1 - 4
                                act.wait_ge(pt[1], pair * len(LONG) + LONG.index(s) + 1)
                                act.activation(prob_t[s % 2][:, 4:4 + n, :], bank[1][:, 0:n * P].rearrange("p (b t) -> p b t", t=P), ACT.Copy).then_inc(pt_out[1], 1)
                            if s >= 3 and s % 2 == 1:
                                fo_copy(g, act, pair, (s - 3) // 2, fo_turned, fo_out, fo_stored, foT)
                        fo_copy(g, act, pair, QB - 1, fo_turned, fo_out, fo_stored, foT)

            @block.vector
            def _(dve):
                dve.nop().then_inc(pt_out[0], 1)
                dve.nop().then_inc(pv_out, 1)
                dve.nop().then_inc(inv_done, 2)
                split_lo(g, dve, job(0, 0, 1))
                dve.memset(ones[:], 1.0)
                dve.memset(nb[:], 0.0)
                for n in range(NCH):
                    dve.wait_ge(g.bank_free[n], 2)
                ch = Chain(dve, ff_chain)
                ch.link(dve.tensor_scalar(zn[:], z[:], -1.0, None, ALU.mult))
                ch.link(dve.tensor_tensor(zn[:], zn[:], z[:], ALU.min))
                dve.wait_ge(ff_act, 2)
                ch.link(dve.scalar_tensor_tensor(lf[:], z[:], 0.0, ez[:], ALU.min, ALU.subtract))
                dve.nop().then_inc(ff_ready, 1)
                ch.link(dve.tensor_tensor_scan(cum[:], ones[:], lf[:, 0:SEQ], 0.0, ALU.mult, ALU.add))
                ch.link(dve.tensor_scalar(cum[:], cum[:], -1.0, None, ALU.mult))
                for part in range(3):
                    out = nb[32 * part:32 * part + FH, :]
                    src = cum if part == 0 else rest
                    ch.link(dve.tensor_copy(out, src[:]))
                    if part < 2:
                        ch.link(dve.tensor_copy(zn[:, 0:SEQ], out))
                        ch.link(dve.tensor_tensor(rest[:], src[:], zn[:, 0:SEQ], ALU.subtract))
                dve.nop().then_inc(parts_ready, 1)
                dve.wait_ge(const_land, 64)

                with dve.Fori(0, NIT) as it:
                    for u in range(2):
                        pair = it * 2 + u
                        j0 = it * 6 + 1 + 3 * u
                        for w in range(3):
                            split_lo(g, dve, job(it * 6 + 1, 1, 3 * u + w + 1))
                            if w == 1:
                                dve.wait_ge(pv, pair * STEPS)
                                dve.tensor_copy(sel[:], sel_all[:, ds(pair * 2, 2), :]).then_inc(sel_ready, 1)
                        for n in range(NCH):
                            chunk_ready(g, dve, j0 + 2, n)
                            dve.tensor_copy(vT[:, chunk(n)], bank[n][:, 0:TC]).then_inc(g.bank_free[n], 1)

                        def maxima(s):
                            i = s // 2
                            dve.wait_ge(logits, pair * STEPS + s + 1)
                            dve.tensor_reduce(nmax[s % 2][:], g.pair[s % 2][:, 0:(i + 1) * P], AX.X, ALU.max, negate=True).then_inc(row_max, 1)

                        def normalise(s):
                            i, r = s // 2, s % 2
                            dve.wait_ge(pv, pair * STEPS + s + 1)
                            dve.wait_ge(fo_out, pair * QB + 1)
                            dve.tensor_scalar(o_rows[:, i, r * HD:(r + 1) * HD], bank[2][:, 0:HD], inv[s % 2][:], None, ALU.mult).then_inc(pv_out, 1)

                        maxima(0)
                        for s in range(STEPS):
                            if s + 1 < STEPS:
                                maxima(s + 1)
                            n = min(s // 2 + 1, 4)
                            dve.wait_ge(pt[0], pair * STEPS + s + 1)
                            dve.tensor_copy(prob_t[s % 2][:, 0:n, :], bank[0][:, 0:n * P].rearrange("p (b t) -> p b t", t=P)).then_inc(pt_out[0], 1)
                            dve.wait_ge(pv_out, pair * STEPS + s)
                            dve.reciprocal(inv[s % 2][:], psum_row[s % 2][:]).then_inc(inv_done, 1)
                            dve.wait_ge(inv_done, pair * STEPS + s + 3)
                            if s >= 1:
                                normalise(s - 1)
                        normalise(STEPS - 1)


def fo_copy(g, act, pair, i, fo_turned, fo_out, fo_stored, foT):
    if i == 0:
        act.wait_ge(fo_stored, pair * 16)
    act.wait_ge(fo_turned, pair * QB + i + 1)
    act.activation(foT[:, i * P:(i + 1) * P], g.bank[7][:, 0:P], ACT.Copy).then_inc(fo_out, 1)



GRP = 2
NG = NPG // GRP
SLOTS = 4
VALUES_A = (1,) * 6 + (1,) * 3 + (1,) * 7
KEYS_A = (1, 2, 1, 1, 2, 1) + (1,) * 3 + (1, 1, 1, 1, 1, 0, 0)
VALUES_B = (1,) * 12 + (2, 2)
VALUES_B_LAST = (2,) * 8
KEYS_B = (1,) + (1, 1, 1, 0) + (3,) + (1,) * 6 + (1, 1, 1, 0)
assert all(sum(s) == NG for s in (VALUES_A, KEYS_A, VALUES_B, VALUES_B_LAST, KEYS_B))


def take(counts, e):
    return range(sum(counts[:e]), sum(counts[:e + 1]))


def share(total, parts, e):
    return range(total * e // parts, total * (e + 1) // parts)


def retain(nc, g, a, c, o):
    with ExitStack() as ctx:
        sb = lambda n, s, d=F32: ctx.enter_context(nc.sbuf_tensor(n, s, d))
        sem = lambda n: ctx.enter_context(nc.semaphore(n))
        keys = [sb(f"cache_keys{i}", [P, GRP, FH * HD]) for i in range(SLOTS)]
        vals = [sb(f"cache_vals{i}", [P, GRP, FH * HD]) for i in range(SLOTS)]
        pages = sb("page_list", [1, NS * NPG], I32)
        qb = [sb(f"q_wide{i}", [P, FH * HD]) for i in range(2)]
        score = [sb(f"score{i}", [P, NPG + 1, FH]) for i in range(2)]
        new_prod = g.qnew
        own8 = sb("own8", [NS, NS, FH])
        own = sb("own", [NS, NS])
        own_col = sb("own_col", [P, NS, NS])
        mx, gmx = sb("cache_max", [P, FH]), sb("cache_max_all", [P, FH])
        psum_p = [sb(f"cache_prob_sum{i}", [P, FH]) for i in range(2)]
        ones_col = sb("ones_col", [P, 1])
        inv_l, o_dec = sb("dec_inv", [P, 1]), sb("dec_out", [P, P])
        fos = sb("fox_sample_t", [P, FH // 2, NS])
        cos, sin = sb("cos", [P, T]), sb("sin", [P, T])
        hc = sb("head_const", [P, 2 * P + 4])
        gn = sb("group_norm_cols", [P, 2, 2])
        rqT, rkT = sb("rq_t", [P, T]), sb("rk_t", [P, T])
        rvT = sb("rv_t", [P, 2, T])
        t1, t2 = sb("rot_cos", [P, TC]), sb("rot_sin", [P, TC])
        krows = sb("rk_rows", [P, QB + 1, P])
        vrows = sb("rv_rows", [P, QB + 1, DV])
        qd = sb("q_decayed_t", [P, QB, P])
        inner = sb("inner_t", [P, QB, P])
        state = [sb(f"state{i}", [P, DV]) for i in range(3)]
        st_s = sb("state_samples", [P, NS, DV])
        kmask = inner[0:NS]
        qmask = sb("q_own", [P, NS, NS])
        stats, mv = sb("gn_stats", [P, 6]), sb("gn_mean_var", [P, QB + 1, 2])
        rstd = sb("gn_rstd", [P, QB + 1])
        sg = [t1, t2]
        bank = g.bank

        const_land, hc_land, q_stored, qb_land = sem("ret_const"), sem("hc_land"), sem("q_stored"), [sem("qb_land0"), sem("qb_land1")]
        k_land, v_land = [sem(f"k_land{i}") for i in range(SLOTS)], [sem(f"v_land{i}") for i in range(SLOTS)]
        k_used, v_used = sem("k_used"), sem("v_used")
        k_mult, new_mult, biased, maxed, gmaxed = (sem(n) for n in ("k_mult", "new_mult", "biased", "maxed", "gmaxed"))
        shifted, prob, summed, pv, normed, turned, fos_out, fos_stored = (
            sem(n) for n in ("dec_shifted", "dec_prob", "dec_summed", "dec_pv", "dec_normed", "dec_turned", "dec_fos_out", "dec_fos_stored"))
        inv_ready, setup = sem("dec_inv_ready"), sem("ret_setup")
        rot_part, rot = sem("rot_part"), sem("rot")
        rows_t, rows_out = sem("rows_turned"), sem("rows_out")
        qd_done, ik, ik_out, st_new = sem("qd_done"), sem("ik"), sem("inner_out"), sem("state_new")
        o_mm, o_out, stat, mean, rstd_part, rstd_done, gnd = (sem(n) for n in ("ret_o", "ret_o_out", "gn_stat", "gn_mean", "rstd_part", "rstd_done", "gn_done"))
        rn_t, rn_out = sem("rn_turned"), sem("rn_out")
        gated, g_stored, st_stored, fin_stored = sem("gated"), sem("g_stored"), sem("st_stored"), sem("fin_stored")
        masks, s_land, kv_s, s_new = sem("own_masks"), sem("s_land"), sem("kv_sample"), sem("s_new")
        J0 = 13
        NJ = 6
        IN, QDEC = slice(0, P), slice(P, 2 * P)
        KDEC, CDEC, RDEC = (slice(2 * P + i, 2 * P + i + 1) for i in range(3))
        COLS = (C_RQ, C_RK, C_RV, C_RV + P, C_RG, C_RG + P)
        STEP = (DK, DK, DV, DV, DV, DV)
        NB = QB + 1

        def heads(eng, body):
            with eng.Fori(0, RH - 1) as h:
                body(h, False)
            body(RH - 1, True)

        with nc.Block() as block:
            @block.sync
            def _(sp):
                for dst, src in ((cos, "cos"), (sin, "sin"), (own_col, "own_col")):
                    sp.dma_start(dst[:], c[src]).then_inc(const_land, 16)
                sp.dma_start(own8[:], c["own8"][0:NS]).then_inc(const_land, 16)
                sp.dma_start(own[:], c["own8"][0:NS, :, 0], allow_slow_non_contiguous=True).then_inc(const_land, 16)
                sp.dma_start(pages[:], a["page_table"].rearrange("(a b) p -> a (b p)", a=1)).then_inc(const_land, 16)
                sp.dma_start(g.q_dram, g.qnew[:]).then_inc(q_stored, 16)
                sp.wait_ge(q_stored, 16)
                sp.wait_ge(const_land, 96)

                def load_q(n, u):
                    sp.dma_start(qb[u][:], g.q_dram[ds(n, 1), :].to_broadcast([P, FH * HD])).then_inc(qb_land[u], 16)

                def page_ids(n, q):
                    at = ds(n * NPG + q * (SLOTS * GRP), SLOTS * GRP)
                    return nc.values_load_multi_w_load_instructions(pages[0:1, at], [mybir.EngineType.SP],
                                                                    min_val=0, max_val=POOL - 1)[1]

                def load_group(ring, land, used, cache, n, q, slot, ids):
                    sp.wait_ge(used, n * NG + q * SLOTS + slot + 1)
                    for p in range(GRP):
                        page = cache[ds(ids[slot * GRP + p], 1)].rearrange("n r h e -> (n r) (h e)")
                        sp.dma_start(ring[slot][:, p, :], page).then_inc(land[slot], 16)

                ck, cv = (a[n].rearrange("a n r h e -> (a n) r h e") for n in ("cache_k", "cache_v"))
                load_q(0, 0)
                load_q(1, 1)
                with sp.Fori(0, NG // SLOTS) as q:
                    ids = page_ids(0, q)
                    for slot in range(SLOTS):
                        load_group(keys, k_land, k_used, ck, 0, q, slot, ids)

                def period(n):
                    with sp.Fori(0, NG // SLOTS) as q:
                        key_ids, value_ids = page_ids(n + 1, q), page_ids(n, q)
                        for slot in range(SLOTS):
                            load_group(keys, k_land, k_used, ck, n + 1, q, slot, key_ids)
                            load_group(vals, v_land, v_used, cv, n, q, slot, value_ids)

                with sp.Fori(0, RH - 1) as h:
                    for u in range(2):
                        period(h * 2 + u)
                        sp.wait_ge(new_mult, h * 2 + u + 1)
                        load_q(h * 2 + u + 2, u)
                period(NS - 2)
                with sp.Fori(0, NG // SLOTS) as q:
                    ids = page_ids(NS - 1, q)
                    for slot in range(SLOTS):
                        load_group(vals, v_land, v_used, cv, NS - 1, q, slot, ids)
                sp.wait_ge(fos_out, NS)
                for j in range(FH // 2):
                    sp.dma_start(g.fo_dram[j, :, SEQ:T], fos[:, j, :]).then_inc(fos_stored, 16)
                sp.wait_ge(fos_stored, 16 * (FH // 2))

            @block.gpsimd
            def _(pool):
                def all_max(n):
                    wait_apart(pool, maxed, n + 1, g.mm_chunk)
                    pool.partition_all_reduce(gmx[:], mx[:], P, bass.bass_isa.ReduceOp.max).then_inc(gmaxed, 1)

                def load(h, j):
                    k = j % NJ
                    load_weight(g, pool, job(h * NJ + J0, 1, j), w_in_tile(a, h * STEP[k] + (COLS[k] + j // NJ * STEP[k])))

                for j in range(1, 5):
                    load(0, j)
                all_max(0)

                def body(h, last):
                    pool.wait_ge(gated, h * 6)
                    pool.dma_start(hc[:], c["head_const"][ds(h, 1)].rearrange("a p c -> (a p) c")).then_inc(hc_land, 16)
                    for w, name in enumerate(("ret_gn_w", "ret_gn_b")):
                        pool.dma_start(gn[:, w, :], a[name].rearrange("a (h e p) -> p (a h) e", e=2, p=P)[:, ds(h, 1), :].rearrange("p a e -> p (a e)"),
                                       allow_slow_non_contiguous=True).then_inc(hc_land, 16)
                    load(h, 5)
                    pool.wait_ge(st_stored, h * 16)
                    pool.dma_start(st_s[:], a["state_ret"].rearrange("a b h d e -> d (a h) b e")[:, ds(h, 1)].rearrange("d a b e -> d (a b) e")).then_inc(s_land, 16)
                    pool.wait_ge(hc_land, h * 48 + 48)
                    pool.wait_ge(rot, h * 6 + 3)
                    for t in range(QB):
                        ins = pool.tensor_tensor(qd[:, t, :], rqT[:, t * P:(t + 1) * P], hc[:, QDEC], ALU.mult)
                    ins.then_inc(qd_done, 1)
                    if last:
                        load_weight(g, pool, job(h * NJ + J0, 1, 6), w_in_tile(a, C_GA))
                    else:
                        load(h, 6)
                    all_max(h * 2 + 1)
                    if not last:
                        for j in range(7, 11):
                            load(h, j)
                        all_max(h * 2 + 2)
                heads(pool, body)

            @block.tensor
            def _(pe):
                def cache_values(n, u, i, first):
                    slot = i % SLOTS
                    if first:
                        pe.wait_ge(prob, n + 1)
                        pe.wait_ge(fos_out, n)
                    pe.wait_ge(v_land[slot], n * (NG // SLOTS * GRP * 16) + (i // SLOTS + 1) * GRP * 16)
                    for p in range(GRP):
                        for j in range(4):
                            mm = pe.matmul(bank[7][32 * j:32 * j + 2, 0:P], score[u][:, i * GRP + p, 2 * j:2 * j + 2],
                                           vals[slot][:, p, j * P:(j + 1) * P], start=(first and p == 0), stop=False)
                    mm.then_inc(v_used, 1)

                def cache_tail(n, u):
                    for j in range(4):
                        pe.matmul(bank[7][32 * j:32 * j + 2, 0:P], score[u][0:NS, NPG, 2 * j:2 * j + 2],
                                  g.vnew[:, j * P:(j + 1) * P], start=False, stop=True)
                    pe.wait_ge(summed, n + 1)
                    for j in range(4):
                        mm = pe.matmul(bank[7][32 * j:32 * j + 2, P:P + 1], psum_p[u][:, 2 * j:2 * j + 2],
                                       ones_col[:], start=True, stop=True)
                    mm.then_inc(pv, 1)

                def cache_turn(n):
                    pe.wait_ge(normed, n + 1)
                    pe.transpose(bank[7][:, 2 * P:3 * P], o_dec[:], g.ident[:]).then_inc(turned, 1)

                pe.nop().then_inc(v_used, SLOTS)
                pe.wait_ge(setup, 1)

                for w in range(2):
                    product(g, pe, job(J0, 1, w), g.xh, g.xl)

                def body(h, last):
                    def values_a(e):
                        for i in take(VALUES_A, e):
                            cache_values(h * 2, 0, i, i == 0)

                    def values_b(e):
                        for i in take(VALUES_B_LAST if last else VALUES_B, e):
                            cache_values(h * 2 + 1, 1, i, i == 0)

                    def ending(n):
                        if n == 0:
                            cache_tail(h * 2 + 1, 1)
                        elif n == 2:
                            cache_turn(h * 2 + 1)

                    for w in (2, 3):
                        product(g, pe, job(h * NJ + J0, 1, w), g.xh, g.xl, after=lambda n, w=w: values_a(3 * (w - 2) + n))
                    for n in range(NCH):
                        pe.wait_ge(g.bank_free[n], h * NJ + J0 + 5)
                    pe.wait_ge(rot, h * 6 + 6)
                    for t in range(NB):
                        n = P if t < QB else NS
                        b = bank[3] if t % 2 == 0 else bank[6]
                        if t >= 2:
                            pe.wait_ge(rows_out, h * NB + t - 1)
                        pe.transpose(b[0:n, 0:P], rkT[:, t * P:t * P + n], g.ident[:])
                        for e in range(2):
                            mm = pe.transpose(b[0:n, (1 + e) * P:(2 + e) * P], rvT[:, e, t * P:t * P + n], g.ident[:])
                        mm.then_inc(rows_t, 1)
                        if t % 3 == 2:
                            values_a(6 + t // 3)
                    pe.wait_ge(qd_done, h + 1)

                    def out(t):
                        b = bank[3] if t % 2 == 0 else bank[6]
                        pe.wait_ge(ik_out, h * QB + t + 1)
                        if t >= 1:
                            pe.wait_ge(st_new, h * QB + t)
                        if t >= 2:
                            pe.wait_ge(o_out, h * NB + t - 1)
                        mm = pe.matmul(b[:, 0:DV], inner[:, t, :], vrows[:, t, :], start=True, stop=(t == 0))
                        if t:
                            mm = pe.matmul(b[:, 0:DV], qd[:, t, :], state[t % 3][:], start=False, stop=True)
                        mm.then_inc(o_mm, 1)

                    for t in range(QB):
                        pe.wait_ge(rows_out, h * NB + max(t + 1, NB if t == 0 else 0))
                        if t >= 2:
                            pe.wait_ge(ik_out, h * QB + t - 1)
                            pe.wait_ge(st_new, h * QB + t - 1)
                        b = bank[4 + t % 2]
                        pe.matmul(b[:, 0:P], rkT[:, t * P:(t + 1) * P], rqT[:, t * P:(t + 1) * P], start=True, stop=True)
                        pe.matmul(b[:, P:P + DV], krows[:, t, :], vrows[:, t, :], start=True, stop=True).then_inc(ik, 1)
                        if t >= 1:
                            out(t - 1)
                        if t < QB - 1:
                            values_a(9 + t)
                        if t == QB - 2:
                            cache_tail(h * 2, 0)
                    out(QB - 1)
                    cache_turn(h * 2)
                    pe.wait_ge(masks, h * 2 + 2)
                    pe.wait_ge(st_new, (h + 1) * QB)
                    for b_ in range(NS):
                        if b_ >= 2:
                            pe.wait_ge(s_new, h * NS + b_ - 1)
                        pe.matmul(bank[4 + b_ % 2][:, 0:DV], kmask[:, b_, :], vrows[0:NS, QB, :], start=True, stop=True).then_inc(kv_s, 1)
                    values_b(0)
                    pe.wait_ge(o_out, h * NB + QB)
                    for b_ in range(NS):
                        pe.wait_ge(s_new, h * NS + b_ + 1)
                        mm = pe.matmul(bank[3][0:NS, 0:DV], qmask[:, b_, :], st_s[:, b_, :], start=(b_ == 0), stop=(b_ == NS - 1))
                    mm.then_inc(o_mm, 1)
                    values_b(1)
                    product(g, pe, job(h * NJ + J0, 1, 4), g.xh, g.xl, after=lambda n: values_b(2 + n))
                    for t in range(NB):
                        n = P if t < QB else NS
                        b = bank[3] if t % 2 == 0 else bank[6]
                        pe.wait_ge(gnd, h * NB + t + 1)
                        if t >= 2:
                            wait_apart(pe, rn_out, h * 2 * NB + 2 * t - 2, g.w_split)
                        for e in range(2):
                            mm = pe.transpose(b[:, e * P:e * P + n], vrows[0:n, t, e * P:(e + 1) * P], g.ident[0:n, 0:n])
                        mm.then_inc(rn_t, 1)
                        if t % 3 == 2:
                            values_b(5 + t // 3)
                    if last:
                        product(g, pe, job(h * NJ + J0, 1, 5), g.xh, g.xl, after=ending)
                    else:
                        product(g, pe, job(h * NJ + J0, 1, 5), g.xh, g.xl, after=lambda n: values_b(8 + n))
                        product(g, pe, job(h * NJ + J0, 1, 6), g.xh, g.xl, after=lambda n: values_b(11 + n))
                        product(g, pe, job(h * NJ + J0, 1, 7), g.xh, g.xl, after=ending)
                    pe.wait_ge(rn_out, (h + 1) * 2 * NB)
                heads(pe, body)

            @block.scalar
            def _(act):
                def cache_exp(n, u):
                    act.wait_ge(shifted, n + 1)
                    act.activation(score[u][:], score[u][:], ACT.Exp).then_inc(prob, 1)

                split_hi(g, act, job(J0, 1, 1))
                split_hi(g, act, job(J0, 1, 2))
                cache_exp(0, 0)

                def body(h, last):
                    nxt = lambda w: split_hi(g, act, job(h * NJ + J0, 1, w + 1))
                    for w in (2, 3):
                        nxt(w)
                        for n in range(NCH):
                            chunk_ready(g, act, h * NJ + J0 + w, n)
                            if w == 2 and n == 0:
                                act.wait_ge(g_stored, h * 32)
                            act.activation(rvT[:, w - 2, chunk(n)], bank[n][:, 0:TC], ACT.Copy).then_inc(g.bank_free[n], 1)
                    act.wait_ge(hc_land, h * 48 + 48)
                    for t in range(NB):
                        n = P if t < QB else NS
                        b = bank[3] if t % 2 == 0 else bank[6]
                        act.wait_ge(rows_t, h * NB + t + 1)
                        if t < QB:
                            act.activation(krows[:, t, :], b[:, 0:P], ACT.Copy, scale=hc[:, KDEC])
                        else:
                            act.activation(krows[0:n, t, :], b[0:n, 0:P], ACT.Copy)
                        act.activation(vrows[0:n, t, :], b[0:n, P:P + DV], ACT.Copy).then_inc(rows_out, 1)
                    for t in range(NB):
                        n = P if t < QB else NS
                        b = bank[3] if t % 2 == 0 else bank[6]
                        act.wait_ge(o_mm, h * NB + t + 1)
                        act.activation(vrows[0:n, t, :], b[0:n, 0:DV], ACT.Copy).then_inc(o_out, 1)
                        if t == QB - 1:
                            cache_exp(h * 2 + 1, 1)
                            nxt(4)
                    act.wait_ge(st_new, (h + 1) * QB)
                    act.dma_start(o[8].rearrange("a b h d e -> (a b h) d e")[ds(h, 1)].rearrange("a d e -> (a d) e"), state[QB % 3][:]).then_inc(fin_stored, 16)
                    act.wait_ge(s_new, (h + 1) * NS)
                    act.dma_start(o[9].rearrange("a b h d e -> d (a h) b e")[:, ds(h, 1)].rearrange("d a b e -> d (a b) e"), st_s[:]).then_inc(st_stored, 16)
                    act.wait_ge(rstd_part, h * 2 + 1)
                    act.activation(rstd[:], mv[:, :, 1], ACT.Sqrt).then_inc(rstd_part, 1)
                    for t in range(NB):
                        n = P if t < QB else NS
                        b = bank[3] if t % 2 == 0 else bank[6]
                        act.wait_ge(rn_t, h * NB + t + 1)
                        for e in range(2):
                            act.activation(rvT[:, e, t * P:t * P + n], b[:, e * P:e * P + n], ACT.Identity,
                                           scale=gn[:, 0, e:e + 1], bias=gn[:, 1, e:e + 1]).then_inc(rn_out, 1)
                    for w in (4, 5):
                        if w == 5:
                            nxt(5)
                        for n in range(NCH):
                            k = 3 * (w - 4) + n
                            chunk_ready(g, act, h * NJ + J0 + w, n)
                            act.wait_ge(gated, h * 6 + max(0, k - 1))
                            act.activation(sg[k % 2][:], bank[n][:, 0:TC], ACT.Silu).then_inc(g.bank_free[n], 1)
                        act.wait_ge(gated, h * 6 + 3 * (w - 3))
                        act.dma_start(g.g_dram[ds(h * 2 + (w - 4), 1)].rearrange("a p t -> (a p) t"), rvT[:, w - 4, :]).then_inc(g_stored, 16)
                    if not last:
                        nxt(6)
                        nxt(7)
                        cache_exp(h * 2 + 2, 0)
                heads(act, body)
                act.wait_ge(g_stored, RH * 32)
                act.wait_ge(st_stored, RH * 16)
                act.wait_ge(fin_stored, RH * 16)

            @block.vector
            def _(dve):
                def cache_logits(n, u, i):
                    if i < NG:
                        slot = i % SLOTS
                        if i == 0:
                            dve.wait_ge(qb_land[u], wide_count(n, u))
                        dve.wait_ge(k_land[slot], n * (NG // SLOTS * GRP * 16) + (i // SLOTS + 1) * GRP * 16)
                        dve.tensor_tensor(keys[slot][:], keys[slot][:], qb[u][:].unsqueeze(1).to_broadcast([P, GRP, FH * HD]), ALU.mult).then_inc(k_mult, 1)
                    if i >= 1:
                        slot = (i - 1) % SLOTS
                        dve.wait_ge(k_mult, n * NG + i)
                        dve.tensor_reduce(score[u][:, (i - 1) * GRP:i * GRP, :],
                                          keys[slot][:].rearrange("p g (h e) -> p g h e", e=HD), AX.X, ALU.add).then_inc(k_used, 1)

                def wide_count(n, u):
                    return (n - u) * 8 + 16

                def cache_max(n, u):
                    cache_logits(n, u, NG)
                    dve.tensor_tensor(new_prod[:], g.knew[:], qb[u][0:NS, :], ALU.mult).then_inc(new_mult, 1)
                    dve.wait_ge(new_mult, n + 1)
                    dve.tensor_reduce(score[u][0:NS, NPG, :], new_prod[:].rearrange("p (h e) -> p h e", e=HD), AX.X, ALU.add).then_inc(biased, 1)
                    dve.wait_ge(biased, n * 2 + 1)
                    dve.wait_ge(k_used, (n + 1) * NG + SLOTS)
                    dve.tensor_tensor(score[u][:], score[u][:], g.dec_bias[:, ds(n, 1)].rearrange("p a s h -> p (a s) h"), ALU.add).then_inc(biased, 1)
                    dve.wait_ge(biased, n * 2 + 2)
                    dve.tensor_reduce(mx[:], score[u][:].rearrange("p s h -> p h s"), AX.X, ALU.max).then_inc(maxed, 1)

                def cache_shift(n, u):
                    dve.wait_ge(gmaxed, n + 1)
                    dve.tensor_tensor(score[u][:], score[u][:], gmx[:].unsqueeze(1).to_broadcast([P, NPG + 1, FH]), ALU.subtract).then_inc(shifted, 1)

                def cache_sum(n, u):
                    dve.wait_ge(prob, n + 1)
                    dve.tensor_reduce(psum_p[u][:], score[u][:].rearrange("p s h -> p h s"), AX.X, ALU.add).then_inc(summed, 1)

                def cache_norm(n):
                    dve.wait_ge(pv, n + 1)
                    dve.reciprocal(inv_l[:], bank[7][:, P:P + 1]).then_inc(inv_ready, 1)
                    dve.wait_ge(inv_ready, n + 1)
                    dve.tensor_scalar(o_dec[:], bank[7][:, 0:P], inv_l[:], None, ALU.mult).then_inc(normed, 1)

                def cache_out(n):
                    dve.wait_ge(turned, n + 1)
                    for r in range(2):
                        rows = slice(r * HD, (r + 1) * HD)
                        ins = dve.tensor_copy(fos[rows, :, ds(n, 1)].rearrange("p j n -> p (j n)"),
                                              bank[7][rows, 2 * P + r:3 * P:32])
                    ins.then_inc(fos_out, 1)

                dve.nop().then_inc(k_used, SLOTS)
                dve.wait_ge(q_stored, 16)
                dve.wait_ge(const_land, 96)
                dve.memset(ones_col[:], 1.0)
                dve.memset(bank[7][:, :], 1.0)
                dve.memset(mv[:], 1.0)
                for u in range(2):
                    dve.memset(score[u][:], 0.0)
                dve.tensor_tensor(own8[:], own8[:], g.lfnew[:].unsqueeze(1).to_broadcast([NS, NS, FH]), ALU.mult).then_inc(setup, 1)
                dve.wait_ge(setup, 1)
                dve.tensor_tensor(g.dec_bias[0:NS, :, NPG, :], g.dec_bias[0:NS, :, NPG, :], own8[:], ALU.subtract).then_inc(setup, 1)
                dve.wait_ge(setup, 2)
                def rotate(j, r0, w, n):
                    dst, scale, k, b = (rqT, rkT)[w], (1.0, DK ** -0.5)[w], 3 * w + n, bank[n]
                    chunk_ready(g, dve, j, n)
                    dve.wait_ge(rot, r0 + k)
                    dve.scalar_tensor_tensor(t1[:], b[:, 0:TC], scale, cos[:, chunk(n)], ALU.mult, ALU.mult).then_inc(rot_part, 1)
                    for r in range(2):
                        src, out = slice((1 - r) * 64, (2 - r) * 64), slice(r * 64, (r + 1) * 64)
                        ins = dve.scalar_tensor_tensor(t2[out, :], b[src, 0:TC], scale, sin[src, chunk(n)], ALU.mult, ALU.mult)
                    ins.then_inc(g.bank_free[n], 1)
                    dve.wait_ge(g.bank_free[n], j + 2)
                    dve.tensor_tensor(dst[:, chunk(n)], t1[:], t2[:], ALU.add).then_inc(rot, 1)

                for w in range(2):
                    split_lo(g, dve, job(J0, 1, w + 1))
                    for n in range(NCH):
                        rotate(J0 + w, 0, w, n)
                        for i in share(NG, 6, 3 * w + n):
                            cache_logits(0, 0, i)
                cache_max(0, 0)
                cache_shift(0, 0)

                def body(h, last):
                    def keys_a(e):
                        for i in take(KEYS_A, e):
                            cache_logits(h * 2 + 1, 1, i)

                    def keys_b(e):
                        if not last:
                            for i in take(KEYS_B, e):
                                cache_logits(h * 2 + 2, 0, i)

                    nxt = lambda w: split_lo(g, dve, job(h * NJ + J0, 1, w + 1))
                    nxt(2)
                    keys_a(0)
                    cache_sum(h * 2, 0)
                    for e in range(1, 6):
                        keys_a(e)
                    nxt(3)
                    for e in range(6, 9):
                        keys_a(e)
                    for t in range(QB):
                        b = bank[4 + t % 2]
                        dve.wait_ge(ik, h * QB + t + 1)
                        dve.tensor_tensor(inner[:, t, :], b[:, 0:P], hc[:, IN], ALU.mult).then_inc(ik_out, 1)
                        if t == 0:
                            dve.wait_ge(fin_stored, h * 16)
                            dve.tensor_copy(state[1][:], b[:, P:P + DV]).then_inc(st_new, 1)
                        else:
                            dve.wait_ge(st_new, h * QB + t)
                            if t >= 2:
                                dve.wait_ge(o_mm, h * NB + t - 1)
                            dve.scalar_tensor_tensor(state[(t + 1) % 3][:], state[t % 3][:], hc[:, CDEC], b[:, P:P + DV], ALU.mult, ALU.add).then_inc(st_new, 1)
                        if t < QB - 1:
                            keys_a(9 + t)
                        if t == QB - 2:
                            cache_max(h * 2 + 1, 1)
                    cache_norm(h * 2)
                    cache_shift(h * 2 + 1, 1)
                    cache_out(h * 2)
                    dve.wait_ge(o_mm, h * NB + QB)
                    dve.tensor_tensor(kmask, krows[0:NS, QB, :].unsqueeze(1).to_broadcast([NS, NS, DK]),
                                      own[:].unsqueeze(2).to_broadcast([NS, NS, DK]), ALU.mult).then_inc(masks, 1)
                    dve.tensor_tensor(qmask[:], rqT[:, SEQ:T].unsqueeze(1).to_broadcast([P, NS, NS]), own_col[:], ALU.mult).then_inc(masks, 1)
                    dve.wait_ge(s_land, h * 16 + 16)
                    for b_ in range(NS):
                        dve.wait_ge(kv_s, h * NS + b_ + 1)
                        dve.scalar_tensor_tensor(st_s[:, b_, :], st_s[:, b_, :], hc[:, RDEC], bank[4 + b_ % 2][:, 0:DV], ALU.mult, ALU.add).then_inc(s_new, 1)
                    nxt(4)
                    keys_b(0)
                    for t in range(NB):
                        n = P if t < QB else NS
                        dve.wait_ge(o_out, h * NB + t + 1)
                        dve.wait_ge(mean, h * NB + t)
                        dve.bn_stats(stats[0:n, :], vrows[0:n, t, :]).then_inc(stat, 1)
                        wait_apart(dve, stat, h * NB + t + 1, g.mm_chunk)
                        dve.bn_aggr(mv[0:n, t, :], stats[0:n, :]).then_inc(mean, 1)
                        if t % 2:
                            keys_b(1 + t // 2)
                    dve.wait_ge(mean, (h + 1) * NB)
                    dve.tensor_scalar(mv[:, :, 1], mv[:, :, 1], EPS, None, ALU.add).then_inc(rstd_part, 1)
                    dve.wait_ge(rstd_part, h * 2 + 2)
                    dve.reciprocal(rstd[:], rstd[:]).then_inc(rstd_done, 1)
                    dve.wait_ge(rstd_done, h + 1)
                    for t in range(NB):
                        n = P if t < QB else NS
                        dve.tensor_scalar(vrows[0:n, t, :], vrows[0:n, t, :], mv[0:n, t, 0:1], rstd[0:n, t:t + 1], ALU.subtract, ALU.mult).then_inc(gnd, 1)
                    cache_sum(h * 2 + 1, 1)
                    keys_b(5)
                    for w in (4, 5):
                        if w == 5:
                            nxt(5)
                        for n in range(NCH):
                            k = 3 * (w - 4) + n
                            dve.wait_ge(g.bank_free[n], h * NJ + J0 + w + 2)
                            dve.wait_ge(rn_out, (h + 1) * 2 * NB)
                            dve.tensor_tensor(rvT[:, w - 4, chunk(n)], rvT[:, w - 4, chunk(n)], sg[k % 2][:], ALU.mult).then_inc(gated, 1)
                            keys_b(6 + k)
                    if not last:
                        for w in (6, 7):
                            nxt(w)
                            for n in range(NCH):
                                rotate(h * NJ + (J0 + w), h * 6 + 6, w - 6, n)
                                if w == 6 or n == 0:
                                    keys_b(12 + 3 * (w - 6) + n)
                                elif n == 1:
                                    cache_norm(h * 2 + 1)
                                    cache_max(h * 2 + 2, 0)
                        cache_shift(h * 2 + 2, 0)
                        cache_out(h * 2 + 1)
                    else:
                        cache_norm(h * 2 + 1)
                        cache_out(h * 2 + 1)
                heads(dve, body)



def tile_of(w, f, k0=0, kt=KD):
    return w.rearrange("a (k p) c -> p (a k) c", p=P)[:, k0:k0 + kt, ds(f * P, P)]


def finish(nc, g, a, c, o):
    JA, JB = 37, 37 + 2 * KD
    JO = JB + 2 * KD
    JF = JO + KD
    KB = FH // 2
    sections, f0, j0 = [], 0, JF
    for n in (8, 7, 7):
        sections.append((f0, n, j0, j0 + 2 * n))
        f0, j0 = f0 + n, j0 + 2 * n + KD
    JEND = j0
    assert f0 == FT
    with ExitStack() as ctx:
        sb = lambda n, s, d=F32: ctx.enter_context(nc.sbuf_tensor(n, s, d))
        sem = lambda n: ctx.enter_context(nc.semaphore(n))
        at = nc.sbuf_base
        acc = sb("acc", [P, KD, T])
        mh = nc.alloc_sbuf_tensor_at("merged_hi", [P, KD, T], F32R, offset=at)
        at = nc.sbuf_base
        gh, gl = sb("moving_hi", [P, KD, T], F32R), sb("moving_lo", [P, KD, T], F32R)
        z = nc.alloc_sbuf_tensor_at("z", [P, KD, T], F32, offset=at)
        y = [nc.alloc_sbuf_tensor_at(f"y{i}", [P, D], F32, offset=g.x_at + i * D * 4) for i in range(2)]
        wide = [nc.alloc_sbuf_tensor_at(f"ln2_wide{i}", [P, D], F32, offset=g.x_at + (2 + i) * D * 4) for i in range(2)]
        stage = [sb(f"stage{i}", [P, T + 2]) for i in range(2)]
        gate = [sb(f"gate{i}", [P, T]) for i in range(2)]
        tmp = [sb(f"chunk_tmp{i}", [P, TC]) for i in range(2)]
        ln_cols = sb("ln1_cols", [P, 2, KD])
        over = sb("one_over_width", [P, P])
        zsum, rstd, sq = stage[0], stage[1], gate
        up, act_in = stage
        fc = sb("conv_cols_tile", [P, 20])
        cr = gate[0][0:NS + 2, 0:P]
        bank = g.bank
        s_land, s_hi, s_lo, ln_land = [sem("stage_land0"), sem("stage_land1")], sem("stage_hi"), sem("stage_lo"), sem("ln_land")
        m_part, m_sum, m_hi, m_lo, over_set = sem("m_part"), sem("m_sum"), sem("m_hi"), sem("m_lo"), sem("over_set")
        z_part, z_done, z_summed, mean, centred, squared, var, root, inv = (
            sem(n) for n in ("z_part", "z_done", "z_summed", "mean", "centred", "squared", "var", "root", "inv_root"))
        normed, affine, h_hi, h_lo, h_scaled = (sem(n) for n in ("z_normed", "h_affine", "h_hi", "h_lo", "h_scaled"))
        fc_done, c1, conv, gelu, a_hi, a_lo = (sem(n) for n in ("fc_done", "conv_first", "conv_step", "gelu", "a_hi", "a_lo"))
        cr_t, cr_out, cr_stored = sem("conv_rows_turned"), sem("conv_rows_out"), sem("conv_rows_stored")
        y_t, stat, y_mean, y_var, y_root, y_inv, y_bias, y_norm, y_mul, y_add, wide_land = (
            sem(n) for n in ("y_turned", "y_stat", "y_mean", "y_var", "y_root", "y_inv", "y_bias", "y_norm", "y_mul", "y_add", "wide_land"))
        y_stored = [sem("y_stored0"), sem("y_stored1")]
        NT = QB + 1
        stats = [sb(f"ln2_stats{i}", [P, 2, 6]) for i in range(2)]
        mv2 = [sb(f"ln2_mean_var{i}", [P, 4]) for i in range(2)]
        old_stored = sem("old_conv_stored")

        with nc.Block() as block:
            @block.sync
            def _(sp):
                for w, name in enumerate(("ln1_w", "ln1_b")):
                    sp.dma_start(ln_cols[:, w, :], a[name].rearrange("a (k p) -> p (a k)", p=P), allow_slow_non_contiguous=True).then_inc(ln_land, 16)
                for n in range(KD + KB):
                    if n >= 2:
                        sp.wait_ge(s_lo, n - 1)
                    sp.dma_start(stage[n % 2][:, 0:T], g.g_dram[n] if n < KD else g.fo_dram[n - KD]).then_inc(s_land[n % 2], 16)
                sp.dma_start(o[11][:, :, 0, :], a["state_conv"][:, :, 1, :]).then_inc(old_stored, 16)
                with sp.Fori(0, FT) as f:
                    sp.wait_ge(cr_out, f + 1)
                    sp.dma_start(o[10].rearrange("a b w f -> (a b w) f")[:, ds(f * P, P)], cr[0:2]).then_inc(cr_stored, 16)
                    sp.dma_start(o[11].rearrange("a b w f -> (a b) w f")[:, 1, ds(f * P, P)], cr[2:2 + NS]).then_inc(cr_stored, 16)
                sp.wait_ge(g.mm_chunk, NCH * (RING + sections[-1][3]))
                for w, name in enumerate(("ln2_w", "ln2_b")):
                    sp.dma_start(wide[w][:], a[name].to_broadcast([P, D])).then_inc(wide_land, 16)
                for t in range(NT):
                    sp.wait_ge(y_add, t + 1)
                    if t < QB:
                        sp.dma_start(o[0][0, t * P:(t + 1) * P, :], y[t % 2][:]).then_inc(y_stored[t % 2], 16)
                    else:
                        sp.dma_start(o[1].rearrange("b t d -> (b t) d"), y[t % 2][0:NS, :]).then_inc(y_stored[t % 2], 16)
                sp.wait_ge(y_stored[0], 16 * (NT - NT // 2))
                sp.wait_ge(y_stored[1], 16 * (NT // 2))
                sp.wait_ge(cr_stored, 32 * FT)
                sp.wait_ge(old_stored, 16)

            @block.gpsimd
            def _(pool):
                pool.memset(over[:], 1.0 / D).then_inc(over_set, 1)
                assert C_GA + D == C_GB

                def branch(it, base, col, w, kt, more=True):
                    load_weight(g, pool, job(base, 1, 1), tile_of(w, it * 2, 0, kt), kt)
                    load_weight(g, pool, job(base, 1, 2), w_in_tile(a, it * (2 * P) + (col + P)))
                    load_weight(g, pool, job(base, 1, 3), tile_of(w, it * 2 + 1, 0, kt), kt)
                    if more:
                        load_weight(g, pool, job(base, 1, 4), w_in_tile(a, it * (2 * P) + (col + 2 * P)))
                with pool.Fori(0, KD // 2) as it:
                    branch(it, it * 4 + JA, C_GA, a["w_pa"], KD)
                with pool.Fori(0, KD // 2 - 1) as it:
                    branch(it, it * 4 + JB, C_GB, a["w_pb"], KB)
                branch(KD // 2 - 1, (KD // 2 - 1) * 4 + JB, C_GB, a["w_pb"], KB, more=False)
                with pool.Fori(0, KD // 2) as it:
                    for u in range(2):
                        load_weight(g, pool, job(it * 2 + JO, JO % 2, u), tile_of(a["w_o"], it * 2 + u))
                def up_and_gate(i, f0, ju):
                    for u, w in enumerate((a["w_up"], a["w_gate"])):
                        load_weight(g, pool, job(i * 2 + ju, ju % 2, u), tile_of(w, i + f0))
                for s, (f0, n, ju, jd) in enumerate(sections):
                    if s == 0:
                        up_and_gate(0, f0, ju)
                        for k in range(NCH):
                            pool.wait_ge(affine, (k + 1) * KD)
                            pool.tensor_scalar(acc[:, :, chunk(k)], z[:, :, chunk(k)], ALPHA, None, ALU.mult).then_inc(h_scaled, 1)
                    with pool.Fori(1 if s == 0 else 0, n) as i:
                        up_and_gate(i, f0, ju)
                    with pool.Fori(0, KD // 2) as it:
                        for u in range(2):
                            load_weight(g, pool, job(it * 2 + jd, jd % 2, u), tile_of(a["w_down"], it * 2 + u, f0, n), n)
                for t in range(NT):
                    n = P if t < QB else NS
                    pool.wait_ge(y_mul, t + 1)
                    pool.tensor_tensor(y[t % 2][0:n, :], y[t % 2][0:n, :], wide[1][0:n, :], ALU.add).then_inc(y_add, 1)

            @block.tensor
            def _(pe):
                with pe.Fori(0, KD // 2) as it:
                    for u in range(2):
                        product(g, pe, job(it * 4 + JA, 1, 2 * u), g.xh, g.xl)
                        pe.wait_ge(s_lo, KD)
                        product(g, pe, job(it * 4 + JA, 1, 2 * u + 1), gh, gl)
                with pe.Fori(0, KD // 2) as it:
                    for u in range(2):
                        product(g, pe, job(it * 4 + JB, 1, 2 * u), g.xh, g.xl)
                        pe.wait_ge(s_lo, KD + KB)
                        product(g, pe, job(it * 4 + JB, 1, 2 * u + 1), gh[:, 0:KB, :], gh[:, KB:2 * KB, :], KB)
                pe.wait_ge(m_lo, NCH * KD)
                pe.wait_ge(over_set, 1)

                def mean_of(n):
                    pe.wait_ge(z_summed, NCH * (KD - 1) + n + 1)
                    pe.matmul(bank[3 + n][:, 0:TC], over[:], zsum[:, chunk(n)], start=True, stop=True).then_inc(mean, 1)

                def var_of(n):
                    if n == 2:
                        pe.wait_ge(root, 1)
                    for k in range(KD):
                        pe.wait_ge(squared, n * KD + k + 1)
                        pe.matmul(bank[6 + n % 2][:, 0:TC], over[:], sq[k % 2][:, 0:TC], start=(k == 0), stop=(k == KD - 1)).then_inc(var, 1)
                with pe.Fori(0, KD // 2 - 1) as it:
                    for u in range(2):
                        product(g, pe, job(it * 2 + JO, JO % 2, u), mh, gl)
                product(g, pe, job(JO + KD - 2, JO % 2, 0), mh, gl)
                product(g, pe, job(JO + KD - 2, JO % 2, 1), mh, gl, after=lambda n: mean_of(n - 1) if n else None)
                var_of(0)
                mean_of(2)
                var_of(1)
                var_of(2)
                for f0, n, ju, jd in sections:
                    with pe.Fori(0, n) as i:
                        product(g, pe, job(i * 2 + ju, ju % 2, 0), g.xh, g.xl, before=lambda k: pe.wait_ge(h_lo, k + 1))
                        product(g, pe, job(i * 2 + ju, ju % 2, 1), g.xh, g.xl)
                        pe.wait_ge(cr_out, i + f0)
                        pe.transpose(bank[3][0:NS + 2, 0:P], up[:, SEQ:SEQ + NS + 2], g.ident[:]).then_inc(cr_t, 1)
                    with pe.Fori(0, KD // 2) as it:
                        for u in range(2):
                            product(g, pe, job(it * 2 + jd, jd % 2, u), gh, gl, n, before=lambda k: pe.wait_ge(a_lo, f0 + n))
                for k in range(NCH):
                    pe.wait_ge(g.bank_free[k], JEND + 1)
                for t in range(NT):
                    n = P if t < QB else NS
                    if t >= 2:
                        pe.wait_ge(y_norm, t - 1)
                    for k in range(KD):
                        mm = pe.transpose(g.pair[t % 2][0:n, k * P:(k + 1) * P], acc[:, k, t * P:t * P + n], g.ident[:])
                    mm.then_inc(y_t, 1)

            @block.scalar
            def _(act):
                def stage_hi(n):
                    dst = gh[:, n, :]
                    act.wait_ge(s_land[n % 2], 16 * (n // 2 + 1))
                    act.activation(dst, stage[n % 2][:, 0:T], ACT.Copy).then_inc(s_hi, 1)

                def gates(it, base, local, slot):
                    for n in range(NCH):
                        chunk_ready(g, act, base + local, n)
                        act.activation(gate[slot][:, chunk(n)], bank[n][:, 0:TC], ACT.Sigmoid).then_inc(g.bank_free[n], 1)
                for n in range(KD):
                    stage_hi(n)
                with act.Fori(0, KD // 2) as it:
                    for u in range(2):
                        split_hi(g, act, job(it * 4 + JA, 1, 2 * u + 1))
                        gates(it, it * 4 + JA, 2 * u, u)
                        split_hi(g, act, job(it * 4 + JA, 1, 2 * u + 2))
                act.wait_ge(g.mm_chunk, NCH * (RING + JB))
                for n in range(KD, KD + KB):
                    act.wait_ge(s_land[n % 2], 16 * (n // 2 + 1))
                    act.activation(gh[:, n - KD, :], stage[n % 2][:, 0:T], ACT.Copy).then_inc(s_hi, 1)
                with act.Fori(0, KD // 2) as it:
                    for u in range(2):
                        split_hi(g, act, job(it * 4 + JB, 1, 2 * u + 1), KB)
                        gates(it, it * 4 + JB, 2 * u, u)
                        split_hi(g, act, job(it * 4 + JB, 1, 2 * u + 2))
                with act.Fori(0, KD // 2) as it:
                    for u in range(2):
                        split_hi(g, act, job(it * 2 + JO, JO % 2, u + 1))
                for n in range(NCH):
                    act.wait_ge(centred, n + 1)
                    for k in range(KD):
                        i = n * KD + k
                        if i >= 2:
                            act.wait_ge(var, i - 1)
                        act.activation(sq[k % 2][:, 0:TC], z[:, k, chunk(n)], ACT.Square).then_inc(squared, 1)
                    act.wait_ge(var, (n + 1) * KD)
                    act.activation(rstd[:, chunk(n)], bank[6 + n % 2][:, 0:TC], ACT.Sqrt, bias=g.eps[:]).then_inc(root, 1)
                    act.wait_ge(affine, (n + 1) * KD)
                    act.activation(g.xh[:, :, chunk(n)], z[:, :, chunk(n)], ACT.Copy).then_inc(h_hi, 1)
                act.wait_ge(h_lo, NCH)
                act.wait_ge(z_part, 2)
                for s, (f0, n, ju, jd) in enumerate(sections):
                    with act.Fori(0, n) as i:
                        f = i + f0
                        split_hi(g, act, job(i * 2 + ju, ju % 2, 1))
                        act.wait_ge(conv, f * 5)
                        act.wait_ge(cr_t, f)
                        act.activation(fc[:], g.conv_cols[:, ds(f, 1), :].rearrange("p a c -> p (a c)"), ACT.Copy).then_inc(fc_done, 1)
                        for k in range(NCH):
                            chunk_ready(g, act, i * 2 + ju, k)
                            act.activation(up[:, 2 + k * TC:2 + (k + 1) * TC], bank[k][:, 0:TC], ACT.Copy).then_inc(g.bank_free[k], 1)
                        for k in range(NCH):
                            act.wait_ge(g.bank_free[k], i * 2 + ju + 2)
                        act.wait_ge(fc_done, f + 1)
                        act.wait_ge(a_lo, f)
                        act.activation(act_in[:, 0:SEQ], up[:, 0:SEQ], ACT.Identity, scale=fc[:, 16:17], bias=fc[:, 19:20]).then_inc(c1, 1)
                        split_hi(g, act, job(i * 2 + ju, ju % 2, 2))
                        act.wait_ge(conv, f * 5 + 5)
                        act.activation(act_in[:, 0:T], act_in[:, 0:T], ACT.Gelu_apprx_tanh).then_inc(gelu, 1)
                        for k in range(NCH):
                            act.wait_ge(g.bank_free[k], i * 2 + ju + 3)
                        if s == 0:
                            act.wait_ge(h_scaled, NCH)
                        act.activation(gh[:, ds(i, 1), :].rearrange("p a t -> p (a t)"), act_in[:, 0:T], ACT.Copy).then_inc(a_hi, 1)
                        act.wait_ge(cr_t, f + 1)
                        act.wait_ge(cr_stored, f * 32)
                        act.activation(cr, bank[3][0:NS + 2, 0:P], ACT.Copy).then_inc(cr_out, 1)

                    def down(it, last):
                        for u in range(2):
                            if not (last and u):
                                split_hi(g, act, job(it * 2 + jd, jd % 2, u + 1))
                    with act.Fori(0, KD // 2 - 1) as it:
                        down(it, False)
                    down(KD // 2 - 1, s == len(sections) - 1)
                for t in range(NT):
                    n = P if t < QB else NS
                    act.wait_ge(y_var, t + 1)
                    act.activation(mv2[t % 2][0:n, 2:3], mv2[t % 2][0:n, 1:2], ACT.Sqrt, bias=g.eps[0:n]).then_inc(y_root, 1)
                    act.wait_ge(y_bias, t + 1)
                    if t >= 2:
                        act.wait_ge(y_stored[t % 2], 16 * (t // 2))
                    act.activation(y[t % 2][0:n, :], g.pair[t % 2][0:n, :], ACT.Identity, scale=mv2[t % 2][0:n, 2:3], bias=mv2[t % 2][0:n, 3:4]).then_inc(y_norm, 1)

            @block.vector
            def _(dve):
                def stage_lo(n, src, dst):
                    dve.wait_ge(s_hi, n + 1)
                    dve.tensor_tensor(dst, stage[n % 2][:, 0:T], src.bitcast(F32), ALU.subtract).then_inc(s_lo, 1)
                for n in range(KD):
                    stage_lo(n, gh[:, n, :], gl[:, n, :])
                with dve.Fori(0, KD // 2) as it:
                    for u in range(2):
                        split_lo(g, dve, job(it * 4 + JA, 1, 2 * u + 1))
                        split_lo(g, dve, job(it * 4 + JA, 1, 2 * u + 2))
                        for n in range(NCH):
                            chunk_ready(g, dve, it * 4 + JA + (2 * u + 1), n)
                            dve.tensor_tensor(acc[:, ds(it * 2 + u, 1), chunk(n)].rearrange("p a t -> p (a t)"), bank[n][:, 0:TC], gate[u][:, chunk(n)], ALU.mult).then_inc(g.bank_free[n], 1)
                for n in range(KD, KD + KB):
                    stage_lo(n, gh[:, n - KD, :], gh[:, n - KD + KB, :])
                with dve.Fori(0, KD // 2) as it:
                    for u in range(2):
                        split_lo(g, dve, job(it * 4 + JB, 1, 2 * u + 1), KB)
                        split_lo(g, dve, job(it * 4 + JB, 1, 2 * u + 2))
                        for n in range(NCH):
                            i = (it * 2 + u) * NCH + n
                            j = it * 4 + JB + (2 * u + 1)
                            t = tmp[0]
                            cols = lambda x: x[:, ds(it * 2 + u, 1), chunk(n)].rearrange("p a t -> p (a t)")
                            chunk_ready(g, dve, j, n)
                            dve.wait_ge(m_lo, i)
                            dve.tensor_tensor(t[:], bank[n][:, 0:TC], gate[u][:, chunk(n)], ALU.mult).then_inc(g.bank_free[n], 1)
                            dve.wait_ge(g.bank_free[n], j + 2)
                            dve.tensor_tensor(t[:], t[:], cols(acc), ALU.add).then_inc(m_sum, 1)
                            dve.wait_ge(m_sum, i + 1)
                            dve.tensor_scalar(cols(mh), t[:], 1.0, None, ALU.mult).then_inc(m_hi, 1)
                            dve.wait_ge(m_hi, i + 1)
                            dve.tensor_tensor(cols(gl), t[:], cols(mh).bitcast(F32), ALU.subtract).then_inc(m_lo, 1)
                dve.wait_ge(s_lo, KD + KB)
                dve.memset(zsum[:], 0.0).then_inc(z_part, 1)
                dve.wait_ge(z_part, 1)

                def projected(it, u):
                    split_lo(g, dve, job(it * 2 + JO, JO % 2, u + 1))
                    for n in range(NCH):
                        i = (it * 2 + u) * NCH + n
                        j = it * 2 + JO + u
                        cols = lambda x: x[:, ds(it * 2 + u, 1), chunk(n)].rearrange("p a t -> p (a t)")
                        chunk_ready(g, dve, j, n)
                        dve.wait_ge(z_done, i)
                        dve.scalar_tensor_tensor(tmp[0][:], cols(g.xh).bitcast(F32), ALPHA, bank[n][:, 0:TC], ALU.mult, ALU.add).then_inc(g.bank_free[n], 1)
                        dve.wait_ge(g.bank_free[n], j + 2)
                        dve.scalar_tensor_tensor(cols(z), cols(g.xl).bitcast(F32), ALPHA, tmp[0][:], ALU.mult, ALU.add).then_inc(z_done, 1)
                        dve.wait_ge(z_done, i + 1)
                        dve.wait_ge(z_summed, i)
                        dve.tensor_tensor(zsum[:, chunk(n)], zsum[:, chunk(n)], cols(z), ALU.add).then_inc(z_summed, 1)
                with dve.Fori(0, KD // 2) as it:
                    for u in range(2):
                        projected(it, u)
                dve.wait_ge(ln_land, 32)

                def wide_chunk(x):
                    return x.unsqueeze(1).to_broadcast([P, KD, TC])

                def centre(n):
                    dve.wait_ge(mean, n + 1)
                    dve.tensor_tensor(z[:, :, chunk(n)], z[:, :, chunk(n)], wide_chunk(bank[3 + n][:, 0:TC]), ALU.subtract).then_inc(centred, 1)
                centre(0)
                for n in range(NCH):
                    if n + 1 < NCH:
                        centre(n + 1)
                    dve.wait_ge(root, n + 1)
                    dve.reciprocal(rstd[:, chunk(n)], rstd[:, chunk(n)]).then_inc(inv, 1)
                    dve.wait_ge(inv, n + 1)
                    dve.tensor_tensor(z[:, :, chunk(n)], z[:, :, chunk(n)], wide_chunk(rstd[:, chunk(n)]), ALU.mult).then_inc(normed, 1)
                    dve.wait_ge(normed, n + 1)
                    for k in range(KD):
                        dve.tensor_scalar(z[:, k, chunk(n)], z[:, k, chunk(n)], ln_cols[:, 0, k:k + 1], ln_cols[:, 1, k:k + 1], ALU.mult, ALU.add).then_inc(affine, 1)
                    dve.wait_ge(h_hi, n + 1)
                    dve.tensor_tensor(g.xl[:, :, chunk(n)], z[:, :, chunk(n)], g.xh[:, :, chunk(n)].bitcast(F32), ALU.subtract).then_inc(h_lo, 1)
                dve.memset(up[:, 0:2], 0.0).then_inc(z_part, 1)
                for s, (f0, n, ju, jd) in enumerate(sections):
                    with dve.Fori(0, n) as i:
                        f = i + f0
                        split_lo(g, dve, job(i * 2 + ju, ju % 2, 1))
                        dve.wait_ge(a_lo, f)
                        old = fc[:, 0:2 * NS].rearrange("p (b w) -> p w b", w=2)
                        new = act_in[:, SEQ:T]
                        dve.wait_ge(a_hi, f)
                        dve.wait_ge(fc_done, f + 1)
                        dve.tensor_scalar(new, old[:, 0, :], fc[:, 16:17], fc[:, 19:20], ALU.mult, ALU.add).then_inc(conv, 1)
                        dve.wait_ge(c1, f + 1)
                        dve.scalar_tensor_tensor(act_in[:, 0:SEQ], up[:, 1:1 + SEQ], fc[:, 17:18], act_in[:, 0:SEQ], ALU.mult, ALU.add).then_inc(conv, 1)
                        dve.wait_ge(conv, f * 5 + 1)
                        dve.scalar_tensor_tensor(new, old[:, 1, :], fc[:, 17:18], new, ALU.mult, ALU.add).then_inc(conv, 1)
                        dve.wait_ge(conv, f * 5 + 3)
                        dve.scalar_tensor_tensor(act_in[:, 0:SEQ], up[:, 2:2 + SEQ], fc[:, 18:19], act_in[:, 0:SEQ], ALU.mult, ALU.add).then_inc(conv, 1)
                        dve.scalar_tensor_tensor(new, up[:, 2 + SEQ:2 + T], fc[:, 18:19], new, ALU.mult, ALU.add).then_inc(conv, 1)
                        split_lo(g, dve, job(i * 2 + ju, ju % 2, 2))
                        dve.wait_ge(gelu, f + 1)
                        for k in range(NCH):
                            chunk_ready(g, dve, i * 2 + ju + 1, k)
                            dve.tensor_tensor(act_in[:, chunk(k)], act_in[:, chunk(k)], bank[k][:, 0:TC], ALU.mult).then_inc(g.bank_free[k], 1)
                        dve.wait_ge(a_hi, f + 1)
                        dve.tensor_tensor(gl[:, ds(i, 1), :].rearrange("p a t -> p (a t)"), act_in[:, 0:T],
                                          gh[:, ds(i, 1), :].rearrange("p a t -> p (a t)").bitcast(F32), ALU.subtract).then_inc(a_lo, 1)

                    def down(it, last):
                        for u in range(2):
                            if not (last and u):
                                split_lo(g, dve, job(it * 2 + jd, jd % 2, u + 1))
                            for k in range(NCH):
                                cols = acc[:, ds(it * 2 + u, 1), chunk(k)].rearrange("p a t -> p (a t)")
                                chunk_ready(g, dve, it * 2 + jd + u, k)
                                dve.tensor_tensor(cols, cols, bank[k][:, 0:TC], ALU.add).then_inc(g.bank_free[k], 1)
                    if s == 0:
                        dve.wait_ge(h_scaled, NCH)
                    with dve.Fori(0, KD // 2 - 1) as it:
                        down(it, False)
                    down(KD // 2 - 1, s == len(sections) - 1)
                dve.wait_ge(wide_land, 32)
                for t in range(NT + 1):
                    if t < NT:
                        n = P if t < QB else NS
                        v, st = mv2[t % 2], stats[t % 2]
                        dve.wait_ge(y_t, t + 1)
                        if t >= 2:
                            dve.wait_ge(y_norm, t - 1)
                        for half in range(2):
                            dve.bn_stats(st[0:n, half, :], g.pair[t % 2][0:n, half * 512:(half + 1) * 512]).then_inc(stat, 1)
                        dve.wait_ge(stat, 2 * t + 2)
                        dve.bn_aggr(v[0:n, 0:2], st[0:n].rearrange("p a s -> p (a s)")).then_inc(y_var, 1)
                        dve.wait_ge(y_root, t + 1)
                        dve.reciprocal(v[0:n, 2:3], v[0:n, 2:3]).then_inc(y_inv, 1)
                        dve.wait_ge(y_inv, t + 1)
                        dve.scalar_tensor_tensor(v[0:n, 3:4], v[0:n, 0:1], -1.0, v[0:n, 2:3], ALU.mult, ALU.mult).then_inc(y_bias, 1)
                    if t >= 1:
                        n = P if t - 1 < QB else NS
                        dve.wait_ge(y_norm, t)
                        dve.tensor_tensor(y[(t - 1) % 2][0:n, :], y[(t - 1) % 2][0:n, :], wide[0][0:n, :], ALU.mult).then_inc(y_mul, 1)


def w_in_tile(a, col, m=P):
    w = a["w_in"].rearrange("a (k p) c -> p (a k) c", p=P)
    return w[:, :, ds(col, m)]


def build_program(nc, a, c, o, debug=None):
    with ExitStack() as ctx:
        sb = lambda n, s, d=F32: ctx.enter_context(nc.sbuf_tensor(n, s, d))
        sem = lambda n: ctx.enter_context(nc.semaphore(n))
        g = Shared()
        ps = lambda n, w: ctx.enter_context(nc.psum_tensor(n, [P, w], F32))
        g.pair = [ps("banks34", 1024), ps("banks56", 1024)]
        g.bank = ([ps(f"bank{n}", 512) for n in range(NCH)]
                  + [g.pair[i // 2][:, 512 * (i % 2):512 * (i % 2) + 512] for i in range(4)] + [ps("bank7", 512)])
        g.ident = sb("ident", [P, P])
        g.x_at = nc.sbuf_base
        g.xh, g.xl = sb("x_hi", [P, KD, T], F32R), sb("x_lo", [P, KD, T], F32R)
        g.conv_cols, g.eps = sb("conv_cols", [P, FT, 20]), sb("eps", [P, 1])
        g.w_raw = [sb(f"w_raw{i}", [P, KD, P]) for i in range(RING)]
        g.w_hi = [sb(f"w_hi{i}", [P, KD, P], F32R) for i in range(RING)]
        g.w_lo = [sb(f"w_lo{i}", [P, KD, P], F32R) for i in range(RING)]
        g.w_land = [sem(f"w_land{i}") for i in range(RING)]
        g.w_rounded, g.w_split, g.mm_chunk = sem("w_rounded"), sem("w_split"), sem("mm_chunk")
        g.bank_free = [sem(f"bank_free{n}") for n in range(NCH)]
        attention_part = ExitStack()
        g.qnew, g.knew, g.vnew = (attention_part.enter_context(nc.sbuf_tensor(n, [NS, FH * HD], F32)) for n in ("q_new", "k_new", "v_new"))
        g.lfnew = attention_part.enter_context(nc.sbuf_tensor("logf_new", [NS, FH], F32))
        g.fo_dram = nc.dram_tensor("fox_t_scratch", [FH // 2, P, T], F32).ap()
        g.q_dram = nc.dram_tensor("q_new_scratch", [NS, FH * HD], F32).ap()
        g.g_dram = nc.dram_tensor("gated_t_scratch", [KD, P, T], F32).ap()
        g.dec_bias = attention_part.enter_context(nc.sbuf_tensor("dec_bias", [P, NS, NPG + 1, FH], F32))
        prepare(nc, g, a, c)
        fox(nc, g, a, c, o)
        retain(nc, g, a, c, o)
        if debug:
            debug(nc, g)
        attention_part.close()
        finish(nc, g, a, c, o)


_INS = ["x_prompt", "x_sample", "cache_k", "cache_v", "cache_logf", "state_ret", "state_conv", "page_table",
        "w_in", "b_f", "ret_gn_w", "ret_gn_b", "w_pa", "w_pb", "w_o", "ln1_w", "ln1_b",
        "w_up", "w_gate", "conv_w", "conv_b", "w_down", "ln2_w", "ln2_b"]
_OUTS = [(1, SEQ, D), (NS, 1, D), (1, 1, SEQ, FH, HD), (1, 1, SEQ, FH, HD), (1, 1, SEQ, FH),
         (1, NS, 1, FH, HD), (1, NS, 1, FH, HD), (1, NS, 1, FH),
         (1, 1, RH, DK, DV), (1, NS, RH, DK, DV), (1, 1, 2, DFF), (1, NS, 2, DFF)]


def kernel(**inputs):
    import numpy as _np
    import concourse.bacc as _bacc
    from concourse import mybir as _mybir
    from concourse.bass_utils import run_bass_kernel_spmd as _run

    nc = _bacc.Bacc("TRN2", target_bir_lowering=False, num_devices=1)
    arrays, args, consts = {}, {}, {}
    for name in _INS:
        x = _np.ascontiguousarray(inputs[name])
        arrays[f"in_{name}_dram"] = x
        args[name] = nc.dram_tensor(f"in_{name}_dram", x.shape, _mybir.dt.from_np(x.dtype), kind="ExternalInput").ap()
    for name, x in constants().items():
        arrays[f"const_{name}_dram"] = x
        consts[name] = nc.dram_tensor(f"const_{name}_dram", x.shape, _mybir.dt.from_np(x.dtype), kind="ExternalInput").ap()
    outs = [nc.dram_tensor(f"out_{i}_dram", shape, _mybir.dt.float32, kind="ExternalOutput").ap() for i, shape in enumerate(_OUTS)]
    build_program(nc, args, consts, outs)
    r = _run(nc, [arrays], core_ids=[0])
    return tuple(r.results[0][f"out_{i}_dram"] for i in range(len(_OUTS)))
```

```python
from contextlib import ExitStack

import numpy as np

import concourse.bass as bass
from concourse import mybir

F32 = mybir.dt.float32
F32R = mybir.dt.float32r
BF16 = mybir.dt.bfloat16
I32 = mybir.dt.int32
ACT = mybir.ActivationFunctionType
ALU = mybir.AluOpType
AX = mybir.AxisListType

P = 128
D = 1024
SEQ = 1024
NS = 8
T = SEQ + NS
KD = D // P
NCH = 3
TC = T // NCH
RH, DK, DV = 4, 128, 256
FH, HD = 8, 64
NPG, PG = 32, 128
POOL = 320
DFF = 2816
FT = DFF // P
ALPHA = 2.0 ** 0.25
EPS = 1e-5
BIG = -1.0e30
QB = SEQ // P
C_RQ, C_RK, C_RV, C_RG = 0, 512, 1024, 2048
C_FQ, C_FK, C_FV, C_FF, C_GA, C_GB = 3072, 3584, 4096, 4608, 4616, 5640
RING = 2

ds = bass.ds


def chunk(n):
    return slice(n * TC, (n + 1) * TC)


class Shared:
    pass


class Chain:

    def __init__(self, eng, sem, base=0):
        self.eng, self.sem, self.base, self.n = eng, sem, base, 0

    def link(self, ins):
        self.n += 1
        ins.then_inc(self.sem, 1)
        self.eng.wait_ge(self.sem, self.base + self.n)


def wait_apart(eng, sem, value, held):
    value = value if isinstance(value, int) else eng.to_reg(value)
    eng.wait_ge(held, 1)
    eng.wait_ge(sem, value)



def job(base, parity, local):
    return base + local, (parity + local) % RING


def load_weight(g, eng, jb, src, kt=KD, m=P):
    j, slot = jb
    wait_apart(eng, g.w_split, j + 1, g.mm_chunk)
    eng.dma_start(g.w_raw[slot][:, 0:kt, 0:m], src).then_inc(g.w_land[slot], 16)


def split_hi(g, act, jb, kt=KD, m=P):
    j, slot = jb
    act.wait_ge(g.w_land[slot], (j - slot) * (16 // RING) + 16)
    act.wait_ge(g.mm_chunk, NCH * (j + 1))
    act.activation(g.w_hi[slot][:, 0:kt, 0:m], g.w_raw[slot][:, 0:kt, 0:m], ACT.Copy).then_inc(g.w_rounded, 1)


def split_lo(g, dve, jb, kt=KD, m=P):
    j, slot = jb
    dve.wait_ge(g.w_rounded, j + 1)
    dve.tensor_tensor(g.w_lo[slot][:, 0:kt, 0:m], g.w_raw[slot][:, 0:kt, 0:m],
                      g.w_hi[slot][:, 0:kt, 0:m].bitcast(F32), ALU.subtract).then_inc(g.w_split, 1)


def product(g, pe, jb, xh, xl, kt=KD, m=P, before=None, ready=None, after=None):
    j, slot = jb
    pe.wait_ge(g.w_split, RING + j + 1)
    for n in range(NCH):
        pe.wait_ge(g.bank_free[n], j + 1)
        if before:
            before(n)
        for k in range(kt):
            if ready and n == 0:
                ready(k)
            for i, (w, x) in enumerate(((g.w_hi, xh), (g.w_hi, xl), (g.w_lo, xh))):
                mm = pe.matmul(g.bank[n][0:m, 0:TC], w[slot][:, k, 0:m], x[:, k, chunk(n)],
                               start=(k == 0 and i == 0), stop=(k == kt - 1 and i == 2))
        mm.then_inc(g.mm_chunk, 1)
        if after:
            after(n)


def chunk_ready(g, eng, j, n):
    eng.wait_ge(g.mm_chunk, NCH * (RING + j) + n + 1)



def constants(bf16=None):
    bf16 = bf16 or mybir.dt.np(BF16)
    f = np.float32
    c = {}
    i = np.arange(P)
    c["ident"] = np.eye(P, dtype=f)
    c["later_row"] = (i[:, None] > i[None, :]).astype(f)
    b, pg = i // NPG, i % NPG
    c["later_page"] = ((b[:, None] == b[None, :]) & (pg[:, None] > pg[None, :])).astype(f)
    pos = np.concatenate([np.arange(SEQ), np.full(NS, NPG * PG)]).astype(f)
    half = DK // 2
    freq = np.power(f(10000.0), -(np.arange(half, dtype=f) / f(half))).astype(f)
    ang = (freq[:, None] * pos[None, :]).astype(f)
    c["cos"] = np.concatenate([np.cos(ang)] * 2).astype(f)
    c["sin"] = np.concatenate([np.sin(ang), -np.sin(ang)]).astype(f)
    lg = np.log(1.0 - 2.0 ** (-5.0 - np.arange(RH, dtype=np.float64)))
    rel = i[None, :] - i[:, None]
    intra = np.where(rel[:, None, :] >= 0, np.exp(lg[None, :, None] * np.maximum(rel, 0)[:, None, :]), 0.0)
    hc = np.zeros((RH, P, 2 * P + 4))
    hc[:, :, 0:P] = intra.transpose(1, 0, 2)
    hc[:, :, P:2 * P] = np.exp(lg[:, None] * (i + 1.0)[None, :])[:, None, :]
    hc[:, :, 2 * P] = np.exp(lg[:, None] * (P - 1.0 - i)[None, :])
    hc[:, :, 2 * P + 1] = np.exp(lg * P)[:, None]
    hc[:, :, 2 * P + 2] = np.exp(lg)[:, None]
    c["head_const"] = hc.astype(f)
    c["sel_head"] = (i[:, None] % 32 == np.arange(FH)[None, :]).astype(f)
    c["causal"] = np.where(i[None, :] <= i[:, None], 0.0, BIG).astype(bf16)
    c["ident_b"] = np.eye(P, dtype=f).astype(bf16)
    own = (i[:, None] == np.arange(NS)[None, :]).astype(f)
    c["own8"] = np.repeat(own[:, :, None], FH, 2).astype(f)
    c["other8"] = np.repeat(((1 - own) * BIG)[:, :, None], FH, 2).astype(f)
    c["own_col"] = np.ascontiguousarray(np.broadcast_to(np.eye(NS)[None], (P, NS, NS))).astype(f)
    return c



def prepare(nc, g, a, c, o):
    with ExitStack() as ctx:
        sb = lambda n, s, d=F32: ctx.enter_context(nc.sbuf_tensor(n, s, d))
        sem = lambda n: ctx.enter_context(nc.semaphore(n))
        STAGES = 4
        stage = [sb(f"x_stage{i}", [P, D]) for i in range(STAGES)]
        ids = sb("page_ids", [P, 2], I32)
        rows = [sb(f"logf_rows{i}", [P, PG * FH]) for i in range(2)]
        row_t = sb("logf_rows_t", [P, 2, FH, P])
        total = [sb(f"page_total{i}", [P, FH]) for i in range(2)]
        total_b = [sb(f"page_total_wide{i}", [P, FH, P]) for i in range(2)]
        later_row = sb("later_row", [P, P])
        later_page = sb("later_page", [P, P])
        z, ez, zn = sb("ff_z", [FH, T]), sb("ff_e", [FH, T]), sb("ff_neg", [FH, T])
        bf_col = sb("b_f_col", [FH, 1])
        x_land = [sem(f"x_land{i}") for i in range(STAGES)]
        xs_land, const_land, ids_land = sem("xs_land"), sem("const_land"), sem("ids_land")
        rows_land = [sem(f"rows_land{i}") for i in range(2)]
        x_turned, x_rounded, x_split = sem("x_turned"), sem("x_rounded"), sem("x_split")
        total_done, wide_done, rows_turned, rows_copied, bias_mm = (
            sem(n) for n in ("total_done", "wide_done", "rows_turned", "rows_copied", "bias_mm"))
        bias_land = sem("bias_land")
        conv_rows = sb("conv_rows", [20, DFF])
        conv_land, conv_turned = sem("conv_land"), sem("conv_turned")
        ff_chain, ff_act = sem("ff_chain"), sem("ff_act")
        bank = g.bank
        sums = [*bank[0:NCH], bank[4]]

        x_in = a["x_prompt"].rearrange("a (t p) d -> (a t) p d", p=P)
        with nc.Block() as block:
            @block.sync
            def _(sp):
                sp.dma_start(g.ident[:], c["ident"]).then_inc(const_land, 16)
                with sp.Fori(0, QB // STAGES) as it:
                    for u in range(STAGES):
                        sp.wait_ge(x_turned, it * (2 * STAGES) + 2 * u + 2)
                        sp.dma_start(stage[u][:], x_in[ds(it * STAGES + u, 1)].rearrange("a p d -> (a p) d")).then_inc(x_land[u], 16)
                sp.wait_ge(x_turned, 2 * QB + 2)
                sp.dma_start(stage[0][0:NS, :], a["x_sample"].rearrange("b t d -> (b t) d")).then_inc(xs_land, 16)
                sp.dma_start(bf_col[:], a["b_f"].rearrange("d h -> h d"), allow_slow_non_contiguous=True).then_inc(const_land, 16)
                sp.dma_start(later_row[:], c["later_row"]).then_inc(const_land, 16)
                sp.dma_start(later_page[:], c["later_page"]).then_inc(const_land, 16)
                sp.dma_start(conv_rows[0:16, :], a["state_conv"].rearrange("a b w f -> (a b w) f")).then_inc(conv_land, 16)
                sp.dma_start(conv_rows[16:19, :], a["conv_w"].rearrange("a w f -> (a w) f")).then_inc(conv_land, 16)
                sp.dma_start(conv_rows[19:20, :], a["conv_b"]).then_inc(conv_land, 16)
                sp.dma_start(g.dec_bias[:, :, NPG, :], c["other8"]).then_inc(bias_land, 16)
                sp.wait_ge(bias_land, 16)

            @block.tensor
            def _(pe):
                pe.nop().then_inc(x_turned, 2 * STAGES)
                pe.nop().then_inc(g.mm_chunk, NCH * RING)
                pe.wait_ge(const_land, 16)

                def turn(q, u, rows_n):
                    for half in range(2):
                        pe.wait_ge(x_split, q * 2 + half + 1)
                        for k in range(4):
                            mm = pe.transpose(bank[2 * (u % 2) + half][:, k * P:k * P + rows_n],
                                              stage[u][0:rows_n, (4 * half + k) * P:(4 * half + k + 1) * P],
                                              g.ident[0:rows_n, 0:rows_n])
                        mm.then_inc(x_turned, 1)
                with pe.Fori(0, QB // STAGES) as it:
                    for u in range(STAGES):
                        pe.wait_ge(x_land[u], it * 16 + 16)
                        turn(it * STAGES + u, u, P)
                pe.wait_ge(xs_land, 16)
                turn(QB, 0, NS)
                for n in range(4):
                    s, hg = n // 2, n % 2
                    pe.wait_ge(rows_land[s], 16)
                    view = rows[s][:].rearrange("p (r h) -> p h r", h=FH)
                    for h in range(4):
                        mm = pe.transpose(bank[4 + n][:, h * P:(h + 1) * P], view[:, 4 * hg + h, :], g.ident[:])
                    mm.then_inc(rows_turned, 1)
                pe.wait_ge(x_split, 2 * QB + 6)
                product(g, pe, job(0, 0, 0), g.xh, g.xl, m=FH)
                pe.wait_ge(conv_land, 48)
                for f in range(FT):
                    mm = pe.transpose(bank[3][:, f * 20:(f + 1) * 20], conv_rows[:, f * P:(f + 1) * P], g.ident[0:20, 0:20])
                mm.then_inc(conv_turned, 1)
                pe.wait_ge(const_land, 64)
                for n in range(4):
                    s, hg = n // 2, n % 2
                    pe.wait_ge(wide_done, s + 1)
                    pe.wait_ge(rows_copied, n + 1)
                    if n < NCH:
                        pe.wait_ge(g.bank_free[n], 2)
                    for h in range(4):
                        pe.matmul(sums[n][:, h * P:(h + 1) * P], later_row[:], row_t[:, s, 4 * hg + h, :], start=True, stop=False)
                        mm = pe.matmul(sums[n][:, h * P:(h + 1) * P], total_b[s][:, 4 * hg + h, :], later_page[:], start=False, stop=True)
                    mm.then_inc(bias_mm, 1)

            @block.scalar
            def _(act):
                split_hi(g, act, job(0, 0, 0), KD, FH)
                split_hi(g, act, job(0, 0, 1))

                def round_half(q, u, rows_n, dst):
                    for half in range(2):
                        act.wait_ge(x_turned, q * 2 + half + (2 * STAGES + 1))
                        act.activation(dst[:, 4 * half:4 * half + 4, :],
                                       bank[2 * (u % 2) + half][:, :].rearrange("p (k t) -> p k t", k=4)[:, :, 0:rows_n],
                                       ACT.Copy).then_inc(x_rounded, 1)
                with act.Fori(0, QB // STAGES) as it:
                    for u in range(STAGES):
                        round_half(it * STAGES + u, u, P, g.xh[:, :, ds((it * STAGES + u) * P, P)])
                round_half(QB, 0, NS, g.xh[:, :, SEQ:T])
                for s in range(2):
                    act.wait_ge(total_done, s + 1)
                    act.activation(total_b[s][:], total[s][:].unsqueeze(2).to_broadcast([P, FH, P]), ACT.Copy).then_inc(wide_done, 1)
                for n in range(4):
                    act.wait_ge(rows_turned, n + 1)
                    act.activation(row_t[:, n // 2, 4 * (n % 2):4 * (n % 2) + 4, :],
                                   bank[4 + n][:, :].rearrange("p (h r) -> p h r", h=4), ACT.Copy).then_inc(rows_copied, 1)
                act.wait_ge(const_land, 64)
                for n in range(NCH):
                    chunk_ready(g, act, 0, n)
                    act.activation(z[:, chunk(n)], bank[n][0:FH, 0:TC], ACT.Identity, bias=bf_col[:]).then_inc(g.bank_free[n], 1)
                act.wait_ge(ff_chain, 2)
                act.activation(ez[:], zn[:], ACT.Exp).then_inc(ff_act, 1)
                act.wait_ge(ff_act, 1)
                act.activation(ez[:], ez[:], ACT.Ln, bias=1.0).then_inc(ff_act, 1)
                act.wait_ge(conv_turned, 1)
                act.activation(g.conv_cols[:], bank[3][:, 0:FT * 20].rearrange("p (f c) -> p f c", c=20), ACT.Copy)
                for n in range(4):
                    s, hg = n // 2, n % 2
                    act.wait_ge(bias_mm, n + 1)
                    for b in range(4):
                        act.activation(
                            g.dec_bias[:, 4 * s + b, 0:NPG, 4 * hg:4 * hg + 4].rearrange("p s h -> p h s"),
                            sums[n][:, :].rearrange("p (h b s) -> p b h s", h=4, b=4)[:, b], ACT.Copy)

            @block.vector
            def _(dve):
                dve.memset(g.eps[:], EPS)
                dve.nop().then_inc(x_split, 4)
                dve.nop().then_inc(g.w_split, RING)
                for n in range(NCH):
                    dve.nop().then_inc(g.bank_free[n], 1)
                split_lo(g, dve, job(0, 0, 0), KD, FH)
                split_lo(g, dve, job(0, 0, 1))

                def split_half(q, u, rows_n, cols):
                    for half in range(2):
                        dve.wait_ge(x_rounded, q * 2 + half + 1)
                        dve.tensor_tensor(g.xl[:, 4 * half:4 * half + 4, cols],
                                          bank[2 * (u % 2) + half][:, :].rearrange("p (k t) -> p k t", k=4)[:, :, 0:rows_n],
                                          g.xh[:, 4 * half:4 * half + 4, cols].bitcast(F32),
                                          ALU.subtract).then_inc(x_split, 1)
                with dve.Fori(0, QB // STAGES) as it:
                    for u in range(STAGES):
                        split_half(it * STAGES + u, u, P, ds((it * STAGES + u) * P, P))
                split_half(QB, 0, NS, slice(SEQ, T))
                for s in range(2):
                    dve.wait_ge(rows_land[s], 16)
                    dve.tensor_reduce(total[s][:], rows[s][:].rearrange("p (r h) -> p h r", h=FH), AX.X, ALU.add).then_inc(total_done, 1)
                for n in range(NCH):
                    dve.wait_ge(g.bank_free[n], 2)
                ch = Chain(dve, ff_chain)
                ch.link(dve.tensor_scalar(zn[:], z[:], -1.0, None, ALU.mult))
                ch.link(dve.tensor_tensor(zn[:], zn[:], z[:], ALU.min))
                dve.wait_ge(ff_act, 2)
                ch.link(dve.scalar_tensor_tensor(g.lf[:], z[:], 0.0, ez[:], ALU.min, ALU.subtract))

            @block.gpsimd
            def _(pool):
                pool.dma_start(ids[:], a["page_table"].rearrange("(s b) p -> (b p) s", s=2), allow_slow_non_contiguous=True).then_inc(ids_land, 16)
                load_weight(g, pool, job(0, 0, 0), w_in_tile(a, C_FF, FH), KD, FH)
                load_weight(g, pool, job(0, 0, 1), w_in_tile(a, C_FQ))
                pool.wait_ge(ids_land, 16)
                for s in range(2):
                    pool.indirect_dma_start(rows[s][:], None, a["cache_logf"].rearrange("a n r h -> (a n) (r h)"),
                                            bass.IndirectOffsetOnAxis(ap=ids[:, s:s + 1], axis=0)).then_inc(rows_land[s], 16)



def fox(nc, g, a, c, o):
    with ExitStack() as ctx:
        sb = lambda n, s, d=F32: ctx.enter_context(nc.sbuf_tensor(n, s, d))
        sem = lambda n: ctx.enter_context(nc.semaphore(n))
        kT, vT = sb("fk_t", [P, T]), sb("fv_t", [P, T])
        q_new_t = sb("fq_new_t", [P, NS])
        q1, q2, k1, k2 = (sb(n, [P, 2, SEQ], F32R) for n in ("q_hi_lo", "q_hi_sel", "k_hi_hi", "k_lo_cum"))
        kv = [sb(f"kv_rows{u}", [P, QB + 1, 2, P]) for u in range(2)]
        prob = [sb(f"prob{i}", [P, SEQ]) for i in range(2)]
        prob_t = [sb(f"prob_t{i}", [P, QB, P]) for i in range(2)]
        o_rows = sb("fox_rows", [P, QB, P])
        foT = sb("fox_t", [P, SEQ])
        nmax = [sb(f"neg_max{i}", [P, 1]) for i in range(2)]
        psum_row = [sb(f"prob_sum{i}", [P, 1]) for i in range(2)]
        inv = [sb(f"prob_inv{i}", [P, 1]) for i in range(2)]
        causal, ident_b = sb("causal", [P, P], BF16), sb("ident_b", [P, P], BF16)
        sel_head = sb("sel_head", [P, FH])
        cum, ones = sb("cum", [FH, SEQ]), sb("ones8", [P, SEQ])
        bank = g.bank
        const_land, kv_stored, fo_stored = sem("fox_const"), [sem("kv_stored0"), sem("kv_stored1")], sem("fo_stored")
        turned, turned_out = sem("kv_turned"), sem("kv_turned_out")
        logits, row_max, expd = sem("logits"), sem("row_max"), sem("expd")
        pt = [sem("prob_turned0"), sem("prob_turned1")]
        pt_out = [sem("prob_t_out0"), sem("prob_t_out1")]
        sum_chain, parts_ready, lf_turned = (sem(n) for n in ("sum_chain", "parts_ready", "lf_turned"))
        hi_out = sem("qk_hi_out")
        pv, pv_out, inv_done, sel_ready = sem("pv"), sem("pv_out"), sem("inv_done"), sem("sel_ready")
        fo_turned, fo_out = sem("fo_turned"), sem("fo_out")
        STEPS = 2 * QB
        LONG = [s for s in range(STEPS) if s // 2 >= 4]

        k_out = o[2].rearrange("d b (t p) h e -> (d b) p t (h e)", p=P)
        v_out = o[3].rearrange("d b (t p) h e -> (d b) p t (h e)", p=P)
        NIT = FH // 4

        def own(r):
            return slice(r * HD, (r + 1) * HD)

        def prompt_chunk(n):
            end = min((n + 1) * TC, SEQ)
            return slice(n * TC, end), end - n * TC

        with nc.Block() as block:
            @block.gpsimd
            def _(pool):
                with pool.Fori(0, NIT) as it:
                    for u in range(2):
                        for w, col in enumerate((C_FQ, C_FK, C_FV)):
                            j = 3 * u + w
                            if j == 0:
                                continue
                            load_weight(g, pool, job(it * 6 + 1, 1, j), w_in_tile(a, it * (2 * P) + (col + u * P)))
                    load_weight(g, pool, job(it * 6 + 1, 1, 6), w_in_tile(a, (1 - it) * (C_FQ + 2 * P)))

            @block.sync
            def _(sp):
                for dst, src in ((causal, "causal"), (ident_b, "ident_b"), (sel_head, "sel_head")):
                    sp.dma_start(dst[:], c[src]).then_inc(const_land, 16)
                with sp.Fori(0, NIT) as it:
                    for u in range(2):
                        pair = it * 2 + u
                        sp.wait_ge(turned_out, (pair + 1) * (QB + 1))
                        sp.dma_start(k_out[0][:, :, ds(pair * P, P)], kv[u][:, 0:QB, 0, :]).then_inc(kv_stored[u], 16)
                        sp.dma_start(v_out[0][:, :, ds(pair * P, P)], kv[u][:, 0:QB, 1, :]).then_inc(kv_stored[u], 16)
                        sp.wait_ge(fo_out, (pair + 1) * QB + 1)
                        sp.dma_start(g.fo_dram[ds(pair, 1), :, 0:SEQ].rearrange("a p t -> (a p) t"), foT[:]).then_inc(fo_stored, 16)
                sp.wait_ge(fo_stored, 2 * NIT * 16)
                for u in range(2):
                    sp.wait_ge(kv_stored[u], NIT * 32)

            @block.tensor
            def _(pe):
                with pe.Fori(0, NIT) as it:
                    for u in range(2):
                        pair = it * 2 + u
                        for w in range(3):
                            j = 3 * u + w
                            product(g, pe, job(it * 6 + 1, 1, j), g.xh, g.xl)
                        for n in range(NCH):
                            pe.wait_ge(g.bank_free[n], it * 6 + 3 * u + 5)
                        for t in range(QB + 1):
                            n = P if t < QB else NS
                            b = bank[7] if t % 2 == 0 else bank[3]
                            if t >= 2:
                                pe.wait_ge(turned_out, pair * (QB + 1) + t - 1)
                            pe.transpose(b[0:n, 0:P], kT[:, t * P:t * P + n], g.ident[:])
                            mm = pe.transpose(b[0:n, P:2 * P], vT[:, t * P:t * P + n], g.ident[:])
                            if t == QB:
                                mm = pe.transpose(b[0:n, 2 * P:3 * P], q_new_t[:], g.ident[:])
                            mm.then_inc(turned, 1)
                        pe.wait_ge(turned_out, (pair + 1) * (QB + 1))
                        pe.wait_ge(sel_ready, pair + 1)
                        pe.wait_ge(const_land, 48)
                        pe.wait_ge(parts_ready, 1)

                        def qk(s):
                            i, r = s // 2, s % 2
                            pe.wait_ge(expd, pair * STEPS + s + 1)
                            for piece in range(0, i + 1, 4):
                                n = min(4, i + 1 - piece)
                                out = bank[3 + 2 * (s % 2) + piece // 4]
                                last = piece + n == i + 1
                                pe.matmul(out[:, 0:n * P], q1[:, r, i * P:(i + 1) * P], k1[:, r, piece * P:(piece + n) * P],
                                          start=True, stop=False, skip_group_check=True)
                                mm = pe.matmul(out[:, 0:n * P], q2[:, r, i * P:(i + 1) * P], k2[:, r, piece * P:(piece + n) * P],
                                               start=False, stop=not last, skip_group_check=True)
                                if last:
                                    mm = pe.matmul(out[:, (n - 1) * P:n * P], ident_b[:], causal[:],
                                                   start=False, stop=True, skip_group_check=True)
                            mm.then_inc(logits, 1)

                        def turn_prob(s):
                            i = s // 2
                            pe.wait_ge(expd, pair * STEPS + s + 3)
                            for part in range(1 if i < 4 else 2):
                                done = pair * STEPS + s if part == 0 else pair * len(LONG) + LONG.index(s)
                                pe.wait_ge(pt_out[part], done + 1)
                                for n, blk in enumerate(range(4 * part, min(i + 1, 4 * part + 4))):
                                    mm = pe.transpose(bank[part][:, n * P:(n + 1) * P], prob[s % 2][:, blk * P:(blk + 1) * P], g.ident[:])
                                mm.then_inc(pt[part], 1)

                        def values(s):
                            i, r = s // 2, s % 2
                            pe.wait_ge(pt_out[0], pair * STEPS + s + 2)
                            if i >= 4:
                                pe.wait_ge(pt_out[1], pair * len(LONG) + LONG.index(s) + 2)
                            pe.wait_ge(pv_out, pair * STEPS + s + 1)
                            for blk in range(i + 1):
                                mm = pe.matmul(bank[2][:, 0:HD], prob_t[s % 2][:, blk, :], kv[u][:, blk, 1, r * HD:(r + 1) * HD],
                                               start=(blk == 0), stop=(blk == i))
                            mm.then_inc(pv, 1)

                        def turn_out(i):
                            pe.wait_ge(pv_out, pair * STEPS + 2 * i + 3)
                            pe.wait_ge(fo_out, pair * QB + i + 1)
                            pe.transpose(bank[7][:, 0:P], o_rows[:, i, :], g.ident[:]).then_inc(fo_turned, 1)

                        pe.wait_ge(fo_out, pair * QB + 1)
                        qk(0)
                        for s in range(STEPS):
                            if s + 1 < STEPS:
                                qk(s + 1)
                            turn_prob(s)
                            if s >= 1:
                                values(s - 1)
                            if s >= 3 and s % 2 == 1:
                                turn_out((s - 3) // 2)
                        values(STEPS - 1)
                        turn_out(QB - 1)
                        pe.wait_ge(fo_out, (pair + 1) * QB + 1)
                for t in range(QB + 1):
                    n = P if t < QB else NS
                    mm = pe.transpose(bank[3][0:n, t * FH:(t + 1) * FH], g.lf[:, t * P:t * P + n], g.ident[0:FH, 0:FH])
                mm.then_inc(lf_turned, 1)

            @block.scalar
            def _(act):
                act.nop().then_inc(expd, 2)
                act.nop().then_inc(pt_out[1], 1)
                act.nop().then_inc(fo_out, 1)
                with act.Fori(0, NIT) as it:
                    for u in range(2):
                        pair = it * 2 + u
                        j0 = it * 6 + 1 + 3 * u
                        for w, parts in ((0, (q1, q2)), (1, (k1,))):
                            split_hi(g, act, job(it * 6 + 1, 1, 3 * u + w + 1))
                            for n in range(NCH):
                                chunk_ready(g, act, j0 + w, n)
                                cols, width = prompt_chunk(n)
                                for dst in parts:
                                    for r in range(2):
                                        ins = act.activation(dst[own(r), r, cols], bank[n][own(r), 0:width], ACT.Copy,
                                                             scale=HD ** -0.5 if w == 0 else 1.0)
                                if w == 0 and n == NCH - 1:
                                    ins = act.activation(q_new_t[:], bank[n][:, width:TC], ACT.Copy, scale=HD ** -0.5)
                                if w == 1:
                                    ins = act.activation(kT[:, chunk(n)], bank[n][:, 0:TC], ACT.Copy)
                                ins.then_inc(hi_out, 1)
                        split_hi(g, act, job(it * 6 + 1, 1, 3 * u + 3))
                        act.wait_ge(kv_stored[u], it * 32)
                        for t in range(QB + 1):
                            n = P if t < QB else NS
                            b = bank[7] if t % 2 == 0 else bank[3]
                            act.wait_ge(turned, pair * (QB + 1) + t + 1)
                            if t == QB:
                                act.activation(g.knew[:, ds(pair * P, P)], b[0:NS, 0:P], ACT.Copy)
                                act.activation(g.vnew[:, ds(pair * P, P)], b[0:NS, P:2 * P], ACT.Copy)
                                act.activation(g.qnew[:, ds(pair * P, P)], b[0:NS, 2 * P:3 * P], ACT.Copy).then_inc(turned_out, 1)
                            else:
                                act.activation(kv[u][:, t, :, :], b[:, 0:2 * P].rearrange("p (w e) -> p w e", w=2), ACT.Copy).then_inc(turned_out, 1)

                        def softmax(s):
                            i = s // 2
                            act.wait_ge(row_max, pair * STEPS + s + 1)
                            act.wait_ge(pt_out[0], pair * STEPS + s)
                            act.wait_ge(pt_out[1], pair * len(LONG) + max(0, s - 2 - LONG[0] + 1) + 1)
                            act.wait_ge(inv_done, pair * STEPS + s + 1)
                            span = (i + 1) * P
                            act.activation(prob[s % 2][:, 0:span], g.pair[s % 2][:, 0:span], ACT.Exp,
                                           bias=nmax[s % 2][:], accum_out=psum_row[s % 2][:]).then_inc(expd, 1)

                        softmax(0)
                        for s in range(STEPS):
                            if s + 1 < STEPS:
                                softmax(s + 1)
                            if s in LONG:
                                n = s // 2 + 1 - 4
                                act.wait_ge(pt[1], pair * len(LONG) + LONG.index(s) + 1)
                                act.activation(prob_t[s % 2][:, 4:4 + n, :], bank[1][:, 0:n * P].rearrange("p (b t) -> p b t", t=P), ACT.Copy).then_inc(pt_out[1], 1)
                            if s >= 3 and s % 2 == 1:
                                fo_copy(g, act, pair, (s - 3) // 2, fo_turned, fo_out, fo_stored, foT)
                        fo_copy(g, act, pair, QB - 1, fo_turned, fo_out, fo_stored, foT)
                act.wait_ge(lf_turned, 1)
                act.activation(g.lf_rows[:, 0:QB, :], bank[3][:, 0:QB * FH].rearrange("p (t h) -> p t h", h=FH), ACT.Copy)
                act.activation(g.lfnew[:], bank[3][0:NS, QB * FH:(QB + 1) * FH], ACT.Copy)
                act.activation(g.lf_rows[0:NS, QB, :], bank[3][0:NS, QB * FH:(QB + 1) * FH], ACT.Copy)

            @block.vector
            def _(dve):
                dve.nop().then_inc(pt_out[0], 1)
                dve.nop().then_inc(pv_out, 1)
                dve.nop().then_inc(inv_done, 2)
                dve.memset(ones[:], 0.0).then_inc(sum_chain, 1)
                dve.wait_ge(sum_chain, 1)
                ch = Chain(dve, sum_chain, 1)
                for r in range(2):
                    ch.link(dve.tensor_copy(k2[own(1 - r), r, :], ones[own(1 - r), :]))
                ch.link(dve.memset(ones[:], 1.0))
                ch.link(dve.tensor_tensor_scan(cum[:], ones[0:FH, :], g.lf[:, 0:SEQ], 0.0, ALU.mult, ALU.add))
                ch.link(dve.tensor_scalar(cum[:], cum[:], -1.0, None, ALU.mult))
                ch.link(dve.tensor_copy(k2[0:FH, 1, :], cum[:]))
                ch.link(dve.tensor_copy(k2[HD:HD + FH, 0, :], cum[:]))
                for at, r in ((32, 1), (HD + 32, 0)):
                    ch.link(dve.tensor_tensor(k2[at:at + FH, r, :], cum[:], k2[0:FH, 1, :].bitcast(F32), ALU.subtract))
                dve.nop().then_inc(parts_ready, 1)
                dve.wait_ge(const_land, 48)
                with dve.Fori(0, NIT) as it:
                    for u in range(2):
                        pair = it * 2 + u
                        j0 = it * 6 + 1 + 3 * u
                        for w in range(3):
                            split_lo(g, dve, job(it * 6 + 1, 1, 3 * u + w + 1))
                            if w == 1:
                                dve.wait_ge(pv, pair * STEPS)
                                for r in range(2):
                                    ins = dve.tensor_scalar(q2[own(1 - r), r, :], ones[own(1 - r), :], sel_head[own(1 - r), ds(pair * 2 + r, 1)], None, ALU.mult)
                                ins.then_inc(sel_ready, 1)
                            if w == 2:
                                continue
                            for n in range(NCH):
                                cols, width = prompt_chunk(n)
                                dve.wait_ge(hi_out, pair * 6 + 3 * w + n + 1)
                                for r in range(2):
                                    if w == 0:
                                        ins = dve.scalar_tensor_tensor(q1[own(1 - r), r, cols], bank[n][own(r), 0:width], HD ** -0.5,
                                                                       q1[own(r), r, cols].bitcast(F32), ALU.mult, ALU.subtract)
                                    else:
                                        dve.tensor_copy(k1[own(1 - r), r, cols], bank[n][own(r), 0:width])
                                        ins = dve.tensor_tensor(k2[own(r), r, cols], bank[n][own(r), 0:width],
                                                                k1[own(r), r, cols].bitcast(F32), ALU.subtract)
                                ins.then_inc(g.bank_free[n], 1)
                        for n in range(NCH):
                            chunk_ready(g, dve, j0 + 2, n)
                            dve.tensor_copy(vT[:, chunk(n)], bank[n][:, 0:TC]).then_inc(g.bank_free[n], 1)

                        def maxima(s):
                            i = s // 2
                            dve.wait_ge(logits, pair * STEPS + s + 1)
                            dve.tensor_reduce(nmax[s % 2][:], g.pair[s % 2][:, 0:(i + 1) * P], AX.X, ALU.max, negate=True).then_inc(row_max, 1)

                        def normalise(s):
                            i, r = s // 2, s % 2
                            dve.wait_ge(pv, pair * STEPS + s + 1)
                            dve.wait_ge(fo_out, pair * QB + 1)
                            dve.tensor_scalar(o_rows[:, i, r * HD:(r + 1) * HD], bank[2][:, 0:HD], inv[s % 2][:], None, ALU.mult).then_inc(pv_out, 1)

                        maxima(0)
                        for s in range(STEPS):
                            if s + 1 < STEPS:
                                maxima(s + 1)
                            n = min(s // 2 + 1, 4)
                            dve.wait_ge(pt[0], pair * STEPS + s + 1)
                            dve.tensor_copy(prob_t[s % 2][:, 0:n, :], bank[0][:, 0:n * P].rearrange("p (b t) -> p b t", t=P)).then_inc(pt_out[0], 1)
                            dve.wait_ge(pv_out, pair * STEPS + s)
                            dve.reciprocal(inv[s % 2][:], psum_row[s % 2][:]).then_inc(inv_done, 1)
                            dve.wait_ge(inv_done, pair * STEPS + s + 3)
                            if s >= 1:
                                normalise(s - 1)
                        normalise(STEPS - 1)


def fo_copy(g, act, pair, i, fo_turned, fo_out, fo_stored, foT):
    if i == 0:
        act.wait_ge(fo_stored, pair * 16)
    act.wait_ge(fo_turned, pair * QB + i + 1)
    act.activation(foT[:, i * P:(i + 1) * P], g.bank[7][:, 0:P], ACT.Copy).then_inc(fo_out, 1)



GRP = 2
NG = NPG // GRP
SLOTS = 4
VALUES_A = (1,) * 6 + (1,) * 3 + (1,) * 7
KEYS_A = (1, 2, 1, 1, 2, 1) + (1,) * 3 + (1, 1, 1, 1, 1, 0, 0)
VALUES_B = (1,) * 12 + (2, 2)
VALUES_B_LAST = (2,) * 8
KEYS_B = (1,) + (1, 1, 2, 1) + (2,) + (1,) * 6 + (1, 1, 0, 0)
assert all(sum(s) == NG for s in (VALUES_A, KEYS_A, VALUES_B, VALUES_B_LAST, KEYS_B))


def take(counts, e):
    return range(sum(counts[:e]), sum(counts[:e + 1]))


def share(total, parts, e):
    return range(total * e // parts, total * (e + 1) // parts)


def retain(nc, g, a, c, o):
    with ExitStack() as ctx:
        sb = lambda n, s, d=F32: ctx.enter_context(nc.sbuf_tensor(n, s, d))
        sem = lambda n: ctx.enter_context(nc.semaphore(n))
        keys = [sb(f"cache_keys{i}", [P, GRP, FH * HD]) for i in range(SLOTS)]
        vals = [sb(f"cache_vals{i}", [P, GRP, FH * HD]) for i in range(SLOTS)]
        pages = sb("page_list", [1, NS * NPG], I32)
        qb = [sb(f"q_wide{i}", [P, FH * HD]) for i in range(2)]
        score = [sb(f"score{i}", [P, NPG + 1, FH]) for i in range(2)]
        new_prod = g.qnew
        own8 = sb("own8", [NS, NS, FH])
        own = sb("own", [NS, NS])
        own_col = sb("own_col", [P, NS, NS])
        mx, gmx = sb("cache_max", [P, FH]), sb("cache_max_all", [P, FH])
        psum_p = [sb(f"cache_prob_sum{i}", [P, FH]) for i in range(2)]
        ones_col = sb("ones_col", [P, 1])
        inv_l, o_dec = sb("dec_inv", [P, 1]), sb("dec_out", [P, P])
        fos = sb("fox_sample_t", [P, FH // 2, NS])
        cos, sin = sb("cos", [P, T]), sb("sin", [P, T])
        hc = sb("head_const", [P, 2 * P + 4])
        gn = sb("group_norm_cols", [P, 2, 2])
        rqT, rkT = sb("rq_t", [P, T]), sb("rk_t", [P, T])
        rvT = sb("rv_t", [P, 2, T])
        t1, t2 = sb("rot_cos", [P, TC]), sb("rot_sin", [P, TC])
        krows = sb("rk_rows", [P, QB + 1, P])
        vrows = sb("rv_rows", [P, QB + 1, DV])
        qd = sb("q_decayed_t", [P, QB, P])
        inner = sb("inner_t", [P, QB, P])
        state = [sb(f"state{i}", [P, DV]) for i in range(3)]
        st_s = sb("state_samples", [P, NS, DV])
        kmask = inner[0:NS]
        qmask = sb("q_own", [P, NS, NS])
        stats, mv = sb("gn_stats", [P, 6]), sb("gn_mean_var", [P, QB + 1, 2])
        rstd = sb("gn_rstd", [P, QB + 1])
        sg = [t1, t2]
        bank = g.bank

        const_land, hc_land, q_stored, qb_land = sem("ret_const"), sem("hc_land"), sem("q_stored"), [sem("qb_land0"), sem("qb_land1")]
        k_land, v_land = [sem(f"k_land{i}") for i in range(SLOTS)], [sem(f"v_land{i}") for i in range(SLOTS)]
        k_used, v_used = sem("k_used"), sem("v_used")
        k_mult, new_mult, biased, maxed, gmaxed = (sem(n) for n in ("k_mult", "new_mult", "biased", "maxed", "gmaxed"))
        shifted, prob, summed, pv, normed, turned, fos_out, fos_stored = (
            sem(n) for n in ("dec_shifted", "dec_prob", "dec_summed", "dec_pv", "dec_normed", "dec_turned", "dec_fos_out", "dec_fos_stored"))
        inv_ready, setup, new_stored, pages_land = sem("dec_inv_ready"), sem("ret_setup"), sem("new_stored"), sem("pages_land")
        rot_part, rot = sem("rot_part"), sem("rot")
        rows_t, rows_out = sem("rows_turned"), sem("rows_out")
        qd_done, ik, ik_out, st_new = sem("qd_done"), sem("ik"), sem("inner_out"), sem("state_new")
        o_mm, o_out, stat, mean, rstd_part, rstd_done, gnd = (sem(n) for n in ("ret_o", "ret_o_out", "gn_stat", "gn_mean", "rstd_part", "rstd_done", "gn_done"))
        rn_t, rn_out = sem("rn_turned"), sem("rn_out")
        gated, g_stored, st_stored, fin_stored = sem("gated"), sem("g_stored"), sem("st_stored"), sem("fin_stored")
        masks, s_land, kv_s, s_new = sem("own_masks"), sem("s_land"), sem("kv_sample"), sem("s_new")
        J0 = 13
        NJ = 6
        IN, QDEC = slice(0, P), slice(P, 2 * P)
        KDEC, CDEC, RDEC = (slice(2 * P + i, 2 * P + i + 1) for i in range(3))
        COLS = (C_RQ, C_RK, C_RV, C_RV + P, C_RG, C_RG + P)
        STEP = (DK, DK, DV, DV, DV, DV)
        NB = QB + 1

        def heads(eng, body):
            with eng.Fori(0, RH - 1) as h:
                body(h, False)
            body(RH - 1, True)

        with nc.Block() as block:
            @block.sync
            def _(sp):
                sp.dma_start(g.q_dram, g.qnew[:]).then_inc(q_stored, 16)
                sp.dma_start(pages[:], a["page_table"].rearrange("(a b) p -> a (b p)", a=1)).then_inc(pages_land, 16)
                for dst, src in ((cos, "cos"), (sin, "sin"), (own_col, "own_col")):
                    sp.dma_start(dst[:], c[src]).then_inc(const_land, 16)
                sp.dma_start(own8[:], c["own8"][0:NS]).then_inc(const_land, 16)
                sp.dma_start(own[:], c["own8"][0:NS, :, 0], allow_slow_non_contiguous=True).then_inc(const_land, 16)
                sp.wait_ge(q_stored, 16)
                sp.wait_ge(pages_land, 16)

                def load_q(n, u):
                    sp.dma_start(qb[u][:], g.q_dram[ds(n, 1), :].to_broadcast([P, FH * HD])).then_inc(qb_land[u], 16)

                def page_ids(n, q):
                    at = ds(n * NPG + q * (SLOTS * GRP), SLOTS * GRP)
                    return nc.values_load_multi_w_load_instructions(pages[0:1, at], [mybir.EngineType.SP],
                                                                    min_val=0, max_val=POOL - 1)[1]

                def load_group(ring, land, used, cache, n, q, slot, ids):
                    sp.wait_ge(used, n * NG + q * SLOTS + slot + 1)
                    for p in range(GRP):
                        page = cache[ds(ids[slot * GRP + p], 1)].rearrange("n r h e -> (n r) (h e)")
                        sp.dma_start(ring[slot][:, p, :], page).then_inc(land[slot], 16)

                ck, cv = (a[n].rearrange("a n r h e -> (a n) r h e") for n in ("cache_k", "cache_v"))
                load_q(0, 0)
                load_q(1, 1)
                with sp.Fori(0, NG // SLOTS) as q:
                    ids = page_ids(0, q)
                    for slot in range(SLOTS):
                        load_group(keys, k_land, k_used, ck, 0, q, slot, ids)

                def period(n):
                    with sp.Fori(0, NG // SLOTS) as q:
                        key_ids, value_ids = page_ids(n + 1, q), page_ids(n, q)
                        for slot in range(SLOTS):
                            load_group(keys, k_land, k_used, ck, n + 1, q, slot, key_ids)
                            load_group(vals, v_land, v_used, cv, n, q, slot, value_ids)

                with sp.Fori(0, RH - 1) as h:
                    for u in range(2):
                        period(h * 2 + u)
                        sp.wait_ge(new_mult, h * 2 + u + 1)
                        load_q(h * 2 + u + 2, u)
                period(NS - 2)
                with sp.Fori(0, NG // SLOTS) as q:
                    ids = page_ids(NS - 1, q)
                    for slot in range(SLOTS):
                        load_group(vals, v_land, v_used, cv, NS - 1, q, slot, ids)
                sp.dma_start(o[5].rearrange("d b t h e -> (d b t) (h e)"), g.knew[:]).then_inc(new_stored, 16)
                sp.dma_start(o[6].rearrange("d b t h e -> (d b t) (h e)"), g.vnew[:]).then_inc(new_stored, 16)
                sp.dma_start(o[4].rearrange("d b (t p) h -> p (d b t) h", p=P), g.lf_rows[:, 0:QB, :]).then_inc(new_stored, 16)
                sp.dma_start(o[7].rearrange("d b t h -> (d b t) h"), g.lf_rows[0:NS, QB, :]).then_inc(new_stored, 16)
                sp.wait_ge(new_stored, 64)
                sp.wait_ge(fos_out, NS)
                for j in range(FH // 2):
                    sp.dma_start(g.fo_dram[j, :, SEQ:T], fos[:, j, :]).then_inc(fos_stored, 16)
                sp.wait_ge(fos_stored, 16 * (FH // 2))

            @block.gpsimd
            def _(pool):
                def all_max(n):
                    wait_apart(pool, maxed, n + 1, g.mm_chunk)
                    pool.partition_all_reduce(gmx[:], mx[:], P, bass.bass_isa.ReduceOp.max).then_inc(gmaxed, 1)

                def load(h, j):
                    k = j % NJ
                    load_weight(g, pool, job(h * NJ + J0, 1, j), w_in_tile(a, h * STEP[k] + (COLS[k] + j // NJ * STEP[k])))

                for j in range(1, 5):
                    load(0, j)
                all_max(0)

                def body(h, last):
                    pool.wait_ge(gated, h * 6)
                    pool.dma_start(hc[:], c["head_const"][ds(h, 1)].rearrange("a p c -> (a p) c")).then_inc(hc_land, 16)
                    for w, name in enumerate(("ret_gn_w", "ret_gn_b")):
                        pool.dma_start(gn[:, w, :], a[name].rearrange("a (h e p) -> p (a h) e", e=2, p=P)[:, ds(h, 1), :].rearrange("p a e -> p (a e)"),
                                       allow_slow_non_contiguous=True).then_inc(hc_land, 16)
                    load(h, 5)
                    pool.wait_ge(st_stored, h * 16)
                    pool.dma_start(st_s[:], a["state_ret"].rearrange("a b h d e -> d (a h) b e")[:, ds(h, 1)].rearrange("d a b e -> d (a b) e")).then_inc(s_land, 16)
                    pool.wait_ge(hc_land, h * 48 + 48)
                    pool.wait_ge(rot, h * 6 + 3)
                    for t in range(QB):
                        ins = pool.tensor_tensor(qd[:, t, :], rqT[:, t * P:(t + 1) * P], hc[:, QDEC], ALU.mult)
                    ins.then_inc(qd_done, 1)
                    if last:
                        load_weight(g, pool, job(h * NJ + J0, 1, 6), w_in_tile(a, C_GA))
                    else:
                        load(h, 6)
                    all_max(h * 2 + 1)
                    if not last:
                        for j in range(7, 11):
                            load(h, j)
                        all_max(h * 2 + 2)
                heads(pool, body)

            @block.tensor
            def _(pe):
                def cache_values(n, u, i, first):
                    slot = i % SLOTS
                    if first:
                        pe.wait_ge(prob, n + 1)
                        pe.wait_ge(fos_out, n)
                    pe.wait_ge(v_land[slot], n * (NG // SLOTS * GRP * 16) + (i // SLOTS + 1) * GRP * 16)
                    for p in range(GRP):
                        for j in range(4):
                            mm = pe.matmul(bank[7][32 * j:32 * j + 2, 0:P], score[u][:, i * GRP + p, 2 * j:2 * j + 2],
                                           vals[slot][:, p, j * P:(j + 1) * P], start=(first and p == 0), stop=False)
                    mm.then_inc(v_used, 1)

                def cache_tail(n, u):
                    for j in range(4):
                        pe.matmul(bank[7][32 * j:32 * j + 2, 0:P], score[u][0:NS, NPG, 2 * j:2 * j + 2],
                                  g.vnew[:, j * P:(j + 1) * P], start=False, stop=True)
                    pe.wait_ge(summed, n + 1)
                    for j in range(4):
                        mm = pe.matmul(bank[7][32 * j:32 * j + 2, P:P + 1], psum_p[u][:, 2 * j:2 * j + 2],
                                       ones_col[:], start=True, stop=True)
                    mm.then_inc(pv, 1)

                def cache_turn(n):
                    pe.wait_ge(normed, n + 1)
                    pe.transpose(bank[7][:, 2 * P:3 * P], o_dec[:], g.ident[:]).then_inc(turned, 1)

                pe.nop().then_inc(v_used, SLOTS)

                for w in range(2):
                    product(g, pe, job(J0, 1, w), g.xh, g.xl)
                pe.wait_ge(setup, 1)

                def body(h, last):
                    def values_a(e):
                        for i in take(VALUES_A, e):
                            cache_values(h * 2, 0, i, i == 0)

                    def values_b(e):
                        for i in take(VALUES_B_LAST if last else VALUES_B, e):
                            cache_values(h * 2 + 1, 1, i, i == 0)

                    def ending(n):
                        if n == 0:
                            cache_tail(h * 2 + 1, 1)
                        elif n == 2:
                            cache_turn(h * 2 + 1)

                    for w in (2, 3):
                        product(g, pe, job(h * NJ + J0, 1, w), g.xh, g.xl, after=lambda n, w=w: values_a(3 * (w - 2) + n))
                    for n in range(NCH):
                        pe.wait_ge(g.bank_free[n], h * NJ + J0 + 5)
                    pe.wait_ge(rot, h * 6 + 6)
                    for t in range(NB):
                        n = P if t < QB else NS
                        b = bank[3] if t % 2 == 0 else bank[6]
                        if t >= 2:
                            pe.wait_ge(rows_out, h * NB + t - 1)
                        pe.transpose(b[0:n, 0:P], rkT[:, t * P:t * P + n], g.ident[:])
                        for e in range(2):
                            mm = pe.transpose(b[0:n, (1 + e) * P:(2 + e) * P], rvT[:, e, t * P:t * P + n], g.ident[:])
                        mm.then_inc(rows_t, 1)
                        if t % 3 == 2:
                            values_a(6 + t // 3)
                    pe.wait_ge(qd_done, h + 1)

                    def out(t):
                        b = bank[3] if t % 2 == 0 else bank[6]
                        pe.wait_ge(ik_out, h * QB + t + 1)
                        if t >= 1:
                            pe.wait_ge(st_new, h * QB + t)
                        if t >= 2:
                            pe.wait_ge(o_out, h * NB + t - 1)
                        mm = pe.matmul(b[:, 0:DV], inner[:, t, :], vrows[:, t, :], start=True, stop=(t == 0))
                        if t:
                            mm = pe.matmul(b[:, 0:DV], qd[:, t, :], state[t % 3][:], start=False, stop=True)
                        mm.then_inc(o_mm, 1)

                    for t in range(QB):
                        pe.wait_ge(rows_out, h * NB + max(t + 1, NB if t == 0 else 0))
                        if t >= 2:
                            pe.wait_ge(ik_out, h * QB + t - 1)
                            pe.wait_ge(st_new, h * QB + t - 1)
                        b = bank[4 + t % 2]
                        pe.matmul(b[:, 0:P], rkT[:, t * P:(t + 1) * P], rqT[:, t * P:(t + 1) * P], start=True, stop=True)
                        pe.matmul(b[:, P:P + DV], krows[:, t, :], vrows[:, t, :], start=True, stop=True).then_inc(ik, 1)
                        if t >= 1:
                            out(t - 1)
                        if t < QB - 1:
                            values_a(9 + t)
                        if t == QB - 2:
                            cache_tail(h * 2, 0)
                    out(QB - 1)
                    cache_turn(h * 2)
                    pe.wait_ge(masks, h * 2 + 2)
                    pe.wait_ge(st_new, (h + 1) * QB)
                    for b_ in range(NS):
                        if b_ >= 2:
                            pe.wait_ge(s_new, h * NS + b_ - 1)
                        pe.matmul(bank[4 + b_ % 2][:, 0:DV], kmask[:, b_, :], vrows[0:NS, QB, :], start=True, stop=True).then_inc(kv_s, 1)
                    values_b(0)
                    pe.wait_ge(o_out, h * NB + QB)
                    for b_ in range(NS):
                        pe.wait_ge(s_new, h * NS + b_ + 1)
                        mm = pe.matmul(bank[3][0:NS, 0:DV], qmask[:, b_, :], st_s[:, b_, :], start=(b_ == 0), stop=(b_ == NS - 1))
                    mm.then_inc(o_mm, 1)
                    values_b(1)
                    product(g, pe, job(h * NJ + J0, 1, 4), g.xh, g.xl, after=lambda n: values_b(2 + n))
                    for t in range(NB):
                        n = P if t < QB else NS
                        b = bank[3] if t % 2 == 0 else bank[6]
                        pe.wait_ge(gnd, h * NB + t + 1)
                        if t >= 2:
                            wait_apart(pe, rn_out, h * 2 * NB + 2 * t - 2, g.w_split)
                        for e in range(2):
                            mm = pe.transpose(b[:, e * P:e * P + n], vrows[0:n, t, e * P:(e + 1) * P], g.ident[0:n, 0:n])
                        mm.then_inc(rn_t, 1)
                        if t % 3 == 2:
                            values_b(5 + t // 3)
                    if last:
                        product(g, pe, job(h * NJ + J0, 1, 5), g.xh, g.xl, after=ending)
                    else:
                        product(g, pe, job(h * NJ + J0, 1, 5), g.xh, g.xl, after=lambda n: values_b(8 + n))
                        product(g, pe, job(h * NJ + J0, 1, 6), g.xh, g.xl, after=lambda n: values_b(11 + n))
                        product(g, pe, job(h * NJ + J0, 1, 7), g.xh, g.xl, after=ending)
                    pe.wait_ge(rn_out, (h + 1) * 2 * NB)
                heads(pe, body)

            @block.scalar
            def _(act):
                def cache_exp(n, u):
                    act.wait_ge(shifted, n + 1)
                    act.activation(score[u][:], score[u][:], ACT.Exp).then_inc(prob, 1)

                split_hi(g, act, job(J0, 1, 1))
                split_hi(g, act, job(J0, 1, 2))
                cache_exp(0, 0)

                def body(h, last):
                    nxt = lambda w: split_hi(g, act, job(h * NJ + J0, 1, w + 1))
                    for w in (2, 3):
                        nxt(w)
                        for n in range(NCH):
                            chunk_ready(g, act, h * NJ + J0 + w, n)
                            if w == 2 and n == 0:
                                act.wait_ge(g_stored, h * 32)
                            act.activation(rvT[:, w - 2, chunk(n)], bank[n][:, 0:TC], ACT.Copy).then_inc(g.bank_free[n], 1)
                    act.wait_ge(hc_land, h * 48 + 48)
                    for t in range(NB):
                        n = P if t < QB else NS
                        b = bank[3] if t % 2 == 0 else bank[6]
                        act.wait_ge(rows_t, h * NB + t + 1)
                        if t < QB:
                            act.activation(krows[:, t, :], b[:, 0:P], ACT.Copy, scale=hc[:, KDEC])
                        else:
                            act.activation(krows[0:n, t, :], b[0:n, 0:P], ACT.Copy)
                        act.activation(vrows[0:n, t, :], b[0:n, P:P + DV], ACT.Copy).then_inc(rows_out, 1)
                    for t in range(NB):
                        n = P if t < QB else NS
                        b = bank[3] if t % 2 == 0 else bank[6]
                        act.wait_ge(o_mm, h * NB + t + 1)
                        act.activation(vrows[0:n, t, :], b[0:n, 0:DV], ACT.Copy).then_inc(o_out, 1)
                        if t == QB - 1:
                            cache_exp(h * 2 + 1, 1)
                            nxt(4)
                    act.wait_ge(st_new, (h + 1) * QB)
                    act.dma_start(o[8].rearrange("a b h d e -> (a b h) d e")[ds(h, 1)].rearrange("a d e -> (a d) e"), state[QB % 3][:]).then_inc(fin_stored, 16)
                    act.wait_ge(s_new, (h + 1) * NS)
                    act.dma_start(o[9].rearrange("a b h d e -> d (a h) b e")[:, ds(h, 1)].rearrange("d a b e -> d (a b) e"), st_s[:]).then_inc(st_stored, 16)
                    act.wait_ge(rstd_part, h * 2 + 1)
                    act.activation(rstd[:], mv[:, :, 1], ACT.Sqrt).then_inc(rstd_part, 1)
                    for t in range(NB):
                        n = P if t < QB else NS
                        b = bank[3] if t % 2 == 0 else bank[6]
                        act.wait_ge(rn_t, h * NB + t + 1)
                        for e in range(2):
                            act.activation(rvT[:, e, t * P:t * P + n], b[:, e * P:e * P + n], ACT.Identity,
                                           scale=gn[:, 0, e:e + 1], bias=gn[:, 1, e:e + 1]).then_inc(rn_out, 1)
                    for w in (4, 5):
                        if w == 5:
                            nxt(5)
                        for n in range(NCH):
                            k = 3 * (w - 4) + n
                            chunk_ready(g, act, h * NJ + J0 + w, n)
                            act.wait_ge(gated, h * 6 + max(0, k - 1))
                            act.activation(sg[k % 2][:], bank[n][:, 0:TC], ACT.Silu).then_inc(g.bank_free[n], 1)
                        act.wait_ge(gated, h * 6 + 3 * (w - 3))
                        act.dma_start(g.g_dram[ds(h * 2 + (w - 4), 1)].rearrange("a p t -> (a p) t"), rvT[:, w - 4, :]).then_inc(g_stored, 16)
                    if not last:
                        nxt(6)
                        nxt(7)
                        cache_exp(h * 2 + 2, 0)
                heads(act, body)
                act.wait_ge(g_stored, RH * 32)
                act.wait_ge(st_stored, RH * 16)
                act.wait_ge(fin_stored, RH * 16)

            @block.vector
            def _(dve):
                def cache_logits(n, u, i):
                    if i < NG:
                        slot = i % SLOTS
                        if i == 0:
                            dve.wait_ge(qb_land[u], wide_count(n, u))
                        dve.wait_ge(k_land[slot], n * (NG // SLOTS * GRP * 16) + (i // SLOTS + 1) * GRP * 16)
                        dve.tensor_tensor(keys[slot][:], keys[slot][:], qb[u][:].unsqueeze(1).to_broadcast([P, GRP, FH * HD]), ALU.mult).then_inc(k_mult, 1)
                    if i >= 1:
                        slot = (i - 1) % SLOTS
                        dve.wait_ge(k_mult, n * NG + i)
                        dve.tensor_reduce(score[u][:, (i - 1) * GRP:i * GRP, :],
                                          keys[slot][:].rearrange("p g (h e) -> p g h e", e=HD), AX.X, ALU.add).then_inc(k_used, 1)

                def wide_count(n, u):
                    return (n - u) * 8 + 16

                def cache_max(n, u):
                    cache_logits(n, u, NG)
                    dve.tensor_tensor(new_prod[:], g.knew[:], qb[u][0:NS, :], ALU.mult).then_inc(new_mult, 1)
                    dve.wait_ge(new_mult, n + 1)
                    dve.tensor_reduce(score[u][0:NS, NPG, :], new_prod[:].rearrange("p (h e) -> p h e", e=HD), AX.X, ALU.add).then_inc(biased, 1)
                    dve.wait_ge(biased, n * 2 + 1)
                    dve.wait_ge(k_used, (n + 1) * NG + SLOTS)
                    dve.tensor_tensor(score[u][:], score[u][:], g.dec_bias[:, ds(n, 1)].rearrange("p a s h -> p (a s) h"), ALU.add).then_inc(biased, 1)
                    dve.wait_ge(biased, n * 2 + 2)
                    dve.tensor_reduce(mx[:], score[u][:].rearrange("p s h -> p h s"), AX.X, ALU.max).then_inc(maxed, 1)

                def cache_shift(n, u):
                    dve.wait_ge(gmaxed, n + 1)
                    dve.tensor_tensor(score[u][:], score[u][:], gmx[:].unsqueeze(1).to_broadcast([P, NPG + 1, FH]), ALU.subtract).then_inc(shifted, 1)

                def cache_sum(n, u):
                    dve.wait_ge(prob, n + 1)
                    dve.tensor_reduce(psum_p[u][:], score[u][:].rearrange("p s h -> p h s"), AX.X, ALU.add).then_inc(summed, 1)

                def cache_norm(n):
                    dve.wait_ge(pv, n + 1)
                    dve.reciprocal(inv_l[:], bank[7][:, P:P + 1]).then_inc(inv_ready, 1)
                    dve.wait_ge(inv_ready, n + 1)
                    dve.tensor_scalar(o_dec[:], bank[7][:, 0:P], inv_l[:], None, ALU.mult).then_inc(normed, 1)

                def cache_out(n):
                    dve.wait_ge(turned, n + 1)
                    for r in range(2):
                        rows = slice(r * HD, (r + 1) * HD)
                        ins = dve.tensor_copy(fos[rows, :, ds(n, 1)].rearrange("p j n -> p (j n)"),
                                              bank[7][rows, 2 * P + r:3 * P:32])
                    ins.then_inc(fos_out, 1)

                dve.nop().then_inc(k_used, SLOTS)
                split_lo(g, dve, job(J0, 1, 1))
                dve.wait_ge(q_stored, 16)
                dve.wait_ge(const_land, 80)
                dve.memset(ones_col[:], 1.0)
                dve.memset(bank[7][:, :], 1.0)
                dve.memset(mv[:], 1.0)
                for u in range(2):
                    dve.memset(score[u][:], 0.0)
                dve.tensor_tensor(own8[:], own8[:], g.lfnew[:].unsqueeze(1).to_broadcast([NS, NS, FH]), ALU.mult).then_inc(setup, 1)
                dve.wait_ge(setup, 1)
                dve.tensor_tensor(g.dec_bias[0:NS, :, NPG, :], g.dec_bias[0:NS, :, NPG, :], own8[:], ALU.subtract).then_inc(setup, 1)
                dve.wait_ge(setup, 2)
                def rotate(j, r0, w, n):
                    dst, scale, k, b = (rqT, rkT)[w], (1.0, DK ** -0.5)[w], 3 * w + n, bank[n]
                    chunk_ready(g, dve, j, n)
                    dve.wait_ge(rot, r0 + k)
                    dve.scalar_tensor_tensor(t1[:], b[:, 0:TC], scale, cos[:, chunk(n)], ALU.mult, ALU.mult).then_inc(rot_part, 1)
                    for r in range(2):
                        src, out = slice((1 - r) * 64, (2 - r) * 64), slice(r * 64, (r + 1) * 64)
                        ins = dve.scalar_tensor_tensor(t2[out, :], b[src, 0:TC], scale, sin[src, chunk(n)], ALU.mult, ALU.mult)
                    ins.then_inc(g.bank_free[n], 1)
                    dve.wait_ge(g.bank_free[n], j + 2)
                    dve.tensor_tensor(dst[:, chunk(n)], t1[:], t2[:], ALU.add).then_inc(rot, 1)

                for w in range(2):
                    if w:
                        split_lo(g, dve, job(J0, 1, 2))
                    for n in range(NCH):
                        rotate(J0 + w, 0, w, n)
                        for i in share(NG, 6, 3 * w + n):
                            cache_logits(0, 0, i)
                cache_max(0, 0)
                cache_shift(0, 0)

                def body(h, last):
                    def keys_a(e):
                        for i in take(KEYS_A, e):
                            cache_logits(h * 2 + 1, 1, i)

                    def keys_b(e):
                        if not last:
                            for i in take(KEYS_B, e):
                                cache_logits(h * 2 + 2, 0, i)

                    nxt = lambda w: split_lo(g, dve, job(h * NJ + J0, 1, w + 1))
                    nxt(2)
                    keys_a(0)
                    cache_sum(h * 2, 0)
                    for e in range(1, 6):
                        keys_a(e)
                    nxt(3)
                    for e in range(6, 9):
                        keys_a(e)
                    for t in range(QB):
                        b = bank[4 + t % 2]
                        dve.wait_ge(ik, h * QB + t + 1)
                        dve.tensor_tensor(inner[:, t, :], b[:, 0:P], hc[:, IN], ALU.mult).then_inc(ik_out, 1)
                        if t == 0:
                            dve.wait_ge(fin_stored, h * 16)
                            dve.tensor_copy(state[1][:], b[:, P:P + DV]).then_inc(st_new, 1)
                        else:
                            dve.wait_ge(st_new, h * QB + t)
                            if t >= 2:
                                dve.wait_ge(o_mm, h * NB + t - 1)
                            dve.scalar_tensor_tensor(state[(t + 1) % 3][:], state[t % 3][:], hc[:, CDEC], b[:, P:P + DV], ALU.mult, ALU.add).then_inc(st_new, 1)
                        if t < QB - 1:
                            keys_a(9 + t)
                        if t == QB - 2:
                            cache_max(h * 2 + 1, 1)
                    cache_norm(h * 2)
                    cache_shift(h * 2 + 1, 1)
                    cache_out(h * 2)
                    dve.wait_ge(o_mm, h * NB + QB)
                    dve.tensor_tensor(kmask, krows[0:NS, QB, :].unsqueeze(1).to_broadcast([NS, NS, DK]),
                                      own[:].unsqueeze(2).to_broadcast([NS, NS, DK]), ALU.mult).then_inc(masks, 1)
                    dve.tensor_tensor(qmask[:], rqT[:, SEQ:T].unsqueeze(1).to_broadcast([P, NS, NS]), own_col[:], ALU.mult).then_inc(masks, 1)
                    dve.wait_ge(s_land, h * 16 + 16)
                    for b_ in range(NS):
                        dve.wait_ge(kv_s, h * NS + b_ + 1)
                        dve.scalar_tensor_tensor(st_s[:, b_, :], st_s[:, b_, :], hc[:, RDEC], bank[4 + b_ % 2][:, 0:DV], ALU.mult, ALU.add).then_inc(s_new, 1)
                    nxt(4)
                    keys_b(0)
                    for t in range(NB):
                        n = P if t < QB else NS
                        dve.wait_ge(o_out, h * NB + t + 1)
                        dve.wait_ge(mean, h * NB + t)
                        dve.bn_stats(stats[0:n, :], vrows[0:n, t, :]).then_inc(stat, 1)
                        wait_apart(dve, stat, h * NB + t + 1, g.mm_chunk)
                        dve.bn_aggr(mv[0:n, t, :], stats[0:n, :]).then_inc(mean, 1)
                        if t % 2:
                            keys_b(1 + t // 2)
                    dve.wait_ge(mean, (h + 1) * NB)
                    dve.tensor_scalar(mv[:, :, 1], mv[:, :, 1], EPS, None, ALU.add).then_inc(rstd_part, 1)
                    dve.wait_ge(rstd_part, h * 2 + 2)
                    dve.reciprocal(rstd[:], rstd[:]).then_inc(rstd_done, 1)
                    dve.wait_ge(rstd_done, h + 1)
                    for t in range(NB):
                        n = P if t < QB else NS
                        dve.tensor_scalar(vrows[0:n, t, :], vrows[0:n, t, :], mv[0:n, t, 0:1], rstd[0:n, t:t + 1], ALU.subtract, ALU.mult).then_inc(gnd, 1)
                    cache_sum(h * 2 + 1, 1)
                    keys_b(5)
                    for w in (4, 5):
                        if w == 5:
                            nxt(5)
                        for n in range(NCH):
                            k = 3 * (w - 4) + n
                            dve.wait_ge(g.bank_free[n], h * NJ + J0 + w + 2)
                            dve.wait_ge(rn_out, (h + 1) * 2 * NB)
                            dve.tensor_tensor(rvT[:, w - 4, chunk(n)], rvT[:, w - 4, chunk(n)], sg[k % 2][:], ALU.mult).then_inc(gated, 1)
                            keys_b(6 + k)
                    if not last:
                        for w in (6, 7):
                            nxt(w)
                            for n in range(NCH):
                                rotate(h * NJ + (J0 + w), h * 6 + 6, w - 6, n)
                                if w == 6 or n == 0:
                                    keys_b(12 + 3 * (w - 6) + n)
                                elif n == 1:
                                    cache_norm(h * 2 + 1)
                                    cache_max(h * 2 + 2, 0)
                        cache_shift(h * 2 + 2, 0)
                        cache_out(h * 2 + 1)
                    else:
                        cache_norm(h * 2 + 1)
                        cache_out(h * 2 + 1)
                heads(dve, body)



def tile_of(w, f, k0=0, kt=KD):
    return w.rearrange("a (k p) c -> p (a k) c", p=P)[:, k0:k0 + kt, ds(f * P, P)]


def finish(nc, g, a, c, o):
    JA = 13 + 6 * RH
    JB = JA + 2 * KD
    JO = JB + 2 * KD
    JF = JO + KD
    NT = QB + 1
    assert (NT + 2) * D <= 2 * KD * T
    KB = FH // 2
    LANDS = 4
    FIRST_RAW = 4
    sections, f0, j0 = [], 0, JF
    for n in (8, 7, 7):
        sections.append((f0, n, j0, j0 + 2 * n))
        f0, j0 = f0 + n, j0 + 2 * n + KD
    JEND = j0
    assert f0 == FT
    with ExitStack() as ctx:
        sb = lambda n, s, d=F32: ctx.enter_context(nc.sbuf_tensor(n, s, d))
        sem = lambda n: ctx.enter_context(nc.semaphore(n))
        at = nc.sbuf_base
        acc = sb("acc", [P, KD, T])
        mh = nc.alloc_sbuf_tensor_at("merged_hi", [P, KD, T], F32R, offset=at)
        at = nc.sbuf_base
        gh, gl = sb("moving_hi", [P, KD, T], F32R), sb("moving_lo", [P, KD, T], F32R)
        z = nc.alloc_sbuf_tensor_at("z", [P, KD, T], F32, offset=at)
        g_raw = nc.alloc_sbuf_tensor_at("gated_raw", [P, KD, T], F32, offset=at + KD * T * 4)
        raw = [g_raw[:, n, :] for n in range(KD)] + [z[:, KB + n, :] for n in range(KB)]
        y = [nc.alloc_sbuf_tensor_at(f"y{i}", [P, D], F32, offset=g.x_at + i * D * 4) for i in range(NT)]
        wide = [nc.alloc_sbuf_tensor_at(f"ln2_wide{i}", [P, D], F32, offset=g.x_at + (NT + i) * D * 4) for i in range(2)]
        stage = [sb(f"stage{i}", [P, T + 2]) for i in range(2)]
        gate = [sb(f"gate{i}", [P, T]) for i in range(2)]
        tmp = sb("chunk_tmp", [P, TC])
        ln_cols = sb("ln1_cols", [P, 2, KD])
        over = sb("one_over_width", [P, P])
        zsum, rstd = stage[0], stage[1]
        SQUARES = 2 * NCH
        square = lambda i: gate[i % 2][:, chunk(i % SQUARES // 2)]
        up, act_in = stage
        fc = sb("conv_cols_tile", [P, 20])
        cr = gate[0][0:NS + 2, 0:P]
        bank = g.bank
        s_land, s_hi, s_lo, ln_land = [sem(f"raw_land{i}") for i in range(LANDS)], sem("stage_hi"), sem("stage_lo"), sem("ln_land")
        m_sum, m_hi, m_lo, over_set = sem("m_sum"), sem("m_hi"), sem("m_lo"), sem("over_set")
        z_part, z_done, z_summed, mean, centred, squared, var, root, inv = (
            sem(n) for n in ("z_part", "z_done", "z_summed", "mean", "centred", "squared", "var", "root", "inv_root"))
        normed, h_hi, h_lo, h_scaled = (sem(n) for n in ("z_normed", "h_hi", "h_lo", "h_scaled"))
        fc_done, c1, conv, gelu, a_hi, a_lo = (sem(n) for n in ("fc_done", "conv_first", "conv_step", "gelu", "a_hi", "a_lo"))
        cr_t, cr_out, cr_stored = sem("conv_rows_turned"), sem("conv_rows_out"), sem("conv_rows_stored")
        y_t, stat, y_var, y_root, y_inv, y_bias, y_norm, y_mul, y_add, wide_land = (
            sem(n) for n in ("y_turned", "y_stat", "y_var", "y_root", "y_inv", "y_bias", "y_norm", "y_mul", "y_add", "wide_land"))
        y_stored = sem("y_stored")
        stats = [sb(f"ln2_stats{i}", [P, 2, 6]) for i in range(2)]
        mv2 = [sb(f"ln2_mean_var{i}", [P, 4]) for i in range(2)]
        old_stored = sem("old_conv_stored")

        with nc.Block() as block:
            @block.sync
            def _(sp):
                for n in range(KD + KB):
                    if n == KD:
                        sp.wait_ge(g.mm_chunk, NCH * (RING + JB))
                    if n >= LANDS:
                        sp.wait_ge(s_hi, n - LANDS + 1)
                    sp.dma_start(raw[n], g.g_dram[n] if n < KD else g.fo_dram[n - KD]).then_inc(s_land[n % LANDS], 16)
                for w, name in enumerate(("ln1_w", "ln1_b")):
                    sp.dma_start(ln_cols[:, w, :], a[name].rearrange("a (k p) -> p (a k)", p=P), allow_slow_non_contiguous=True).then_inc(ln_land, 16)
                sp.dma_start(o[11][:, :, 0, :], a["state_conv"][:, :, 1, :]).then_inc(old_stored, 16)
                with sp.Fori(0, FT) as f:
                    sp.wait_ge(cr_out, f + 1)
                    sp.dma_start(o[10].rearrange("a b w f -> (a b w) f")[:, ds(f * P, P)], cr[0:2]).then_inc(cr_stored, 16)
                    sp.dma_start(o[11].rearrange("a b w f -> (a b) w f")[:, 1, ds(f * P, P)], cr[2:2 + NS]).then_inc(cr_stored, 16)
                sp.wait_ge(g.mm_chunk, NCH * (RING + sections[-1][3]))
                for w, name in enumerate(("ln2_w", "ln2_b")):
                    sp.dma_start(wide[w][:], a[name].to_broadcast([P, D])).then_inc(wide_land, 16)
                for t in range(NT):
                    sp.wait_ge(y_add, t + 1)
                    if t < QB:
                        sp.dma_start(o[0][0, t * P:(t + 1) * P, :], y[t][:]).then_inc(y_stored, 16)
                    else:
                        sp.dma_start(o[1].rearrange("b t d -> (b t) d"), y[t][0:NS, :]).then_inc(y_stored, 16)
                sp.wait_ge(y_stored, 16 * NT)
                sp.wait_ge(cr_stored, 32 * FT)
                sp.wait_ge(old_stored, 16)

            @block.gpsimd
            def _(pool):
                pool.memset(over[:], 1.0 / D).then_inc(over_set, 1)
                assert C_GA + D == C_GB

                def branch(it, base, col, w, kt, more=True):
                    load_weight(g, pool, job(base, 1, 1), tile_of(w, it * 2, 0, kt), kt)
                    load_weight(g, pool, job(base, 1, 2), w_in_tile(a, it * (2 * P) + (col + P)))
                    load_weight(g, pool, job(base, 1, 3), tile_of(w, it * 2 + 1, 0, kt), kt)
                    if more:
                        load_weight(g, pool, job(base, 1, 4), w_in_tile(a, it * (2 * P) + (col + 2 * P)))
                with pool.Fori(0, KD // 2) as it:
                    branch(it, it * 4 + JA, C_GA, a["w_pa"], KD)
                with pool.Fori(0, KD // 2 - 1) as it:
                    branch(it, it * 4 + JB, C_GB, a["w_pb"], KB)
                branch(KD // 2 - 1, (KD // 2 - 1) * 4 + JB, C_GB, a["w_pb"], KB, more=False)
                with pool.Fori(0, KD // 2) as it:
                    for u in range(2):
                        load_weight(g, pool, job(it * 2 + JO, JO % 2, u), tile_of(a["w_o"], it * 2 + u))
                def up_and_gate(i, f0, ju):
                    for u, w in enumerate((a["w_up"], a["w_gate"])):
                        load_weight(g, pool, job(i * 2 + ju, ju % 2, u), tile_of(w, i + f0))
                for s, (f0, n, ju, jd) in enumerate(sections):
                    if s == 0:
                        up_and_gate(0, f0, ju)
                        for k in range(NCH):
                            pool.wait_ge(normed, (k + 1) * KD)
                            for t in range(KD):
                                ins = pool.tensor_scalar(acc[:, t, chunk(k)], z[:, t, chunk(k)], ln_cols[:, 1, t:t + 1], ALPHA, ALU.add, ALU.mult)
                            ins.then_inc(h_scaled, 1)
                    with pool.Fori(1 if s == 0 else 0, n) as i:
                        up_and_gate(i, f0, ju)
                    with pool.Fori(0, KD // 2) as it:
                        for u in range(2):
                            load_weight(g, pool, job(it * 2 + jd, jd % 2, u), tile_of(a["w_down"], it * 2 + u, f0, n), n)
                for t in range(QB):
                    pool.wait_ge(y_mul, t + 1)
                    pool.tensor_tensor(y[t][:], y[t][:], wide[1][:], ALU.add).then_inc(y_add, 1)

            @block.tensor
            def _(pe):
                with pe.Fori(0, KD // 2) as it:
                    for u in range(2):
                        product(g, pe, job(it * 4 + JA, 1, 2 * u), g.xh, g.xl)
                        product(g, pe, job(it * 4 + JA, 1, 2 * u + 1), gh, gl, ready=lambda k: pe.wait_ge(s_lo, k + 1))
                with pe.Fori(0, KD // 2) as it:
                    for u in range(2):
                        product(g, pe, job(it * 4 + JB, 1, 2 * u), g.xh, g.xl)
                        product(g, pe, job(it * 4 + JB, 1, 2 * u + 1), gh[:, 0:KB, :], gh[:, KB:2 * KB, :], KB,
                                ready=lambda k: pe.wait_ge(s_lo, KD + k + 1))
                pe.wait_ge(over_set, 1)
                of_m = dict(ready=lambda k: pe.wait_ge(m_lo, NCH * k + 1),
                            before=lambda n: pe.wait_ge(m_lo, NCH * (KD - 1) + n + 1) if n else None)

                def mean_of(n):
                    pe.wait_ge(z_summed, NCH * (KD - 1) + n + 1)
                    pe.matmul(bank[3 + n][:, 0:TC], over[:], zsum[:, chunk(n)], start=True, stop=True).then_inc(mean, 1)

                def var_of(n):
                    if n == 2:
                        pe.wait_ge(root, 1)
                    for k in range(KD):
                        pe.wait_ge(squared, n * KD + k + 1)
                        pe.matmul(bank[6 + n % 2][:, 0:TC], over[:], square(n * KD + k), start=(k == 0), stop=(k == KD - 1)).then_inc(var, 1)
                with pe.Fori(0, KD // 2 - 1) as it:
                    for u in range(2):
                        product(g, pe, job(it * 2 + JO, JO % 2, u), mh, gl, **of_m)
                product(g, pe, job(JO + KD - 2, JO % 2, 0), mh, gl, **of_m)
                product(g, pe, job(JO + KD - 2, JO % 2, 1), mh, gl, **of_m, after=lambda n: mean_of(n - 1) if n else None)
                mean_of(2)
                var_of(0)
                var_of(1)
                var_of(2)
                for f0, n, ju, jd in sections:
                    with pe.Fori(0, n) as i:
                        product(g, pe, job(i * 2 + ju, ju % 2, 0), g.xh, g.xl, before=lambda k: pe.wait_ge(h_lo, (k + 1) * KD))
                        product(g, pe, job(i * 2 + ju, ju % 2, 1), g.xh, g.xl)
                        pe.wait_ge(cr_out, i + f0)
                        pe.transpose(bank[3][0:NS + 2, 0:P], up[:, SEQ:SEQ + NS + 2], g.ident[:]).then_inc(cr_t, 1)
                    with pe.Fori(0, KD // 2) as it:
                        for u in range(2):
                            product(g, pe, job(it * 2 + jd, jd % 2, u), gh, gl, n, ready=lambda k: pe.wait_ge(a_lo, f0 + k + 1))
                for k in range(NCH):
                    pe.wait_ge(g.bank_free[k], JEND + 1)
                for t in range(NT):
                    n = P if t < QB else NS
                    if t >= 2:
                        pe.wait_ge(y_norm, t - 1)
                    for k in range(KD):
                        mm = pe.transpose(g.pair[t % 2][0:n, k * P:(k + 1) * P], acc[:, k, t * P:t * P + n], g.ident[:])
                    mm.then_inc(y_t, 1)

            @block.scalar
            def _(act):
                def raw_hi(n):
                    act.wait_ge(s_land[n % LANDS], 16 * (n // LANDS + 1))
                    act.activation(gh[:, n % KD, :], raw[n], ACT.Copy).then_inc(s_hi, 1)

                def gates(job, slot, chunks=range(NCH)):
                    for n in chunks:
                        chunk_ready(g, act, job, n)
                        act.activation(gate[slot][:, chunk(n)], bank[n][:, 0:TC], ACT.Sigmoid).then_inc(g.bank_free[n], 1)
                def branch(base, kt, last=False):
                    for u in range(2):
                        split_hi(g, act, job(base, 1, 2 * u + 2))
                        if not (last and u):
                            split_hi(g, act, job(base, 1, 2 * u + 3), kt)
                            gates(base + (2 * u + 2), (u + 1) % 2)
                LAST = KD // 2 - 1
                for n in range(KD):
                    if n == FIRST_RAW:
                        split_hi(g, act, job(JA, 1, 1))
                    raw_hi(n)
                    if n >= KD - NCH:
                        gates(JA, 0, [n - (KD - NCH)])
                with act.Fori(0, LAST) as it:
                    branch(it * 4 + JA, KD)
                branch(LAST * 4 + JA, KD, last=True)
                split_hi(g, act, job(JB, 1, 1), KB)
                for n in range(KD, KD + KB):
                    raw_hi(n)
                gates(JB, 0)
                with act.Fori(0, LAST) as it:
                    branch(it * 4 + JB, KB)
                branch(LAST * 4 + JB, KB, last=True)
                with act.Fori(0, KD // 2) as it:
                    for u in range(2):
                        split_hi(g, act, job(it * 2 + JO, JO % 2, u + 1))
                def squares(n, tiles=range(KD)):
                    act.wait_ge(centred, n + 1)
                    for k in tiles:
                        i = n * KD + k
                        if i >= SQUARES:
                            act.wait_ge(var, i - SQUARES + 1)
                        act.activation(square(i), z[:, k, chunk(n)], ACT.Square).then_inc(squared, 1)

                def root_of(n):
                    act.wait_ge(var, (n + 1) * KD)
                    act.activation(rstd[:, chunk(n)], bank[6 + n % 2][:, 0:TC], ACT.Sqrt, bias=g.eps[:]).then_inc(root, 1)

                def h_high(n):
                    for k in range(KD):
                        act.wait_ge(normed, n * KD + k + 1)
                        act.activation(g.xh[:, k, chunk(n)], z[:, k, chunk(n)], ACT.Identity, bias=ln_cols[:, 1, k:k + 1]).then_inc(h_hi, 1)
                act.wait_ge(ln_land, 32)
                squares(0)
                squares(1, range(0, 3))
                root_of(0)
                squares(1, range(3, KD))
                squares(2)
                root_of(1)
                h_high(0)
                root_of(2)
                h_high(1)
                h_high(2)
                act.wait_ge(h_lo, NCH * KD)
                act.wait_ge(z_part, 2)
                for s, (f0, n, ju, jd) in enumerate(sections):
                    with act.Fori(0, n) as i:
                        f = i + f0
                        split_hi(g, act, job(i * 2 + ju, ju % 2, 1))
                        act.wait_ge(conv, f * 5)
                        act.wait_ge(cr_t, f)
                        act.activation(fc[:], g.conv_cols[:, ds(f, 1), :].rearrange("p a c -> p (a c)"), ACT.Copy).then_inc(fc_done, 1)
                        for k in range(NCH):
                            chunk_ready(g, act, i * 2 + ju, k)
                            act.activation(up[:, 2 + k * TC:2 + (k + 1) * TC], bank[k][:, 0:TC], ACT.Copy).then_inc(g.bank_free[k], 1)
                        for k in range(NCH):
                            act.wait_ge(g.bank_free[k], i * 2 + ju + 2)
                        act.wait_ge(fc_done, f + 1)
                        act.wait_ge(a_lo, f)
                        act.activation(act_in[:, 0:SEQ], up[:, 0:SEQ], ACT.Identity, scale=fc[:, 16:17], bias=fc[:, 19:20]).then_inc(c1, 1)
                        split_hi(g, act, job(i * 2 + ju, ju % 2, 2))
                        act.wait_ge(conv, f * 5 + 5)
                        act.activation(act_in[:, 0:T], act_in[:, 0:T], ACT.Gelu_apprx_tanh).then_inc(gelu, 1)
                        for k in range(NCH):
                            act.wait_ge(g.bank_free[k], i * 2 + ju + 3)
                        if s == 0:
                            act.wait_ge(h_scaled, NCH)
                        act.activation(gh[:, ds(i, 1), :].rearrange("p a t -> p (a t)"), act_in[:, 0:T], ACT.Copy).then_inc(a_hi, 1)
                        act.wait_ge(cr_t, f + 1)
                        act.wait_ge(cr_stored, f * 32)
                        act.activation(cr, bank[3][0:NS + 2, 0:P], ACT.Copy).then_inc(cr_out, 1)

                    def down(it, last):
                        for u in range(2):
                            if not (last and u):
                                split_hi(g, act, job(it * 2 + jd, jd % 2, u + 1))
                    with act.Fori(0, KD // 2 - 1) as it:
                        down(it, False)
                    down(KD // 2 - 1, s == len(sections) - 1)
                for t in range(NT):
                    n = P if t < QB else NS
                    act.wait_ge(y_var, t + 1)
                    act.activation(mv2[t % 2][0:n, 2:3], mv2[t % 2][0:n, 1:2], ACT.Sqrt, bias=g.eps[0:n]).then_inc(y_root, 1)
                    act.wait_ge(y_bias, t + 1)
                    act.activation(y[t][0:n, :], g.pair[t % 2][0:n, :], ACT.Identity, scale=mv2[t % 2][0:n, 2:3], bias=mv2[t % 2][0:n, 3:4]).then_inc(y_norm, 1)

            @block.vector
            def _(dve):
                def raw_lo(n, dst):
                    dve.wait_ge(s_hi, n + 1)
                    dve.tensor_tensor(dst, raw[n], gh[:, n % KD, :].bitcast(F32), ALU.subtract).then_inc(s_lo, 1)

                def gated_product(it, base, u):
                    for n in range(NCH):
                        chunk_ready(g, dve, base + (2 * u + 1), n)
                        dve.tensor_tensor(acc[:, ds(it * 2 + u, 1), chunk(n)].rearrange("p a t -> p (a t)"), bank[n][:, 0:TC], gate[u][:, chunk(n)], ALU.mult).then_inc(g.bank_free[n], 1)

                def merged(it, base, u):
                    for n in range(NCH):
                        i = (it * 2 + u) * NCH + n
                        j = base + (2 * u + 1)
                        cols = lambda x: x[:, ds(it * 2 + u, 1), chunk(n)].rearrange("p a t -> p (a t)")
                        chunk_ready(g, dve, j, n)
                        dve.wait_ge(m_lo, i)
                        dve.tensor_tensor(tmp[:], bank[n][:, 0:TC], gate[u][:, chunk(n)], ALU.mult).then_inc(g.bank_free[n], 1)
                        dve.wait_ge(g.bank_free[n], j + 2)
                        dve.tensor_tensor(tmp[:], tmp[:], cols(acc), ALU.add).then_inc(m_sum, 1)
                        dve.wait_ge(m_sum, i + 1)
                        dve.tensor_scalar(cols(mh), tmp[:], 1.0, None, ALU.mult).then_inc(m_hi, 1)
                        dve.wait_ge(m_hi, i + 1)
                        dve.tensor_tensor(cols(gl), tmp[:], cols(mh).bitcast(F32), ALU.subtract).then_inc(m_lo, 1)

                def branch(it, base, kt, use, last=False):
                    for u in range(2):
                        split_lo(g, dve, job(base, 1, 2 * u + 2))
                        use(it, base, u)
                        if not (last and u):
                            split_lo(g, dve, job(base, 1, 2 * u + 3), kt)
                LAST = KD // 2 - 1
                for n in range(KD):
                    if n == FIRST_RAW:
                        split_lo(g, dve, job(JA, 1, 1))
                    raw_lo(n, gl[:, n, :])
                dve.memset(zsum[:], 0.0).then_inc(z_part, 1)
                with dve.Fori(0, LAST) as it:
                    branch(it, it * 4 + JA, KD, gated_product)
                branch(LAST, LAST * 4 + JA, KD, gated_product, last=True)
                split_lo(g, dve, job(JB, 1, 1), KB)
                for n in range(KD, KD + KB):
                    raw_lo(n, gh[:, n - KD + KB, :])
                with dve.Fori(0, LAST) as it:
                    branch(it, it * 4 + JB, KB, merged)
                branch(LAST, LAST * 4 + JB, KB, merged, last=True)
                dve.wait_ge(s_lo, KD + KB)
                dve.wait_ge(m_lo, NCH * KD)
                dve.wait_ge(z_part, 1)

                def projected(it, u):
                    split_lo(g, dve, job(it * 2 + JO, JO % 2, u + 1))
                    for n in range(NCH):
                        i = (it * 2 + u) * NCH + n
                        j = it * 2 + JO + u
                        cols = lambda x: x[:, ds(it * 2 + u, 1), chunk(n)].rearrange("p a t -> p (a t)")
                        chunk_ready(g, dve, j, n)
                        dve.wait_ge(z_done, i)
                        dve.scalar_tensor_tensor(tmp[:], cols(g.xh).bitcast(F32), ALPHA, bank[n][:, 0:TC], ALU.mult, ALU.add).then_inc(g.bank_free[n], 1)
                        dve.wait_ge(g.bank_free[n], j + 2)
                        dve.scalar_tensor_tensor(cols(z), cols(g.xl).bitcast(F32), ALPHA, tmp[:], ALU.mult, ALU.add).then_inc(z_done, 1)
                        dve.wait_ge(z_done, i + 1)
                        dve.wait_ge(z_summed, i)
                        dve.tensor_tensor(zsum[:, chunk(n)], zsum[:, chunk(n)], cols(z), ALU.add).then_inc(z_summed, 1)
                with dve.Fori(0, KD // 2) as it:
                    for u in range(2):
                        projected(it, u)
                dve.wait_ge(ln_land, 32)

                def wide_chunk(x):
                    return x.unsqueeze(1).to_broadcast([P, KD, TC])

                def centre(n):
                    dve.wait_ge(mean, n + 1)
                    dve.tensor_tensor(z[:, :, chunk(n)], z[:, :, chunk(n)], wide_chunk(bank[3 + n][:, 0:TC]), ALU.subtract).then_inc(centred, 1)
                for n in range(NCH):
                    centre(n)
                for n in range(NCH):
                    dve.wait_ge(root, n + 1)
                    dve.reciprocal(rstd[:, chunk(n)], rstd[:, chunk(n)]).then_inc(inv, 1)
                    dve.wait_ge(inv, n + 1)
                    for k in range(KD):
                        dve.scalar_tensor_tensor(z[:, k, chunk(n)], z[:, k, chunk(n)], ln_cols[:, 0, k:k + 1], rstd[:, chunk(n)], ALU.mult, ALU.mult).then_inc(normed, 1)
                    for k in range(KD):
                        dve.wait_ge(h_hi, n * KD + k + 1)
                        dve.scalar_tensor_tensor(g.xl[:, k, chunk(n)], z[:, k, chunk(n)], ln_cols[:, 1, k:k + 1],
                                                 g.xh[:, k, chunk(n)].bitcast(F32), ALU.add, ALU.subtract).then_inc(h_lo, 1)
                dve.memset(up[:, 0:2], 0.0).then_inc(z_part, 1)
                for s, (f0, n, ju, jd) in enumerate(sections):
                    with dve.Fori(0, n) as i:
                        f = i + f0
                        split_lo(g, dve, job(i * 2 + ju, ju % 2, 1))
                        dve.wait_ge(a_lo, f)
                        old = fc[:, 0:2 * NS].rearrange("p (b w) -> p w b", w=2)
                        new = act_in[:, SEQ:T]
                        dve.wait_ge(a_hi, f)
                        dve.wait_ge(fc_done, f + 1)
                        dve.tensor_scalar(new, old[:, 0, :], fc[:, 16:17], fc[:, 19:20], ALU.mult, ALU.add).then_inc(conv, 1)
                        dve.wait_ge(c1, f + 1)
                        dve.scalar_tensor_tensor(act_in[:, 0:SEQ], up[:, 1:1 + SEQ], fc[:, 17:18], act_in[:, 0:SEQ], ALU.mult, ALU.add).then_inc(conv, 1)
                        dve.wait_ge(conv, f * 5 + 1)
                        dve.scalar_tensor_tensor(new, old[:, 1, :], fc[:, 17:18], new, ALU.mult, ALU.add).then_inc(conv, 1)
                        dve.wait_ge(conv, f * 5 + 3)
                        dve.scalar_tensor_tensor(act_in[:, 0:SEQ], up[:, 2:2 + SEQ], fc[:, 18:19], act_in[:, 0:SEQ], ALU.mult, ALU.add).then_inc(conv, 1)
                        dve.scalar_tensor_tensor(new, up[:, 2 + SEQ:2 + T], fc[:, 18:19], new, ALU.mult, ALU.add).then_inc(conv, 1)
                        split_lo(g, dve, job(i * 2 + ju, ju % 2, 2))
                        dve.wait_ge(gelu, f + 1)
                        for k in range(NCH):
                            chunk_ready(g, dve, i * 2 + ju + 1, k)
                            dve.tensor_tensor(act_in[:, chunk(k)], act_in[:, chunk(k)], bank[k][:, 0:TC], ALU.mult).then_inc(g.bank_free[k], 1)
                        dve.wait_ge(a_hi, f + 1)
                        dve.tensor_tensor(gl[:, ds(i, 1), :].rearrange("p a t -> p (a t)"), act_in[:, 0:T],
                                          gh[:, ds(i, 1), :].rearrange("p a t -> p (a t)").bitcast(F32), ALU.subtract).then_inc(a_lo, 1)

                    def down(it, last):
                        for u in range(2):
                            if not (last and u):
                                split_lo(g, dve, job(it * 2 + jd, jd % 2, u + 1))
                            for k in range(NCH):
                                cols = acc[:, ds(it * 2 + u, 1), chunk(k)].rearrange("p a t -> p (a t)")
                                chunk_ready(g, dve, it * 2 + jd + u, k)
                                dve.tensor_tensor(cols, cols, bank[k][:, 0:TC], ALU.add).then_inc(g.bank_free[k], 1)
                    if s == 0:
                        dve.wait_ge(h_scaled, NCH)
                    with dve.Fori(0, KD // 2 - 1) as it:
                        down(it, False)
                    down(KD // 2 - 1, s == len(sections) - 1)
                dve.wait_ge(wide_land, 32)

                def scale_rows(t):
                    n = P if t < QB else NS
                    dve.wait_ge(y_norm, t + 1)
                    dve.tensor_tensor(y[t][0:n, :], y[t][0:n, :], wide[0][0:n, :], ALU.mult).then_inc(y_mul, 1)
                for t in range(NT):
                    n = P if t < QB else NS
                    v, st = mv2[t % 2], stats[t % 2]
                    dve.wait_ge(y_t, t + 1)
                    if t >= 2:
                        dve.wait_ge(y_norm, t - 1)
                    for half in range(2):
                        dve.bn_stats(st[0:n, half, :], g.pair[t % 2][0:n, half * 512:(half + 1) * 512]).then_inc(stat, 1)
                    dve.wait_ge(stat, 2 * t + 2)
                    dve.bn_aggr(v[0:n, 0:2], st[0:n].rearrange("p a s -> p (a s)")).then_inc(y_var, 1)
                    if t >= 1:
                        scale_rows(t - 1)
                    dve.wait_ge(y_root, t + 1)
                    dve.reciprocal(v[0:n, 2:3], v[0:n, 2:3]).then_inc(y_inv, 1)
                    dve.wait_ge(y_inv, t + 1)
                    dve.scalar_tensor_tensor(v[0:n, 3:4], v[0:n, 0:1], -1.0, v[0:n, 2:3], ALU.mult, ALU.mult).then_inc(y_bias, 1)
                scale_rows(NT - 1)
                dve.wait_ge(y_mul, NT)
                dve.wait_ge(y_add, QB)
                dve.tensor_tensor(y[QB][0:NS, :], y[QB][0:NS, :], wide[1][0:NS, :], ALU.add).then_inc(y_add, 1)


def w_in_tile(a, col, m=P):
    w = a["w_in"].rearrange("a (k p) c -> p (a k) c", p=P)
    return w[:, :, ds(col, m)]


def build_program(nc, a, c, o):
    with ExitStack() as ctx:
        sb = lambda n, s, d=F32: ctx.enter_context(nc.sbuf_tensor(n, s, d))
        sem = lambda n: ctx.enter_context(nc.semaphore(n))
        g = Shared()
        ps = lambda n, w: ctx.enter_context(nc.psum_tensor(n, [P, w], F32))
        g.pair = [ps("banks34", 1024), ps("banks56", 1024)]
        g.bank = ([ps(f"bank{n}", 512) for n in range(NCH)]
                  + [g.pair[i // 2][:, 512 * (i % 2):512 * (i % 2) + 512] for i in range(4)] + [ps("bank7", 512)])
        g.ident = sb("ident", [P, P])
        g.x_at = nc.sbuf_base
        g.xh, g.xl = sb("x_hi", [P, KD, T], F32R), sb("x_lo", [P, KD, T], F32R)
        g.conv_cols, g.eps = sb("conv_cols", [P, FT, 20]), sb("eps", [P, 1])
        g.w_raw = [sb(f"w_raw{i}", [P, KD, P]) for i in range(RING)]
        g.w_hi = [sb(f"w_hi{i}", [P, KD, P], F32R) for i in range(RING)]
        g.w_lo = [sb(f"w_lo{i}", [P, KD, P], F32R) for i in range(RING)]
        g.w_land = [sem(f"w_land{i}") for i in range(RING)]
        g.w_rounded, g.w_split, g.mm_chunk = sem("w_rounded"), sem("w_split"), sem("mm_chunk")
        g.bank_free = [sem(f"bank_free{n}") for n in range(NCH)]
        attention_part = ExitStack()
        g.qnew, g.knew, g.vnew = (attention_part.enter_context(nc.sbuf_tensor(n, [NS, FH * HD], F32)) for n in ("q_new", "k_new", "v_new"))
        g.lfnew = attention_part.enter_context(nc.sbuf_tensor("logf_new", [NS, FH], F32))
        g.lf_rows = attention_part.enter_context(nc.sbuf_tensor("logf_rows_out", [P, QB + 1, FH], F32))
        g.fo_dram = nc.dram_tensor("fox_t_scratch", [FH // 2, P, T], F32).ap()
        g.q_dram = nc.dram_tensor("q_new_scratch", [NS, FH * HD], F32).ap()
        g.g_dram = nc.dram_tensor("gated_t_scratch", [KD, P, T], F32).ap()
        g.dec_bias = attention_part.enter_context(nc.sbuf_tensor("dec_bias", [P, NS, NPG + 1, FH], F32))
        fox_part = ExitStack()
        g.lf = fox_part.enter_context(nc.sbuf_tensor("logf", [FH, T], F32))
        prepare(nc, g, a, c, o)
        fox(nc, g, a, c, o)
        fox_part.close()
        retain(nc, g, a, c, o)
        attention_part.close()
        finish(nc, g, a, c, o)


_INS = ["x_prompt", "x_sample", "cache_k", "cache_v", "cache_logf", "state_ret", "state_conv", "page_table",
        "w_in", "b_f", "ret_gn_w", "ret_gn_b", "w_pa", "w_pb", "w_o", "ln1_w", "ln1_b",
        "w_up", "w_gate", "conv_w", "conv_b", "w_down", "ln2_w", "ln2_b"]
_OUTS = [(1, SEQ, D), (NS, 1, D), (1, 1, SEQ, FH, HD), (1, 1, SEQ, FH, HD), (1, 1, SEQ, FH),
         (1, NS, 1, FH, HD), (1, NS, 1, FH, HD), (1, NS, 1, FH),
         (1, 1, RH, DK, DV), (1, NS, RH, DK, DV), (1, 1, 2, DFF), (1, NS, 2, DFF)]


def kernel(**inputs):
    import numpy as _np
    import concourse.bacc as _bacc
    from concourse import mybir as _mybir
    from concourse.bass_utils import run_bass_kernel_spmd as _run

    nc = _bacc.Bacc("TRN2", target_bir_lowering=False, num_devices=1)
    arrays, args, consts = {}, {}, {}
    for name in _INS:
        x = _np.ascontiguousarray(inputs[name])
        arrays[f"in_{name}_dram"] = x
        args[name] = nc.dram_tensor(f"in_{name}_dram", x.shape, _mybir.dt.from_np(x.dtype), kind="ExternalInput").ap()
    for name, x in constants().items():
        arrays[f"const_{name}_dram"] = x
        consts[name] = nc.dram_tensor(f"const_{name}_dram", x.shape, _mybir.dt.from_np(x.dtype), kind="ExternalInput").ap()
    outs = [nc.dram_tensor(f"out_{i}_dram", shape, _mybir.dt.float32, kind="ExternalOutput").ap() for i, shape in enumerate(_OUTS)]
    build_program(nc, args, consts, outs)
    r = _run(nc, [arrays], core_ids=[0])
    return tuple(r.results[0][f"out_{i}_dram"] for i in range(len(_OUTS)))
```
